# Optimizing a Trainium2 kernel written in Bass

```python
import jax, jax.numpy as jnp
from jax import lax
import numpy as np
import jax
import jax.numpy as jnp

D_MODEL = 1024
BATCH = 1
SEQ = 256
DEPTH = 1

PLE_DIM = 256
EPS = 1e-6
RET_HEADS = 4
RET_DK = 128
RET_DV = 128
RET_CHUNK = 128
SWA_HEADS = 8
SWA_KV_HEADS = 2
SWA_GROUP = SWA_HEADS // SWA_KV_HEADS
SWA_HD = 64
WINDOW = 128
N_GROUPS = 4
EXPERTS_PER_GROUP = 8
N_EXPERTS = N_GROUPS * EXPERTS_PER_GROUP
EXPERT_FF = 256
TOP_K = 2

RET_QK = RET_HEADS * RET_DK
RET_V = RET_HEADS * RET_DV
SWA_Q = SWA_HEADS * SWA_HD
SWA_KV = SWA_KV_HEADS * SWA_HD
IN_SPLITS = (RET_QK, RET_QK, RET_V, RET_V, SWA_Q, SWA_KV, SWA_KV, D_MODEL, D_MODEL)
IN_WIDTH = sum(IN_SPLITS)


def rms_norm(x, g):
    xf = x.astype(jnp.float32)
    y = xf * lax.rsqrt(jnp.mean(xf * xf, axis=-1, keepdims=True) + EPS)
    return (y * g.astype(jnp.float32)).astype(x.dtype)

def head_group_norm(y, g, b):
    yf = y.astype(jnp.float32)
    mu = jnp.mean(yf, axis=-1, keepdims=True)
    var = jnp.mean(jnp.square(yf - mu), axis=-1, keepdims=True)
    yn = ((yf - mu) * lax.rsqrt(var + EPS)).reshape(y.shape[0], y.shape[1], -1)
    return (yn * g.astype(jnp.float32) + b.astype(jnp.float32)).astype(y.dtype)

def retention_chunkwise(q, k, v):
    dtype = v.dtype
    q = q.astype(jnp.float32)
    k = k.astype(jnp.float32) * (RET_DK ** -0.5)
    v = v.astype(jnp.float32)
    b, s, h, dk = q.shape
    nc = s // RET_CHUNK
    q = q.reshape(b, nc, RET_CHUNK, h, dk)
    k = k.reshape(b, nc, RET_CHUNK, h, dk)
    v = v.reshape(b, nc, RET_CHUNK, h, RET_DV)
    log_gamma = jnp.log1p(-jnp.exp2(-5.0 - jnp.arange(h, dtype=jnp.float32)))
    pos = jnp.arange(RET_CHUNK, dtype=jnp.float32)
    diff = pos[:, None] - pos[None, :]
    decay_mask = jnp.where(diff[None] >= 0.0,
                           jnp.exp(jnp.maximum(diff, 0.0)[None] * log_gamma[:, None, None]), 0.0)
    scores = jnp.einsum('bnihd,bnjhd->bnhij', q, k) * decay_mask
    inner = jnp.einsum('bnhij,bnjhv->bnihv', scores, v)
    zeta = jnp.exp((RET_CHUNK - 1.0 - pos)[None, :] * log_gamma[:, None])
    chunk_kv = jnp.einsum('bnjhd,bnjhv,hj->nbhdv', k, v, zeta)
    chunk_decay = jnp.exp(RET_CHUNK * log_gamma)[None, :, None, None]

    def step(state, kv):
        return chunk_decay * state + kv, state

    _, prev_states = lax.scan(step, jnp.zeros_like(chunk_kv[0]), chunk_kv)
    xi = jnp.exp((pos + 1.0)[None, :] * log_gamma[:, None])
    cross = jnp.einsum('bnihd,nbhdv,hi->bnihv', q, prev_states, xi)
    return (inner + cross).reshape(b, s, h, RET_DV).astype(dtype)

def sliding_window_gqa(q, k, v, sinks):
    b, s = q.shape[:2]
    nb = s // WINDOW
    qb = q.reshape(b, nb, WINDOW, SWA_KV_HEADS, SWA_GROUP, SWA_HD)
    kb = k.reshape(b, nb, WINDOW, SWA_KV_HEADS, SWA_HD)
    vb = v.reshape(b, nb, WINDOW, SWA_KV_HEADS, SWA_HD)
    k_band = jnp.concatenate([jnp.concatenate([jnp.zeros_like(kb[:, :1]), kb[:, :-1]], axis=1), kb], axis=2)
    v_band = jnp.concatenate([jnp.concatenate([jnp.zeros_like(vb[:, :1]), vb[:, :-1]], axis=1), vb], axis=2)
    scores = jnp.einsum('bnqkgd,bnskd->bnkgqs', qb, k_band).astype(jnp.float32) * (SWA_HD ** -0.5)
    qi = jnp.arange(WINDOW)
    sj = jnp.arange(2 * WINDOW)
    rel = qi[:, None] + WINDOW - sj[None, :]
    in_window = (rel >= 0) & (rel < WINDOW)
    key_exists = (jnp.arange(nb)[:, None] * WINDOW - WINDOW + sj[None, :]) >= 0
    mask = in_window[None] & key_exists[:, None, :]
    slopes = jnp.exp2(-8.0 * jnp.arange(1, SWA_HEADS + 1, dtype=jnp.float32) / SWA_HEADS)
    slopes = slopes.reshape(SWA_KV_HEADS, SWA_GROUP)
    alibi = -slopes[:, :, None, None] * rel.astype(jnp.float32)[None, None]
    scores = jnp.where(mask[None, :, None, None], scores + alibi[None, None], -1e30)
    sink = jnp.broadcast_to(sinks.astype(jnp.float32).reshape(1, 1, SWA_KV_HEADS, SWA_GROUP, 1, 1),
                            scores.shape[:-1] + (1,))
    probs = jax.nn.softmax(jnp.concatenate([scores, sink], axis=-1), axis=-1)[..., :-1]
    out = jnp.einsum('bnkgqs,bnskd->bnqkgd', probs.astype(v.dtype), v_band)
    return out.reshape(b, s, SWA_Q)

def hierarchical_moe(h, w_rg, b_rg, w_re, b_re, w_gate, w_up, w_down):
    b, s, d = h.shape
    hf = h.reshape(-1, d)
    g_prob = jax.nn.softmax((hf @ w_rg + b_rg).astype(jnp.float32), axis=-1)
    g_sel = jnp.argmax(g_prob, axis=-1)
    g_w = jnp.take_along_axis(g_prob, g_sel[:, None], axis=-1)
    e_logits = (hf @ w_re + b_re).astype(jnp.float32).reshape(-1, N_GROUPS, EXPERTS_PER_GROUP)
    e_in_group = jnp.take_along_axis(e_logits, g_sel[:, None, None], axis=1)[:, 0]
    top_p, top_i = lax.top_k(jax.nn.softmax(e_in_group, axis=-1), TOP_K)
    top_p = top_p / jnp.sum(top_p, axis=-1, keepdims=True)
    expert_id = g_sel[:, None] * EXPERTS_PER_GROUP + top_i
    combine = jnp.sum(jax.nn.one_hot(expert_id, N_EXPERTS, dtype=jnp.float32)
                      * (g_w * top_p)[..., None], axis=1)
    y = jnp.zeros_like(hf)
    for grp in range(N_GROUPS):
        sl = slice(grp * EXPERTS_PER_GROUP, (grp + 1) * EXPERTS_PER_GROUP)
        hid = jax.nn.silu(jnp.einsum('td,edf->tef', hf, w_gate[sl])) * jnp.einsum('td,edf->tef', hf, w_up[sl])
        y = y + jnp.einsum('tef,efd->td', hid * combine[:, sl, None].astype(hid.dtype), w_down[sl])
    return y.reshape(b, s, d)

def first_inputs(seed: int = 0) -> dict:
    key = jax.random.key(seed)
    ks = jax.random.split(key, 26)
    f32 = jnp.float32
    L = DEPTH

    def nrm(k, shape, scale):
        return jax.random.normal(k, shape, f32) * scale

    def gain(k, shape):
        return 1.0 + 0.02 * jax.random.normal(k, shape, f32)

    return dict(
        x=nrm(ks[0], (BATCH, SEQ, D_MODEL), 1.0),
        p=nrm(ks[1], (L, BATCH, SEQ, PLE_DIM), 1.0),
        mix_norm_g=gain(ks[2], (L, D_MODEL)),
        w_in=nrm(ks[3], (L, D_MODEL, IN_WIDTH), D_MODEL ** -0.5),
        ret_gn_g=gain(ks[4], (L, RET_V)),
        ret_gn_b=nrm(ks[5], (L, RET_V), 0.02),
        w_ret_o=nrm(ks[6], (L, RET_V, D_MODEL), RET_V ** -0.5),
        q_norm_g=gain(ks[7], (L, SWA_HD)),
        k_norm_g=gain(ks[8], (L, SWA_HD)),
        attn_sinks=nrm(ks[9], (L, SWA_HEADS), 0.5),
        w_swa_o=nrm(ks[10], (L, SWA_Q, D_MODEL), SWA_Q ** -0.5),
        w_out=nrm(ks[11], (L, D_MODEL, D_MODEL), D_MODEL ** -0.5),
        ffn_norm_g=gain(ks[12], (L, D_MODEL)),
        w_router_group=nrm(ks[13], (L, D_MODEL, N_GROUPS), D_MODEL ** -0.5),
        b_router_group=nrm(ks[14], (L, N_GROUPS), 0.01),
        w_router_expert=nrm(ks[15], (L, D_MODEL, N_EXPERTS), D_MODEL ** -0.5),
        b_router_expert=nrm(ks[16], (L, N_EXPERTS), 0.01),
        w_exp_gate=nrm(ks[17], (L, N_EXPERTS, D_MODEL, EXPERT_FF), D_MODEL ** -0.5),
        w_exp_up=nrm(ks[18], (L, N_EXPERTS, D_MODEL, EXPERT_FF), D_MODEL ** -0.5),
        w_exp_down=nrm(ks[19], (L, N_EXPERTS, EXPERT_FF, D_MODEL), EXPERT_FF ** -0.5),
        ple_gate_norm_g=gain(ks[20], (L, D_MODEL)),
        w_ple_gate=nrm(ks[21], (L, D_MODEL, D_MODEL), D_MODEL ** -0.5),
        w_ple=nrm(ks[22], (L, PLE_DIM, D_MODEL), PLE_DIM ** -0.5),
        ple_norm_g=gain(ks[23], (L, D_MODEL)),
    )

def first_block(x, p, mix_norm_g, w_in, ret_gn_g, ret_gn_b, w_ret_o, q_norm_g, k_norm_g, attn_sinks,
              w_swa_o, w_out, ffn_norm_g, w_router_group, b_router_group, w_router_expert,
              b_router_expert, w_exp_gate, w_exp_up, w_exp_down, ple_gate_norm_g, w_ple_gate,
              w_ple, ple_norm_g):
    b, s, _ = x.shape
    split_at = [int(c) for c in np.cumsum(IN_SPLITS)[:-1]]
    for i in range(DEPTH):
        h = rms_norm(x, mix_norm_g[i])
        z = h @ w_in[i]
        rq, rk, rv, rg, sq, sk, sv, gate_r, gate_s = jnp.split(z, split_at, axis=-1)
        y_r = retention_chunkwise(rq.reshape(b, s, RET_HEADS, RET_DK),
                                  rk.reshape(b, s, RET_HEADS, RET_DK),
                                  rv.reshape(b, s, RET_HEADS, RET_DV))
        y_r = (jax.nn.silu(rg) * head_group_norm(y_r, ret_gn_g[i], ret_gn_b[i])) @ w_ret_o[i]
        q = rms_norm(sq.reshape(b, s, SWA_HEADS, SWA_HD), q_norm_g[i])
        k = rms_norm(sk.reshape(b, s, SWA_KV_HEADS, SWA_HD), k_norm_g[i])
        v = sv.reshape(b, s, SWA_KV_HEADS, SWA_HD)
        y_s = sliding_window_gqa(q, k, v, attn_sinks[i]) @ w_swa_o[i]
        merged = jax.nn.sigmoid(gate_r) * y_r + jax.nn.sigmoid(gate_s) * y_s
        x = x + merged @ w_out[i]
        x = x + hierarchical_moe(rms_norm(x, ffn_norm_g[i]), w_router_group[i], b_router_group[i],
                                 w_router_expert[i], b_router_expert[i], w_exp_gate[i],
                                 w_exp_up[i], w_exp_down[i])
        ple = rms_norm(p[i] @ w_ple[i], ple_norm_g[i])
        x = x + jax.nn.sigmoid(rms_norm(x, ple_gate_norm_g[i]) @ w_ple_gate[i]) * ple
    return x


DEPTH_2 = 2

CTX_LEN = 256
GRID_W = 64
N_BRANCHES = 3
NA_HEADS = 8
NA_HEAD_DIM = 64
NA_WIDTH = NA_HEADS * NA_HEAD_DIM
NA_WIN_H = 8
NA_WIN_W = 16
GM_GROUPS = 4
GM_CHUNK = 128
GM_GROUP_DIM = 128
GM_WIDTH = GM_GROUPS * GM_GROUP_DIM
MLA_HEADS = 8
MLA_Q_RANK = 256
MLA_KV_RANK = 128
MLA_NOPE = 64
MLA_ROPE = 32
MLA_V = 64
MLA_QK = MLA_NOPE + MLA_ROPE
ROPE_AXIS_PAIRS = MLA_ROPE // 4
ROPE_THETA = 10000.0
FFN_HIDDEN = 4 * D_MODEL
Q_BLOCK = 128
NORM_EPS = 1e-6
NEG_INF = -1e30
MOD_SCALE = 0.5

OFF_NA_K = 0
OFF_NA_V = OFF_NA_K + NA_WIDTH
OFF_MLA_CKV = OFF_NA_V + NA_WIDTH
OFF_MLA_KR = OFF_MLA_CKV + MLA_KV_RANK
N_CTX_COLS = OFF_MLA_KR + MLA_ROPE
OFF_NA_Q = N_CTX_COLS
OFF_GM_U = OFF_NA_Q + NA_WIDTH
OFF_GM_V = OFF_GM_U + GM_WIDTH
OFF_MLA_CQ = OFF_GM_V + GM_WIDTH
OFF_GATES = OFF_MLA_CQ + MLA_Q_RANK
N_IN_COLS = OFF_GATES + N_BRANCHES * D_MODEL


def rms_norm_2(t, gain):
    tf = t.astype(jnp.float32)
    y = tf * lax.rsqrt(jnp.mean(tf * tf, axis=-1, keepdims=True) + NORM_EPS)
    return (y * gain.astype(jnp.float32)).astype(t.dtype)

def layer_norm(t, gain, bias):
    tf = t.astype(jnp.float32)
    mu = jnp.mean(tf, axis=-1, keepdims=True)
    var = jnp.mean(jnp.square(tf - mu), axis=-1, keepdims=True)
    y = (tf - mu) * lax.rsqrt(var + NORM_EPS)
    return (y * gain.astype(jnp.float32) + bias.astype(jnp.float32)).astype(t.dtype)

def modulate(t, shift, scale):
    return t * (1 + scale) + shift

def cols(t, off, width):
    return t[..., off:off + width]

def split_heads(t, n_heads):
    b, n, w = t.shape
    return t.reshape(b, n, n_heads, w // n_heads).transpose(0, 2, 1, 3)

def merge_heads(t):
    b, h, n, d = t.shape
    return t.transpose(0, 2, 1, 3).reshape(b, n, h * d)

def axial_rope(n_tokens):
    t = jnp.arange(n_tokens)
    rows = (t // GRID_W).astype(jnp.float32)
    colsv = (t % GRID_W).astype(jnp.float32)
    freqs = ROPE_THETA ** (-jnp.arange(ROPE_AXIS_PAIRS, dtype=jnp.float32) / ROPE_AXIS_PAIRS)
    ang = jnp.stack([rows[:, None] * freqs, colsv[:, None] * freqs], axis=1)
    return jnp.cos(ang), jnp.sin(ang)

def apply_rope_tail(t, cos, sin):
    head, tail = t[..., :-MLA_ROPE], t[..., -MLA_ROPE:]
    tr = tail.reshape(tail.shape[:-1] + (2, 2, ROPE_AXIS_PAIRS)).astype(jnp.float32)
    x1, x2 = tr[..., 0, :], tr[..., 1, :]
    c, s = cos[:, None], sin[:, None]
    rot = jnp.stack([x1 * c - x2 * s, x2 * c + x1 * s], axis=-2).reshape(tail.shape).astype(t.dtype)
    return jnp.concatenate([head, rot], axis=-1)

def dense_attention(q, k, v):
    b, h, n, d = q.shape
    scale = d ** -0.5
    qb = jnp.moveaxis(q.reshape(b, h, n // Q_BLOCK, Q_BLOCK, d), 2, 0)

    def attend(q_blk):
        s = jnp.einsum('bhqd,bhkd->bhqk', q_blk, k).astype(jnp.float32) * scale
        p = jax.nn.softmax(s, axis=-1).astype(v.dtype)
        return jnp.einsum('bhqk,bhkd->bhqd', p, v)

    out = lax.map(attend, qb)
    return jnp.moveaxis(out, 0, 2).reshape(b, h, n, v.shape[-1])

def neighbourhood_attention(q, k, v, k_ctx, v_ctx, rpb):
    b, h, n, dh = q.shape
    rows = n // GRID_W
    kh = min(NA_WIN_H, rows)
    kw = NA_WIN_W
    scale = dh ** -0.5
    qg = jnp.moveaxis(q.reshape(b, h, rows, GRID_W, dh), 2, 0)
    kg = k.reshape(b, h, rows, GRID_W, dh)
    vg = v.reshape(b, h, rows, GRID_W, dh)
    r = jnp.arange(rows)
    r0 = jnp.clip(r - kh // 2, 0, rows - kh)
    cq = jnp.arange(GRID_W)
    c0 = jnp.clip(cq - kw // 2, 0, GRID_W - kw)
    col_in = (cq[None, :] >= c0[:, None]) & (cq[None, :] < c0[:, None] + kw)
    dc = jnp.clip(cq[None, :] - cq[:, None], -(NA_WIN_W - 1), NA_WIN_W - 1) + NA_WIN_W - 1

    def row_block(args):
        q_r, r_i, r0_i = args
        k_band = lax.dynamic_slice_in_dim(kg, r0_i, kh, axis=2)
        v_band = lax.dynamic_slice_in_dim(vg, r0_i, kh, axis=2)
        dr = r0_i + jnp.arange(kh) - r_i + NA_WIN_H - 1
        bias = rpb[:, dr[None, :, None], dc[:, None, :]].astype(jnp.float32)
        s_loc = jnp.einsum('bhqd,bhkcd->bhqkc', q_r, k_band).astype(jnp.float32) * scale + bias
        s_loc = jnp.where(col_in[:, None, :], s_loc, NEG_INF).reshape(b, h, GRID_W, kh * GRID_W)
        s_ctx = jnp.einsum('bhqd,bhld->bhql', q_r, k_ctx).astype(jnp.float32) * scale
        p = jax.nn.softmax(jnp.concatenate([s_loc, s_ctx], axis=-1), axis=-1).astype(v.dtype)
        p_loc = p[..., :kh * GRID_W].reshape(b, h, GRID_W, kh, GRID_W)
        return (jnp.einsum('bhqkc,bhkcd->bhqd', p_loc, v_band)
                + jnp.einsum('bhql,bhld->bhqd', p[..., kh * GRID_W:], v_ctx))

    out = lax.map(row_block, (qg, r, r0))
    return jnp.moveaxis(out, 0, 2).reshape(b, h, n, dh)

def spatial_gating(u, v, ln_g, ln_b, w_s, b_s):
    b, n, _ = v.shape
    v = layer_norm(v, ln_g, ln_b)
    vc = v.reshape(b, n // GM_CHUNK, GM_CHUNK, GM_GROUPS, GM_GROUP_DIM)
    mixed = jnp.einsum('gpq,bnqgc->bnpgc', w_s, vc) + b_s.T[:, :, None]
    return u * mixed.reshape(b, n, GM_WIDTH)

def mla_queries(c_q, cq_gain, w_uq, q_gain, rope):
    b, n, _ = c_q.shape
    q = (rms_norm_2(c_q, cq_gain) @ w_uq).reshape(b, n, MLA_HEADS, MLA_QK)
    q = rms_norm_2(q, q_gain)
    if rope is not None:
        q = apply_rope_tail(q, rope[0], rope[1])
    return q.transpose(0, 2, 1, 3)

def mla_keys_values(c_kv, k_rope, ckv_gain, w_ukv, k_gain, rope):
    b, n, _ = c_kv.shape
    kv = (rms_norm_2(c_kv, ckv_gain) @ w_ukv).reshape(b, n, MLA_HEADS, MLA_NOPE + MLA_V)
    k_nope, v = kv[..., :MLA_NOPE], kv[..., MLA_NOPE:]
    k_r = jnp.broadcast_to(k_rope[:, :, None, :], (b, n, MLA_HEADS, MLA_ROPE))
    k = rms_norm_2(jnp.concatenate([k_nope, k_r], axis=-1), k_gain)
    if rope is not None:
        k = apply_rope_tail(k, rope[0], rope[1])
    return k.transpose(0, 2, 1, 3), v.transpose(0, 2, 1, 3)

def merge_branches(y_na, y_gm, y_mla, gate_logits, na_w_o, gm_w_o, mla_w_o, w_out):
    g = jax.nn.sigmoid(gate_logits).reshape(gate_logits.shape[:-1] + (N_BRANCHES, D_MODEL))
    y = g[..., 0, :] * (y_na @ na_w_o) + g[..., 1, :] * (y_gm @ gm_w_o) + g[..., 2, :] * (y_mla @ mla_w_o)
    return y @ w_out

def squared_relu_mlp(h, w1, w2):
    return jnp.square(jax.nn.relu(h @ w1)) @ w2

def second_inputs(seed: int = 0) -> dict:
    key = jax.random.key(seed)
    ks = jax.random.split(key, 28)
    f32 = jnp.float32

    def nrm(k, shape, scale):
        return scale * jax.random.normal(k, shape, f32)

    def gain(k, shape):
        return 1.0 + 0.02 * jax.random.normal(k, shape, f32)

    L = DEPTH_2
    return {
        'x': nrm(ks[0], (BATCH, SEQ, D_MODEL), 1.0),
        'c': nrm(ks[1], (BATCH, D_MODEL), 1.0),
        'ctx': nrm(ks[2], (BATCH, CTX_LEN, D_MODEL), 1.0),
        'c_ctx': nrm(ks[3], (D_MODEL,), 1.0),
        'w_mod': nrm(ks[4], (L, D_MODEL, 6 * D_MODEL), MOD_SCALE * D_MODEL ** -0.5),
        'b_mod': nrm(ks[5], (L, 6 * D_MODEL), 0.02),
        'g_norm1': gain(ks[6], (L, D_MODEL)),
        'g_norm2': gain(ks[7], (L, D_MODEL)),
        'w_in': nrm(ks[8], (L, D_MODEL, N_IN_COLS), D_MODEL ** -0.5),
        'na_q_gain': gain(ks[9], (L, NA_HEAD_DIM)),
        'na_k_gain': gain(ks[10], (L, NA_HEAD_DIM)),
        'na_rpb': nrm(ks[11], (L, NA_HEADS, 2 * NA_WIN_H - 1, 2 * NA_WIN_W - 1), 0.1),
        'na_w_o': nrm(ks[12], (L, NA_WIDTH, D_MODEL), NA_WIDTH ** -0.5),
        'gm_ln_g': gain(ks[13], (L, GM_WIDTH)),
        'gm_ln_b': nrm(ks[14], (L, GM_WIDTH), 0.02),
        'gm_w_s': nrm(ks[15], (L, GM_GROUPS, GM_CHUNK, GM_CHUNK), GM_CHUNK ** -0.5),
        'gm_b_s': gain(ks[16], (L, GM_GROUPS, GM_CHUNK)),
        'gm_w_o': nrm(ks[17], (L, GM_WIDTH, D_MODEL), GM_WIDTH ** -0.5),
        'mla_cq_gain': gain(ks[18], (L, MLA_Q_RANK)),
        'mla_ckv_gain': gain(ks[19], (L, MLA_KV_RANK)),
        'mla_w_uq': nrm(ks[20], (L, MLA_Q_RANK, MLA_HEADS * MLA_QK), MLA_Q_RANK ** -0.5),
        'mla_w_ukv': nrm(ks[21], (L, MLA_KV_RANK, MLA_HEADS * (MLA_NOPE + MLA_V)), MLA_KV_RANK ** -0.5),
        'mla_q_gain': gain(ks[22], (L, MLA_QK)),
        'mla_k_gain': gain(ks[23], (L, MLA_QK)),
        'mla_w_o': nrm(ks[24], (L, MLA_HEADS * MLA_V, D_MODEL), (MLA_HEADS * MLA_V) ** -0.5),
        'w_out': nrm(ks[25], (L, D_MODEL, D_MODEL), D_MODEL ** -0.5),
        'ffn_w1': nrm(ks[26], (L, D_MODEL, FFN_HIDDEN), D_MODEL ** -0.5),
        'ffn_w2': nrm(ks[27], (L, FFN_HIDDEN, D_MODEL), FFN_HIDDEN ** -0.5),
    }

def second_block(x, c, ctx, c_ctx, w_mod, b_mod, g_norm1, g_norm2, w_in, na_q_gain, na_k_gain, na_rpb,
              na_w_o, gm_ln_g, gm_ln_b, gm_w_s, gm_b_s, gm_w_o, mla_cq_gain, mla_ckv_gain, mla_w_uq,
              mla_w_ukv, mla_q_gain, mla_k_gain, mla_w_o, w_out, ffn_w1, ffn_w2):
    rope = axial_rope(x.shape[1])
    s_c = jax.nn.silu(c)
    s_ctx = jax.nn.silu(c_ctx)[None]
    for i in range(DEPTH_2):
        last = i == DEPTH_2 - 1
        mod = (s_c @ w_mod[i] + b_mod[i])[:, None, :]
        sh1, sc1, gt1, sh2, sc2, gt2 = jnp.split(mod, 6, axis=-1)
        n_mod_c = 2 * D_MODEL if last else 6 * D_MODEL
        mod_c = (s_ctx @ w_mod[i][:, :n_mod_c] + b_mod[i][:n_mod_c])[:, None, :]
        mc = jnp.split(mod_c, n_mod_c // D_MODEL, axis=-1)

        h = modulate(rms_norm_2(x, g_norm1[i]), sh1, sc1)
        hc = modulate(rms_norm_2(ctx, g_norm1[i]), mc[0], mc[1])
        p = h @ w_in[i]
        pc = hc @ w_in[i][:, :(N_CTX_COLS if last else N_IN_COLS)]

        k_na_c = rms_norm_2(split_heads(cols(pc, OFF_NA_K, NA_WIDTH), NA_HEADS), na_k_gain[i])
        v_na_c = split_heads(cols(pc, OFF_NA_V, NA_WIDTH), NA_HEADS)
        k_mla_c, v_mla_c = mla_keys_values(cols(pc, OFF_MLA_CKV, MLA_KV_RANK), cols(pc, OFF_MLA_KR, MLA_ROPE),
                                           mla_ckv_gain[i], mla_w_ukv[i], mla_k_gain[i], None)

        q_na = rms_norm_2(split_heads(cols(p, OFF_NA_Q, NA_WIDTH), NA_HEADS), na_q_gain[i])
        k_na = rms_norm_2(split_heads(cols(p, OFF_NA_K, NA_WIDTH), NA_HEADS), na_k_gain[i])
        v_na = split_heads(cols(p, OFF_NA_V, NA_WIDTH), NA_HEADS)
        y_na = merge_heads(neighbourhood_attention(q_na, k_na, v_na, k_na_c, v_na_c, na_rpb[i]))
        y_gm = spatial_gating(jax.nn.gelu(cols(p, OFF_GM_U, GM_WIDTH), approximate=False),
                              jax.nn.gelu(cols(p, OFF_GM_V, GM_WIDTH), approximate=False),
                              gm_ln_g[i], gm_ln_b[i], gm_w_s[i], gm_b_s[i])
        q_mla = mla_queries(cols(p, OFF_MLA_CQ, MLA_Q_RANK), mla_cq_gain[i], mla_w_uq[i], mla_q_gain[i], rope)
        k_mla, v_mla = mla_keys_values(cols(p, OFF_MLA_CKV, MLA_KV_RANK), cols(p, OFF_MLA_KR, MLA_ROPE),
                                       mla_ckv_gain[i], mla_w_ukv[i], mla_k_gain[i], rope)
        y_mla = merge_heads(dense_attention(q_mla, jnp.concatenate([k_mla_c, k_mla], axis=2),
                                            jnp.concatenate([v_mla_c, v_mla], axis=2)))
        mix = merge_branches(y_na, y_gm, y_mla, cols(p, OFF_GATES, N_BRANCHES * D_MODEL),
                             na_w_o[i], gm_w_o[i], mla_w_o[i], w_out[i])
        x_new = x + gt1 * mix
        x_new = x_new + gt2 * squared_relu_mlp(modulate(rms_norm_2(x_new, g_norm2[i]), sh2, sc2),
                                               ffn_w1[i], ffn_w2[i])

        if not last:
            q_na_c = rms_norm_2(split_heads(cols(pc, OFF_NA_Q, NA_WIDTH), NA_HEADS), na_q_gain[i])
            y_na_c = merge_heads(dense_attention(q_na_c, k_na_c, v_na_c))
            y_gm_c = spatial_gating(jax.nn.gelu(cols(pc, OFF_GM_U, GM_WIDTH), approximate=False),
                                    jax.nn.gelu(cols(pc, OFF_GM_V, GM_WIDTH), approximate=False),
                                    gm_ln_g[i], gm_ln_b[i], gm_w_s[i], gm_b_s[i])
            q_mla_c = mla_queries(cols(pc, OFF_MLA_CQ, MLA_Q_RANK), mla_cq_gain[i], mla_w_uq[i],
                                  mla_q_gain[i], None)
            y_mla_c = merge_heads(dense_attention(q_mla_c, k_mla_c, v_mla_c))
            mix_c = merge_branches(y_na_c, y_gm_c, y_mla_c, cols(pc, OFF_GATES, N_BRANCHES * D_MODEL),
                                   na_w_o[i], gm_w_o[i], mla_w_o[i], w_out[i])
            ctx = ctx + mc[2] * mix_c
            ctx = ctx + mc[5] * squared_relu_mlp(modulate(rms_norm_2(ctx, g_norm2[i]), mc[3], mc[4]),
                                                 ffn_w1[i], ffn_w2[i])
        x = x_new
    return x


def setup_inputs(seed=0):
    out = dict(first_inputs(seed))
    for name, value in second_inputs(seed + 1).items():
        if name != "x":
            out[name + "_2"] = value
    return out


def reference(
    x, p, mix_norm_g, w_in, ret_gn_g, ret_gn_b, w_ret_o, q_norm_g, k_norm_g, attn_sinks,
    w_swa_o, w_out, ffn_norm_g, w_router_group, b_router_group, w_router_expert,
    b_router_expert, w_exp_gate, w_exp_up, w_exp_down, ple_gate_norm_g, w_ple_gate, w_ple,
    ple_norm_g, c_2, ctx_2, c_ctx_2, w_mod_2, b_mod_2, g_norm1_2, g_norm2_2, w_in_2,
    na_q_gain_2, na_k_gain_2, na_rpb_2, na_w_o_2, gm_ln_g_2, gm_ln_b_2, gm_w_s_2, gm_b_s_2,
    gm_w_o_2, mla_cq_gain_2, mla_ckv_gain_2, mla_w_uq_2, mla_w_ukv_2, mla_q_gain_2,
    mla_k_gain_2, mla_w_o_2, w_out_2, ffn_w1_2, ffn_w2_2,
):
    x = first_block(
        x, p, mix_norm_g, w_in, ret_gn_g, ret_gn_b, w_ret_o, q_norm_g, k_norm_g, attn_sinks,
        w_swa_o, w_out, ffn_norm_g, w_router_group, b_router_group, w_router_expert,
        b_router_expert, w_exp_gate, w_exp_up, w_exp_down, ple_gate_norm_g, w_ple_gate, w_ple,
        ple_norm_g,
    )
    return second_block(
        x, c_2, ctx_2, c_ctx_2, w_mod_2, b_mod_2, g_norm1_2, g_norm2_2, w_in_2, na_q_gain_2,
        na_k_gain_2, na_rpb_2, na_w_o_2, gm_ln_g_2, gm_ln_b_2, gm_w_s_2, gm_b_s_2, gm_w_o_2,
        mla_cq_gain_2, mla_ckv_gain_2, mla_w_uq_2, mla_w_ukv_2, mla_q_gain_2, mla_k_gain_2,
        mla_w_o_2, w_out_2, ffn_w1_2, ffn_w2_2,
    )


_drawn_inputs = setup_inputs


def setup_inputs(seed=0):
    import zlib

    import numpy as np

    out = dict(_drawn_inputs(seed))
    spreads = {}
    factors = {'ret_gn_g': 3.67,
     'q_norm_g': 4.237,
     'k_norm_g': 4.325,
     'b_router_group': 3.081,
     'b_router_expert': 2.678,
     'ple_gate_norm_g': 8.0,
     'ple_norm_g': 6.32,
     'ctx_2': 3.168,
     'g_norm1_2': 8.0,
     'g_norm2_2': 5.313,
     'na_q_gain_2': 8.0,
     'na_k_gain_2': 8.0,
     'na_rpb_2': 43.308,
     'gm_ln_g_2': 8.0,
     'gm_ln_b_2': 8.0,
     'gm_b_s_2': 8.0,
     'mla_cq_gain_2': 8.0,
     'mla_ckv_gain_2': 8.0,
     'mla_w_uq_2': 2.936,
     'mla_q_gain_2': 8.0,
     'mla_k_gain_2': 8.0,
     'attn_sinks': 8.0}
    for name, (base, spread) in spreads.items():
        noise = np.random.default_rng([zlib.crc32(name.encode()), seed]).standard_normal(out[name].shape)
        drawn = base * np.exp(spread * noise) if base else spread * noise
        out[name] = jnp.asarray(drawn.astype(out[name].dtype))
    for name, factor in factors.items():
        out[name] = (out[name] * factor).astype(out[name].dtype)
    return out
```

```python
from contextlib import ExitStack

import numpy as np

import concourse.bass as bass
from concourse import mybir

F32 = mybir.dt.float32
ALU = mybir.AluOpType
ACT = mybir.ActivationFunctionType
AX = mybir.AxisListType

P = 128
D = 1024
KD = D // P
S = 256
ST = S // P
EPS = 1e-6
NEG = -1e30

RET_H, RET_D = 4, 128
SWA_H, SWA_D, SWA_KV = 8, 64, 2
N_GROUPS, PER_GROUP, FF = 4, 8, 256
N_EXP = N_GROUPS * PER_GROUP
FT = FF // P
NA_H, NA_D = 8, 64
GRID_W, WIN_W = 64, 16
GM_G = 4
MLA_H, MLA_QK, MLA_NOPE, MLA_ROPE, MLA_V = 8, 96, 64, 32, 64
FFN = 4 * D

C1 = dict(rq=0, rk=512, rv=1024, rg=1536, sq=2048, sk=2560, sv=2688, gates=2816)
C2 = dict(k=0, v=512, ckv=1024, kr=1152, q=1184, u=1696, gv=2208, cq=2720, gates=2976)

VEC_COLS = [("eps", 1), ("mix_g", 8), ("ffn_g", 8), ("pleg_g", 8), ("ple_g", 8), ("ret_g", 4), ("ret_b", 4),
            ("qn_g", 1), ("kn_g", 1), ("sinks", 8), ("c", 16), ("priority", 8)]
for _l in (0, 1):
    VEC_COLS += [(f"{n}{_l}", w) for n, w in
                 (("g1_", 8), ("g2_", 8), ("naq_", 1), ("nak_", 1), ("cq_", 2), ("ckv_", 1), ("mq_", 1),
                  ("mk_", 1), ("bmod_", 48))]
VEC_AT, _n = {}, 0
for _name, _w in VEC_COLS:
    VEC_AT[_name] = (_n, _w)
    _n += _w
N_VEC = _n

LC_G, LC_B, LC_WS, LC_BS, N_LC = 0, 512, 1024, 1536, 2048

RING = 3
SLOT = 4096
PH_MOE, PH_FIRST, PH_L0, PH_END = 7, 9, 18, 27
ACC = 4
N_P = 3


class Plan:

    def __init__(self):
        self.blocks = []
        self.block_at = {}
        self.block_end = {}
        self.parts = 0
        self.tiles = []
        self.tile_at = {}
        self.freed = {}
        self.read = {"act": 0, "dve": 0}
        self.att = []
        self.att_at = {}
        self.units = 0

    def block(self, name, source, kt, cols):
        self.block_at[name] = len(self.blocks)
        self.blocks.append((name, source, kt, cols))

    def tile(self, name, reader, block=None):
        self.tile_at[name] = len(self.tiles)
        self.tiles.append((name, reader))
        self.read[reader] += 1
        self.freed[name] = (reader, self.read[reader])
        if block is not None:
            self.block_end[block] = ("tile", len(self.tiles))

    def attention(self, n):
        u0 = self.units
        self.units += n

        def put(kind, u):
            self.att_at[(kind, u0 + u)] = len(self.att)
            self.att.append((kind, u0 + u))
        put("S", 0)
        if n > 1:
            put("S", 1)
        for u in range(n):
            put("T", u)
            if u + 2 < n:
                put("S", u + 2)
            put("O", u)


def merge_blocks(plan, L, w_in, gates, w_o, T):
    for b, w in enumerate(w_o):
        for hf in range(2):
            c = gates + b * D + hf * 512
            plan.block(f"{L}gate{b}{hf}", w_in[:, c:c + 512], 8, 512)
            for j in range(4):
                plan.tile(f"{L}gate{b}{hf}{j}", "act", f"{L}gate{b}{hf}")
            plan.block(f"{L}o{b}{hf}", w[:, hf * 512:hf * 512 + 512], 4, 512)
            for j in range(4):
                plan.tile(f"{L}o{b}{hf}{j}", "dve", f"{L}o{b}{hf}")


def make_plan(t):
    plan = Plan()
    for l in range(2):
        for b in range(12):
            plan.block(f"mod{l}{b}", t["w_mod"][l][:, b * 512:b * 512 + 512], 8, 512)
            plan.tile(f"mod{l}{b}", "dve", f"mod{l}{b}")
    plan.tile("n_mix", "act")
    w = t["w_in"]
    for name in ("rq", "rk"):
        plan.block(name, w[:, C1[name]:C1[name] + 512], 8, 512)
        for j in range(4):
            plan.tile(f"{name}{j}", "act", name)
    plan.block("rv", w[:, C1["rv"]:C1["rv"] + 512], 8, 512)
    for j in range(ST):
        plan.tile(f"rv{j}", "act", "rv")
    for name in ("rg", "sq"):
        plan.block(name, w[:, C1[name]:C1[name] + 512], 8, 512)
        for j in range(4):
            plan.tile(f"{name}{j}", "act", name)
    plan.block("sksv", w[:, C1["sk"]:C1["sk"] + 256], 8, 256)
    for j in range(SWA_KV):
        plan.tile(f"sk{j}", "act", "sksv")
    for j in range(ST):
        plan.tile(f"sv{j}", "act", "sksv")
    for h in range(RET_H):
        plan.tile(f"ret_s{h}", "dve")
        plan.tile(f"ret_y{h}", "act")
    for j in range(2):
        plan.tile(f"ret_mean{j}", "dve")
    for j in range(2):
        plan.tile(f"ret_var{j}", "act")
    for j in range(3):
        plan.tile(f"hn1_{j}", "act")
    plan.attention(ST * SWA_H)
    merge_blocks(plan, "A", w, C1["gates"], [t["w_ret_o"], t["w_swa_o"]], S)
    for hf in range(2):
        plan.block(f"Aout{hf}", t["w_out"][:, hf * 512:hf * 512 + 512], 8, 512)
        for j in range(4):
            plan.tile(f"Aout{hf * 4 + j}", "dve", f"Aout{hf}")
    plan.tile("n_ffn", "act")
    plan.block("router", t["w_r"], 8, 36)
    for j in range(ST):
        plan.tile(f"router{j}", "dve", "router")
    plan.tile("combT", "act")
    plan.n_before_moe = len(plan.blocks)
    plan.block("ple", t["w_ple"], 2, 1024)
    for j in range(8):
        plan.tile(f"ple{j}", "act", "ple")
    plan.tile("n_pleg", "act")
    plan.tile("n_ple", "act")
    for hf in range(2):
        plan.block(f"pleg{hf}", t["w_ple_gate"][:, hf * 512:hf * 512 + 512], 8, 512)
        for j in range(4):
            plan.tile(f"pleg{hf * 4 + j}", "act", f"pleg{hf}")
    for l in range(2):
        L = f"B{l}"
        tok = 2 * S if l == 0 else S
        w = t["w_in_2"][l]
        plan.tile(f"{L}n1", "act")

        def fm(name, col, n=4):
            plan.block(L + name, w[:, col:col + n * P], 8, n * P)
            for j in range(n):
                plan.tile(f"{L}{name}{j}", "act", L + name)

        def tm(name, col, n):
            plan.block(L + name, w[:, col:col + 512], 8, 512)
            for j in range(n):
                plan.tile(f"{L}{name}{j}", "act", L + name)
        fm("k", C2["k"])
        tm("v", C2["v"], 4)
        plan.block(L + "ckv", w[:, C2["ckv"]:C2["ckv"] + 160], 8, 160)
        plan.tile(L + "ckv0", "act", L + "ckv")
        plan.tile(L + "kr0", "act", L + "ckv")
        fm("q", C2["q"])
        fm("cq", C2["cq"], 2)
        fm("u", C2["u"])
        tm("gv", C2["gv"], tok // P)
        for j in range(4 + 4 * tok // 512):
            plan.tile(f"{L}hn{j}", "act")
        plan.tile(L + "n_cq", "act")
        plan.tile(L + "n_ckv", "act")
        for j in range(tok // P):
            plan.tile(f"{L}mix{j}", "dve")
        plan.attention(tok // P * NA_H)
        plan.block(L + "uq", t["w_uq"][l], 2, MLA_H * MLA_QK)
        plan.block(L + "ukv", t["w_ukv"][l], 1, MLA_H * (MLA_QK + MLA_V))
        n = 2 * MLA_H

        def raw(i):
            plan.tile(f"{L}raw{i}", "dve", L + ("uq" if i < MLA_H else "ukv"))
        raw(0)
        for i in range(n):
            if i + 1 < n:
                raw(i + 1)
            plan.tile(f"{L}ss{i}", "act")
            plan.tile(f"{L}rx{i}", "dve")
        for j in range(4):
            plan.tile(f"{L}mv{j}", "act", L + "ukv")
        plan.attention(tok // P * MLA_H)
        merge_blocks(plan, L, w, C2["gates"], [t["na_w_o"][l], t["gm_w_o"][l], t["mla_w_o"][l]], tok)
        for hf in range(2):
            plan.block(f"{L}out{hf}", t["w_out_2"][l][:, hf * 512:hf * 512 + 512], 8, 512)
            for j in range(4):
                plan.tile(f"{L}out{hf * 4 + j}", "dve", f"{L}out{hf}")
        plan.tile(f"{L}n2", "act")
        for b in range(8):
            plan.block(f"{L}w1_{b}", t["ffn_w1"][l][:, b * 512:b * 512 + 512], 8, 512)
            for j in range(4):
                plan.tile(f"{L}up{b * 4 + j}", "act", f"{L}w1_{b}")
        for hf in range(2):
            for kb in range(4):
                plan.block(f"{L}w2_{hf}{kb}",
                           t["ffn_w2"][l][kb * D:kb * D + D, hf * 512:hf * 512 + 512], 8, 512)
                if kb < 3:
                    plan.parts += 1
                    plan.block_end[f"{L}w2_{hf}{kb}"] = ("part", plan.parts)
            for j in range(4):
                plan.tile(f"{L}down{hf * 4 + j}", "dve", f"{L}w2_{hf}3")
    return plan


def program(nc, t, out):
    plan = make_plan(t)
    ctx = ExitStack()
    with ctx:
        def sb(name, shape):
            return ctx.enter_context(nc.sbuf_tensor(name, shape, F32))

        def sem(name):
            return ctx.enter_context(nc.semaphore(name))

        X = sb("X", [P, KD, 2 * S])
        H = sb("H", [P, KD, 2 * S])
        ring = sb("ring", [P, RING, SLOT])
        A = sb("A", [P, 16384])
        BR = sb("BR", [P, 4096])
        SQ = sb("SQ", [P, 2, 512])
        SCR = sb("SCR", [P, 2592])
        R = sb("R", [P, 2, 512])
        TMP = sb("TMP", [P, 2, 512])
        CST = sb("CST", [P, 3, P])
        VEC = sb("VEC", [P, N_VEC])
        LC = sb("LC", [P, N_LC])
        ROPE = sb("ROPE", [P, 2 * S + 2 * MLA_QK])
        MOD = sb("MOD", [P, 2, 48, 2])
        MA = sb("MA", [P, 2, 2, KD])
        SC = sb("SC", [P, KD, 2])
        SM = sb("SM", [P, 320])
        PS = ctx.enter_context(nc.psum_tensor("PS", [P, 8, 512], F32))
        comb_rows = t["comb_rows"]

        IDENT, ONES, BLK = CST[:, 0, :], CST[:, 1, :], CST[:, 2, :]
        COS, SIN = ROPE[0:MLA_QK, 0:S], ROPE[0:MLA_QK, S:2 * S]
        ROT = ROPE[0:MLA_QK, 2 * S:2 * S + MLA_QK]
        KR_AT = ROPE[0:MLA_ROPE, 2 * S + MLA_QK:2 * S + 2 * MLA_QK]
        PROB = SCR[:, 0:N_P * 520].rearrange("p (b n) -> p b n", b=N_P)
        PT = SCR[:, N_P * 520:N_P * 520 + 1024].rearrange("p (b n) -> p b n", b=2)
        SG = SCR[:, 0:2048].rearrange("p (j n) -> p j n", j=4)
        EPS_COL = VEC[:, 0:1]
        NM, SUM, RIN, MX = (SM[:, 4 * i:4 * i + N_P] for i in range(4))

        def vec(name, k=0):
            at = VEC_AT[name][0] + k
            return VEC[:, at:at + 1]

        def cut(at, n, w):
            return A[:, at:at + n * w].rearrange("p (n w) -> p n w", n=n)

        RQ, RK, RV, RG = cut(0, 4, S), cut(1024, 4, S), cut(2048, ST, 512), cut(3072, 4, S)
        QK, SV, YR, YS = cut(4096, 6, S), cut(5632, ST, P), cut(5888, 4, S), cut(6912, 4, S)
        RSM = cut(7936, 2, 384)
        PIN = cut(15872, 2, S)
        BRET = BR[:, 0:1536].rearrange("p (h n) -> p h n", h=RET_H)
        BSWA = BR[:, 1536:3584].rearrange("p (h n) -> p h n", h=SWA_H)
        BCOMB = cut(0, N_EXP, S)
        SGM, HID = cut(8192, 2, 512), cut(9216, 2, 512)
        CT = A[0:N_EXP, 10240:10496]
        PL = cut(0, KD, S)
        PLSQ = cut(2048, KD, S)

        loaded_in = sem("loaded_in")
        landed = [sem(f"weights_landed{i}") for i in range(RING)]
        part_used = sem("part_used")
        tile_ready = sem("tile_ready")
        freed = {"act": sem("tile_freed_by_act"), "dve": sem("tile_freed_by_dve")}
        phase = {e: sem(f"phase_{e}") for e in ("pe", "act", "dve")}
        act_step, dve_step = sem("act_step"), sem("dve_step")
        squares, rstd, scaled, normed = sem("squares"), sem("rstd"), sem("scaled"), sem("normed")
        silu_c, modded, evac = sem("silu_c"), sem("modded"), sem("evacuated")
        masked = sem("ret_masked")
        centred, varsq = sem("ret_centred"), sem("ret_varsq")
        hn_sq, hn_rstd = sem("head_squares"), sem("head_rstd")
        scores_ready, negmax, exp_done, probs = (sem("scores_ready"), sem("negmax_ready"), sem("exp_done"),
                                                 sem("probs_ready"))
        pt_ready, pt_copied, o_ready, o_stored = (sem("pt_ready"), sem("pt_copied"), sem("o_ready"),
                                                  sem("o_stored"))
        gate_ready, merged = sem("gate_ready"), sem("merged")
        combined, comb_out, comb_in, comb_t = sem("combined"), sem("comb_out"), sem("comb_in"), sem("comb_t")
        gu_landed = [sem(f"gu_landed{i}") for i in range(2)]
        dn_landed = [sem(f"dn_landed{i}") for i in range(2)]
        gu_ready, moe_silu, moe_mul, moe_hid, moe_down = (sem("gu_ready"), sem("moe_silu"), sem("moe_mul"),
                                                          sem("moe_hid"), sem("moe_down"))
        y_done = sem("moe_y_done")
        ml_sq, ml_rstd = sem("mla_squares"), sem("mla_rstd")
        gv_stats, gv_rstd, lc_loaded, bias_loaded = (sem("gv_stats"), sem("gv_rstd"), sem("lc_loaded"),
                                                     sem("bias_loaded"))
        hid_relu, hid_ready = sem("hid_relu"), sem("hid_ready")
        stored = sem("stored")
        hn_done, gate_used, ml_done = sem("head_norm_done"), sem("gate_used"), sem("mla_done")
        router_group, router_exp, router_top = sem("router_group"), sem("router_exp"), sem("router_top")

        def lens(l):
            T = 2 * S if l == 0 else S
            return dict(
                T=T, NQ=cut(0, 4, T), NK=cut(2048, 4, 512), NV=cut(4096, 4, 512), YN=cut(6144, 4, T),
                U=cut(8192, 4, T), GV=cut(10240, T // P, 512), CQ=cut(12288, 2, T), CKV=cut(13312, 1, 512),
                KR=A[0:MLA_ROPE, 13824:14336], YM=cut(14336, 4, T), MQ=cut(0, MLA_H, T), MV=cut(4096, 4, 512),
                MK=BR[:, :].rearrange("p (h n) -> p h n", h=MLA_H),
                BIAS=BR[:, :].rearrange("p (t h n) -> p t h n", t=ST, h=NA_H),
                Y=BR[:, 0:KD * T].rearrange("p (k n) -> p k n", k=KD),
                HID=cut(0, 32, T))

        def bank_of(name):
            return PS[:, plan.tile_at[name] % ACC, :]

        def att_bank(kind, u):
            return PS[:, 4 + plan.att_at[(kind, u)] % 4, :]

        def swa_units():
            units = []
            for qt in range(ST):
                for h in range(SWA_H):
                    lo, kv = 64 * (h % 2), h // (SWA_H // SWA_KV)
                    keys = [(QK[lo:lo + 64, 4 + kv, (qt - 1) * P if qt else 0:(qt + 1) * P])]
                    nk = P if qt == 0 else 2 * P
                    units.append(dict(
                        q=QK[lo:lo + 64, h // 2, qt * P:qt * P + P], k=keys[0], nk=nk, scale=SWA_D ** -0.5,
                        bias=BSWA[:, h, 2 * P - nk:2 * P], sink=vec("sinks", h),
                        v=[SV[:, j, kv * 64:kv * 64 + 64] for j in range(qt + 1 - nk // P, qt + 1)],
                        out=YS[lo:lo + 64, h // 2, qt * P:qt * P + P], lo=lo))
            return units

        def dense_units(q, k, v, y, dq, T, bias, lo_q):
            units = []
            for qt in range(T // P):
                k0, nk = (0, 512) if qt < ST else (S, S)
                for h in range(8):
                    lo = 64 * (h % 2)
                    units.append(dict(
                        q=q(h, qt * P), k=k(h, k0, nk), nk=nk, scale=dq ** -0.5,
                        bias=bias[:, qt, h, :] if bias is not None and qt < ST else None, sink=None,
                        v=[v[:, j, h * 64:h * 64 + 64] for j in range(k0 // P, (k0 + nk) // P)],
                        out=y[lo:lo + 64, h // 2, qt * P:qt * P + P], lo=lo))
            return units

        def na_units(l):
            b = lens(l)
            return dense_units(
                lambda h, c: b["NQ"][64 * (h % 2):64 * (h % 2) + 64, h // 2, c:c + P],
                lambda h, c, n: b["NK"][64 * (h % 2):64 * (h % 2) + 64, h // 2, c:c + n],
                b["NV"], b["YN"], NA_D, b["T"], b["BIAS"], True)

        def mla_units(l):
            b = lens(l)
            return dense_units(lambda h, c: b["MQ"][0:MLA_QK, h, c:c + P],
                               lambda h, c, n: b["MK"][0:MLA_QK, h, c:c + n],
                               b["MV"], b["YM"], MLA_QK, b["T"], None, False)

        block = ctx.enter_context(nc.Block())

        @block.sync
        def _(sp):
            for dst, src in ((VEC[:, :], t["vec"]), (CST[:, :, :], t["cst"]),
                             (X[:, :, 0:S], t["xT"].rearrange("(k p) n -> p k n", p=P)),
                             (X[:, :, S:2 * S], t["ctxT"].rearrange("(k p) n -> p k n", p=P)),
                             (ROPE[:, :], t["rope"]), (BR[:, 0:3584], t["mask1"]),
                             (SM[0:1, 256:256 + 36], t["b_r"]),
                             (PIN, t["pT"].rearrange("(k p) n -> p k n", p=P)),
                             (LC[:, :], t["lc"][0])):
                sp.dma_start(dst, src).then_inc(loaded_in, 16)

            def after(n):
                for e in ("pe", "act", "dve"):
                    sp.wait_ge(phase[e], n)

            def load_block(n, fresh=False):
                name, src, kt, cols = plan.blocks[n]
                if n >= RING and not fresh:
                    kind, count = plan.block_end[plan.blocks[n - RING][0]]
                    sp.wait_ge(tile_ready if kind == "tile" else part_used, count)
                sp.dma_start(ring[:, n % RING, 0:kt * cols].rearrange("p (k n) -> p k n", k=kt),
                             src.rearrange("(k p) n -> p k n", p=P)).then_inc(landed[n % RING], 16)

            def load_gate_up(e, j):
                for g, w in enumerate((t["w_gate"], t["w_up"])):
                    dst = ring[:, j, :].rearrange("p (g k n) -> p g k n", g=2, k=KD)[:, g]
                    sp.dma_start(dst, w[bass.ds(e, 1)].rearrange("e (k p) n -> p (e k) n", p=P)
                                 ).then_inc(gu_landed[j], 16)

            def load_down(e, j):
                dst = ring[:, 2, j * 2048:j * 2048 + 2048].rearrange("p (k n) -> p k n", k=FT)
                sp.dma_start(dst, t["w_down"][bass.ds(e, 1)].rearrange("e (k p) n -> p (e k) n", p=P)
                             ).then_inc(dn_landed[j], 16)

            for n in range(plan.n_before_moe):
                load_block(n)
            for n in range(plan.n_before_moe - RING, plan.n_before_moe):
                sp.wait_ge(tile_ready, plan.block_end[plan.blocks[n][0]][1])
            for e in range(2):
                load_gate_up(e, e)
                load_down(e, e)
            sp.wait_ge(comb_t, 1)
            sp.dma_start(comb_rows, CT).then_inc(comb_out, 16)
            sp.wait_ge(comb_out, 16)
            for q in range(4):
                r = comb_rows.rearrange("e n -> (e n)")[q * 2048:q * 2048 + 2048]
                sp.dma_start(A[:, q * 2048:q * 2048 + 2048],
                             r.rearrange("(o n) -> o n", o=1).broadcast_to([P, 2048])).then_inc(comb_in, 16)
            with sp.Fori(1, N_EXP // 2) as i:
                for j in range(2):
                    sp.wait_ge(gu_ready, 2 * i + (j - 1))
                    load_gate_up(2 * i + j, j)
                    sp.wait_ge(moe_down, 2 * i + (j - 1))
                    load_down(2 * i + j, j)
            after(PH_MOE)
            for n in range(plan.n_before_moe, plan.block_at["B0v"]):
                load_block(n, fresh=n < plan.n_before_moe + RING)
            after(PH_FIRST)
            sp.dma_start(BR[:, :], t["na_bias"][0]).then_inc(bias_loaded, 16)
            for n in range(plan.block_at["B0v"], plan.block_at["B1v"]):
                load_block(n)
            after(PH_L0)
            sp.dma_start(LC[:, :], t["lc"][1]).then_inc(lc_loaded, 16)
            sp.dma_start(BR[:, :], t["na_bias"][1]).then_inc(bias_loaded, 16)
            for n in range(plan.block_at["B1v"], len(plan.blocks)):
                load_block(n)
            after(PH_END)
            sp.dma_start(out.rearrange("(k p) n -> p k n", p=P), X[:, :, 0:S]).then_inc(stored, 16)
            sp.wait_ge(stored, 16)

        @block.tensor
        def _(pe):
            ph = [0]
            c = dict(squares=0, normed=0, evac=0, hn=0, ml=0, unit=0, merged=0)

            def next_phase():
                ph[0] += 1
                pe.drain().then_inc(phase["pe"], 1)
                for e in ("act", "dve"):
                    pe.wait_ge(phase[e], ph[0])

            def open_tile(name):
                n = plan.tile_at[name]
                if n >= ACC:
                    reader, count = plan.freed[plan.tiles[n - ACC][0]]
                    pe.wait_ge(freed[reader], count)
                return PS[:, n % ACC, :]

            def weights(name):
                n = plan.block_at[name]
                _, _, kt, cols = plan.blocks[n]
                pe.wait_ge(landed[n % RING], 16 * (n // RING + 1))
                return ring[:, n % RING, 0:kt * cols].rearrange("p (k n) -> p k n", k=kt)

            def fm(W, tile, c0, M, rhs, kt, T):
                bank = open_tile(tile)
                for k in range(kt):
                    mm = pe.matmul(bank[0:M, 0:T], W[:, k, c0:c0 + M], rhs(k), start=(k == 0), stop=(k == kt - 1))
                mm.then_inc(tile_ready, 1)

            def tm(W, tile, c0, N, tok, kt=KD):
                bank = open_tile(tile)
                for k in range(kt):
                    mm = pe.matmul(bank[:, 0:N], H[:, k, tok:tok + P], W[:, k, c0:c0 + N], start=(k == 0),
                                   stop=(k == kt - 1))
                mm.then_inc(tile_ready, 1)

            def norm_sums(tile, n, sq, T, lhs=None):
                bank = open_tile(tile)
                for k in range(n):
                    c["squares"] += 1
                    pe.wait_ge(squares, c["squares"])
                    mm = pe.matmul(bank[:, 0:T], ONES, sq(k), start=(k == 0), stop=(k == n - 1))
                mm.then_inc(tile_ready, 1)

            def h_ready(n):
                c["normed"] += n
                pe.wait_ge(normed, c["normed"])

            def h(T):
                return lambda k: H[:, k, 0:T]

            def head_sums(tiles):
                for name in tiles:
                    bank = open_tile(name)
                    pe.wait_ge(hn_sq, c["hn"] + 1)
                    pe.matmul(bank[:, :], BLK, SQ[:, c["hn"] % 2, :], start=True, stop=True).then_inc(tile_ready, 1)
                    c["hn"] += 1

            def attention(units):
                u0 = c["unit"]
                c["unit"] += len(units)

                def open_att(kind, u):
                    m = plan.att_at[(kind, u0 + u)]
                    if m >= 4:
                        kd, old = plan.att[m - 4]
                        pe.wait_ge({"S": exp_done, "T": pt_copied, "O": o_stored}[kd], old + 1)
                    return PS[:, 4 + m % 4, :]

                def scores(u):
                    bank, x = open_att("S", u), units[u]
                    pe.matmul(bank[:, 0:x["nk"]], x["q"], x["k"], start=True, stop=True).then_inc(scores_ready, 1)

                def turn(u):
                    bank, x = open_att("T", u), units[u]
                    pe.wait_ge(probs, u0 + u + 1)
                    n = x["nk"] // P
                    for j in range(n):
                        mm = pe.transpose(bank[:, j * P:j * P + P], PROB[:, (u0 + u) % N_P, j * P:j * P + P], IDENT)
                    mm.then_inc(pt_ready, 1)

                def values(u):
                    bank, x = open_att("O", u), units[u]
                    pe.wait_ge(pt_copied, u0 + u + 1)
                    n = x["nk"] // P
                    for j in range(n):
                        mm = pe.matmul(bank[x["lo"]:x["lo"] + 64, 0:P], x["v"][j],
                                       PT[:, (u0 + u) % 2, j * P:j * P + P], start=(j == 0), stop=(j == n - 1))
                    mm.then_inc(o_ready, 1)

                scores(0)
                scores(1)
                for u in range(len(units)):
                    turn(u)
                    if u + 2 < len(units):
                        scores(u + 2)
                    values(u)

            def merge(L, ys, T):
                for b, y in enumerate(ys):
                    for hf in range(2):
                        W = weights(f"{L}gate{b}{hf}")
                        for j in range(4):
                            fm(W, f"{L}gate{b}{hf}{j}", j * P, P, h(T), KD, T)
                        W = weights(f"{L}o{b}{hf}")
                        for j in range(4):
                            fm(W, f"{L}o{b}{hf}{j}", j * P, P, lambda k: y[:, k, 0:T], 4, T)

            def project_out(L, Y, T):
                c["merged"] += KD
                pe.wait_ge(merged, c["merged"])
                for hf in range(2):
                    W = weights(f"{L}out{hf}")
                    for j in range(4):
                        fm(W, f"{L}out{hf * 4 + j}", j * P, P, lambda k: Y[:, k, 0:T], KD, T)

            pe.wait_ge(loaded_in, 16 * 9)
            pe.wait_ge(silu_c, 1)
            for l in range(2):
                for b in range(12):
                    W = weights(f"mod{l}{b}")
                    bank = open_tile(f"mod{l}{b}")
                    for j in range(4):
                        for k in range(KD):
                            mm = pe.matmul(bank[:, 2 * j:2 * j + 2], W[:, k, j * P:j * P + P], SC[:, k, :],
                                           start=(k == 0), stop=(k == KD - 1))
                    mm.then_inc(tile_ready, 1)

            norm_sums("n_mix", KD, h(S), S)
            h_ready(KD)
            for name in ("rq", "rk"):
                W = weights(name)
                for j in range(4):
                    fm(W, f"{name}{j}", j * P, P, h(S), KD, S)
            W = weights("rv")
            for j in range(ST):
                tm(W, f"rv{j}", 0, 512, j * P)
            for name in ("rg", "sq"):
                W = weights(name)
                for j in range(4):
                    fm(W, f"{name}{j}", j * P, P, h(S), KD, S)
            W = weights("sksv")
            for j in range(SWA_KV):
                bank = open_tile(f"sk{j}")
                for half in range(2):
                    for k in range(KD):
                        mm = pe.matmul(bank[64 * half:64 * half + 64, 0:S], W[:, k, j * 64:j * 64 + 64], H[:, k, 0:S],
                                       start=(k == 0), stop=(k == KD - 1))
                mm.then_inc(tile_ready, 1)
            for j in range(ST):
                tm(W, f"sv{j}", P, P, j * P)
            next_phase()
            for hd in range(RET_H):
                bank = open_tile(f"ret_s{hd}")
                pe.matmul(bank[:, 0:S], RK[:, hd, 0:P], RQ[:, hd, :], start=True, stop=True)
                pe.matmul(bank[:, S:S + P], RK[:, hd, P:S], RQ[:, hd, P:S], start=True, stop=True
                          ).then_inc(tile_ready, 1)
                bank = open_tile(f"ret_y{hd}")
                pe.wait_ge(masked, hd + 1)
                pe.matmul(bank[:, 0:S], RV[:, 0, hd * P:hd * P + P], RSM[:, hd % 2, 0:S], start=True, stop=False)
                pe.matmul(bank[:, P:S], RV[:, 1, hd * P:hd * P + P], RSM[:, hd % 2, S:S + P], start=False, stop=True
                          ).then_inc(tile_ready, 1)
            pe.wait_ge(evac, 1)
            yr = YR.rearrange("p h n -> p (h n)")
            for j in range(2):
                pe.matmul(open_tile(f"ret_mean{j}"), ONES, yr[:, j * 512:j * 512 + 512], start=True, stop=True
                          ).then_inc(tile_ready, 1)
            for j in range(2):
                bank = open_tile(f"ret_var{j}")
                pe.wait_ge(varsq, j + 1)
                pe.matmul(bank, ONES, SQ[:, j, :], start=True, stop=True).then_inc(tile_ready, 1)
            next_phase()
            head_sums([f"hn1_{j}" for j in range(3)])
            next_phase()
            attention(swa_units())
            next_phase()
            merge("A", [YR, YS], S)
            project_out("A", BR[:, 0:KD * S].rearrange("p (k n) -> p k n", k=KD), S)
            next_phase()
            norm_sums("n_ffn", KD, h(S), S)
            h_ready(KD)
            W = weights("router")
            for j in range(ST):
                bank = open_tile(f"router{j}")
                for k in range(KD):
                    pe.matmul(bank[:, 0:36], H[:, k, j * P:j * P + P], W[:, k, :], start=(k == 0), stop=False)
                pe.matmul(bank[:, 0:36], ONES[0:1, :], SM[0:1, 256:256 + 36], start=False, stop=True
                          ).then_inc(tile_ready, 1)
            bank = open_tile("combT")
            for j in range(ST):
                pe.wait_ge(combined, j + 1)
                mm = pe.transpose(bank[0:N_EXP, j * P:j * P + P], SM[:, 64 + 32 * j:96 + 32 * j], IDENT)
            mm.then_inc(tile_ready, 1)
            next_phase()

            Y = [PS[:, 4 + d // 2, (d % 2) * S:(d % 2) * S + S] for d in range(KD)]
            for b in range(4):
                pe.matmul(PS[:, 4 + b, :], TMP[:, 0, 0:P], TMP[:, 0, :], start=True, stop=False, skip_group_check=True)

            def gate_up(j):
                W = ring[:, j, :].rearrange("p (g k n) -> p g k n", g=2, k=KD)
                for g in range(2):
                    for f in range(FT):
                        for k in range(KD):
                            mm = pe.matmul(PS[:, 2 * j + g, f * S:f * S + S], W[:, g, k, f * P:f * P + P],
                                           H[:, k, 0:S], start=(k == 0), stop=(k == KD - 1))
                mm.then_inc(gu_ready, 1)

            def down(j):
                W = ring[:, 2, j * 2048:j * 2048 + 2048].rearrange("p (k n) -> p k n", k=FT)
                for d in range(KD):
                    for f in range(FT):
                        mm = pe.matmul(Y[d], W[:, f, d * P:d * P + P], HID[:, j, f * S:f * S + S], start=False,
                                       stop=False, skip_group_check=True)
                mm.then_inc(moe_down, 1)

            pe.wait_ge(gu_landed[0], 32)
            gate_up(0)
            with pe.Fori(0, N_EXP // 2 - 1) as i:
                pe.wait_ge(gu_landed[1], 32 * i + 32)
                pe.wait_ge(moe_mul, 2 * i + 1)
                gate_up(1)
                pe.wait_ge(dn_landed[0], 16 * i + 16)
                pe.wait_ge(moe_hid, 2 * i + 1)
                down(0)
                pe.wait_ge(gu_landed[0], 32 * i + 64)
                pe.wait_ge(moe_mul, 2 * i + 2)
                gate_up(0)
                pe.wait_ge(dn_landed[1], 16 * i + 16)
                pe.wait_ge(moe_hid, 2 * i + 2)
                down(1)
            pe.wait_ge(gu_landed[1], 32 * (N_EXP // 2))
            pe.wait_ge(moe_mul, N_EXP - 1)
            gate_up(1)
            for j in range(2):
                pe.wait_ge(dn_landed[j], 16 * (N_EXP // 2))
                pe.wait_ge(moe_hid, N_EXP - 1 + j)
                down(j)
            next_phase()

            W = weights("ple")
            for j in range(8):
                fm(W, f"ple{j}", j * P, P, lambda k: PIN[:, k, :], 2, S)
            norm_sums("n_pleg", KD, h(S), S)
            h_ready(KD)
            next_phase()
            norm_sums("n_ple", KD, lambda k: PLSQ[:, k, :], S)
            h_ready(KD)
            for hf in range(2):
                W = weights(f"pleg{hf}")
                for j in range(4):
                    fm(W, f"pleg{hf * 4 + j}", j * P, P, h(S), KD, S)
            next_phase()

            for l in range(2):
                L, b = f"B{l}", lens(l)
                T = b["T"]
                norm_sums(f"{L}n1", KD, h(512), 512)
                h_ready(2 * KD)

                def project_fm(name, T, n=4):
                    W = weights(L + name)
                    for j in range(n):
                        fm(W, f"{L}{name}{j}", j * P, P, h(T), KD, T)
                project_fm("k", 512)
                W = weights(L + "v")
                for j in range(4):
                    tm(W, f"{L}v{j}", 0, 512, j * P)
                W = weights(L + "ckv")
                fm(W, L + "ckv0", 0, P, h(512), KD, 512)
                fm(W, L + "kr0", P, MLA_ROPE, h(512), KD, 512)
                project_fm("q", T)
                project_fm("cq", T, 2)
                project_fm("u", T)
                W = weights(L + "gv")
                for j in range(T // P):
                    tm(W, f"{L}gv{j}", 0, 512, j * P)
                next_phase()
                head_sums([f"{L}hn{j}" for j in range(4 + 4 * T // 512)])
                next_phase()
                norm_sums(L + "n_cq", 2, lambda k: SQ[:, k, 0:T], T)
                next_phase()
                norm_sums(L + "n_ckv", 1, lambda k: SQ[:, 0, :], 512)
                next_phase()
                h_ready(3)
                for q in range(T // P):
                    bank = open_tile(f"{L}mix{q}")
                    for g in range(GM_G):
                        pe.matmul(bank[:, g * P:g * P + P], b["GV"][:, q, g * P:g * P + P],
                                  LC[:, LC_WS + g * P:LC_WS + g * P + P], start=True, stop=False)
                        mm = pe.matmul(bank[:, g * P:g * P + P], ONES[0:1, :],
                                       LC[0:1, LC_BS + g * P:LC_BS + g * P + P], start=False, stop=True)
                    mm.then_inc(tile_ready, 1)
                attention(na_units(l))
                next_phase()
                Wq, Wk = weights(L + "uq"), weights(L + "ukv")

                def raw(i):
                    bank, hd = open_tile(f"{L}raw{i}"), i % MLA_H
                    if i < MLA_H:
                        for k in range(2):
                            mm = pe.matmul(bank[0:MLA_QK, 0:T], Wq[:, k, hd * MLA_QK:hd * MLA_QK + MLA_QK],
                                           b["CQ"][:, k, 0:T], start=(k == 0), stop=(k == 1))
                    else:
                        pe.matmul(bank[0:MLA_QK, :], Wk[:, 0, hd * MLA_QK:hd * MLA_QK + MLA_QK], b["CKV"][:, 0, :],
                                  start=True, stop=False)
                        mm = pe.matmul(bank[0:MLA_QK, :], KR_AT, b["KR"], start=False, stop=True)
                    mm.then_inc(tile_ready, 1)
                raw(0)
                for i in range(2 * MLA_H):
                    if i + 1 < 2 * MLA_H:
                        raw(i + 1)
                    Ti = T if i < MLA_H else 512
                    bank = open_tile(f"{L}ss{i}")
                    pe.wait_ge(ml_sq, c["ml"] + i + 1)
                    pe.matmul(bank[0:MLA_QK, 0:Ti], ONES[0:MLA_QK, 0:MLA_QK], SQ[0:MLA_QK, i % 2, 0:Ti], start=True,
                              stop=True).then_inc(tile_ready, 1)
                    bank = open_tile(f"{L}rx{i}")
                    pe.wait_ge(freed["dve"], plan.freed[f"{L}raw{i}"][1])
                    src = b["MQ"][0:MLA_QK, i, 0:S] if i < MLA_H else b["MK"][0:MLA_QK, i - MLA_H, 0:S]
                    pe.matmul(bank[0:MLA_QK, 0:S], ROT, src, start=True, stop=True).then_inc(tile_ready, 1)
                c["ml"] += 2 * MLA_H
                for j in range(4):
                    bank = open_tile(f"{L}mv{j}")
                    pe.matmul(bank, b["CKV"][:, 0, j * P:j * P + P],
                              Wk[:, 0, MLA_H * MLA_QK:MLA_H * MLA_QK + 512], start=True, stop=True
                              ).then_inc(tile_ready, 1)
                next_phase()
                attention(mla_units(l))
                next_phase()
                merge(L, [b["YN"], b["U"], b["YM"]], T)
                project_out(L, b["Y"], T)
                next_phase()
                norm_sums(f"{L}n2", KD, h(T), T)
                h_ready(T // S * KD)
                for q in range(8):
                    W = weights(f"{L}w1_{q}")
                    for j in range(4):
                        fm(W, f"{L}up{q * 4 + j}", j * P, P, h(T), KD, T)
                pe.wait_ge(hid_ready, 32 * (l + 1))
                for hf in range(2):
                    banks = [open_tile(f"{L}down{hf * 4 + j}") for j in range(4)]
                    for kb in range(4):
                        W = weights(f"{L}w2_{hf}{kb}")
                        for j in range(4):
                            for k in range(8):
                                mm = pe.matmul(banks[j][:, 0:T], W[:, k, j * P:j * P + P],
                                               b["HID"][:, kb * 8 + k, :], start=(kb == 0 and k == 0),
                                               stop=(kb == 3 and k == 7))
                            if kb == 3:
                                mm.then_inc(tile_ready, 1)
                        if kb < 3:
                            mm.then_inc(part_used, 1)
                next_phase()

        @block.scalar
        def _(act):
            ph = [0]
            c = dict(step=0, squares=0, rstd=0, hn=0, hnr=0, ml=0, unit=0, gate=0)

            def next_phase():
                ph[0] += 1
                act.drain().then_inc(phase["act"], 1)
                for e in ("pe", "dve"):
                    act.wait_ge(phase[e], ph[0])

            def step(ins):
                c["step"] += 1
                ins.then_inc(act_step, 1)
                act.wait_ge(act_step, c["step"])

            def bank(name):
                act.wait_ge(tile_ready, plan.tile_at[name] + 1)
                return bank_of(name)

            def inverse_root(name, r, inv, T, M=P):
                act.activation(r, bank(name)[0:M, 0:T], ACT.Ln, bias=VEC[0:M, 0:1], scale=inv
                               ).then_inc(freed["act"], 1)
                act.wait_ge(freed["act"], plan.freed[name][1])
                return act.activation(r, r, ACT.Exp, scale=-0.5)

            def ln_exp():
                act.preload_act_table_set("natural_log_exp_and_others")

            def norm(tile, n, src, sq, T, inv):
                ln_exp()
                for k in range(n):
                    act.activation(sq(k), src(k), ACT.Square).then_inc(squares, 1)
                inverse_root(tile, R[:, 0, 0:T], inv, T).then_inc(rstd, 1)

            def evacuate(name, dst, func=ACT.Copy, M=P, T=512):
                act.activation(dst, bank(name)[0:M, 0:T], func).then_inc(freed["act"], 1)

            def head_norms(tiles, chunk):
                ln_exp()
                n = len(tiles)

                def square(i):
                    act.activation(SQ[:, (c["hn"] + i) % 2, :], chunk(i), ACT.Square).then_inc(hn_sq, 1)
                square(0)
                for i in range(n):
                    if i + 1 < n:
                        square(i + 1)
                    if c["hn"] + i >= 2:
                        act.wait_ge(hn_done, c["hn"] + i - 1)
                    inverse_root(tiles[i], R[:, (c["hn"] + i) % 2, :], 1.0 / 64, 512).then_inc(hn_rstd, 1)
                c["hn"] += n

            def attention(units):
                u0 = c["unit"]
                c["unit"] += len(units)
                ln_exp()

                def expo(u):
                    g, x = u0 + u, units[u]
                    act.wait_ge(negmax, g + 1)
                    if x["bias"] is None:
                        if g >= N_P:
                            act.wait_ge(pt_ready, g - N_P + 1)
                        src, scale, n = att_bank("S", g)[:, 0:x["nk"]], x["scale"], x["nk"]
                    else:
                        n = x["nk"] + (x["sink"] is not None)
                        src, scale = PROB[:, g % N_P, 0:n], 1.0
                    act.activation(PROB[:, g % N_P, 0:n], src, ACT.Exp, bias=NM[:, g % N_P:g % N_P + 1],
                                   scale=scale, accum_out=SUM[:, g % N_P:g % N_P + 1]).then_inc(exp_done, 1)

                def copy_turned(u):
                    g, x = u0 + u, units[u]
                    act.wait_ge(pt_ready, g + 1)
                    if g >= 2:
                        act.wait_ge(o_ready, g - 1)
                    act.activation(PT[:, g % 2, 0:x["nk"]], att_bank("T", g)[:, 0:x["nk"]], ACT.Copy
                                   ).then_inc(pt_copied, 1)
                expo(0)
                for u in range(len(units)):
                    if u + 1 < len(units):
                        expo(u + 1)
                    copy_turned(u)

            def merge(L, n, T):
                for b in range(n):
                    for hf in range(2):
                        for j in range(4):
                            if b or hf:
                                prev = f"{L}o{b if hf else b - 1}{1 - hf}{j}"
                                act.wait_ge(freed["dve"], plan.freed[prev][1])
                            name = f"{L}gate{b}{hf}{j}"
                            evacuate(name, SG[:, j, 0:T], ACT.Sigmoid, T=T)

            act.wait_ge(loaded_in, 16 * 9)
            at = VEC_AT["c"][0]
            act.activation(SC[:, :, :].rearrange("p k s -> p (k s)"), VEC[:, at:at + 16], ACT.Silu
                           ).then_inc(silu_c, 1)

            norm("n_mix", KD, lambda k: X[:, k, 0:S], lambda k: H[:, k, 0:S], S, 1.0 / D)
            for j in range(4):
                evacuate(f"rq{j}", RQ[:, j, :], T=S)
            for j in range(4):
                evacuate(f"rk{j}", RK[:, j, :], T=S)
            for j in range(ST):
                evacuate(f"rv{j}", RV[:, j, :])
            for j in range(4):
                evacuate(f"rg{j}", RG[:, j, :], ACT.Silu, T=S)
            for j in range(4):
                evacuate(f"sq{j}", QK[:, j, :], T=S)
            for j in range(SWA_KV):
                evacuate(f"sk{j}", QK[:, 4 + j, :], T=S)
            for j in range(ST):
                evacuate(f"sv{j}", SV[:, j, :], T=P)
            next_phase()
            ln_exp()
            for hd in range(RET_H):
                act.activation(YR[:, hd, :], bank(f"ret_y{hd}")[:, 0:S], ACT.Copy).then_inc(freed["act"], 1)
            act.drain().then_inc(evac, 1)
            yr = YR.rearrange("p h n -> p (h n)")
            for j in range(2):
                act.wait_ge(centred, j + 1)
                act.activation(SQ[:, j, :], yr[:, j * 512:j * 512 + 512], ACT.Square).then_inc(varsq, 1)
            for j in range(2):
                inverse_root(f"ret_var{j}", R[:, j, :], 1.0 / RET_D, 512).then_inc(rstd, 1)
            next_phase()
            qk = QK.rearrange("p j n -> p (j n)")
            head_norms([f"hn1_{j}" for j in range(3)], lambda i: qk[:, i * 512:i * 512 + 512])
            next_phase()
            attention(swa_units())
            next_phase()
            merge("A", 2, S)
            next_phase()
            norm("n_ffn", KD, lambda k: X[:, k, 0:S], lambda k: H[:, k, 0:S], S, 1.0 / D)
            for j in range(ST):
                r = TMP[:, 1, j * S:j * S + S]
                act.wait_ge(router_group, j + 1)
                act.activation(r[:, 44:48], r[:, 40:44], ACT.Exp, accum_out=r[:, 48:49]).then_inc(router_exp, 1)
                act.wait_ge(router_top, j + 1)
                act.activation(r[:, 107:108], r[:, 106:107], ACT.Exp).then_inc(router_exp, 1)
            evacuate("combT", CT, M=N_EXP, T=S)
            act.wait_ge(freed["act"], plan.freed["combT"][1])
            act.drain().then_inc(comb_t, 1)
            next_phase()

            def moe_act(j):
                act.activation(SGM[:, j, :], PS[:, 2 * j, :], ACT.Silu).then_inc(moe_silu, 1)
            for j in range(2):
                act.wait_ge(gu_ready, j + 1)
                moe_act(j)
            with act.Fori(1, N_EXP // 2) as i:
                for j in range(2):
                    act.wait_ge(gu_ready, 2 * i + (j + 1))
                    act.wait_ge(moe_hid, 2 * i + (j - 1))
                    moe_act(j)
            next_phase()
            for j in range(8):
                evacuate(f"ple{j}", PL[:, j, :], T=S)
            norm("n_pleg", KD, lambda k: X[:, k, 0:S], lambda k: H[:, k, 0:S], S, 1.0 / D)
            next_phase()
            norm("n_ple", KD, lambda k: PL[:, k, :], lambda k: PLSQ[:, k, :], S, 1.0 / D)
            for j in range(8):
                name = f"pleg{j}"
                if j >= 4:
                    act.wait_ge(gate_used, j - 3)
                evacuate(name, SG[:, j % 4, 0:S], ACT.Sigmoid, T=S)
            next_phase()

            for l in range(2):
                L, b = f"B{l}", lens(l)
                T = b["T"]
                norm(f"{L}n1", KD, lambda k: X[:, k, :], lambda k: H[:, k, :], 512, 1.0 / D)
                for j in range(4):
                    evacuate(f"{L}k{j}", b["NK"][:, j, :])
                for j in range(4):
                    evacuate(f"{L}v{j}", b["NV"][:, j, :])
                evacuate(L + "ckv0", b["CKV"][:, 0, :])
                evacuate(L + "kr0", b["KR"], M=MLA_ROPE)
                for j in range(4):
                    evacuate(f"{L}q{j}", b["NQ"][:, j, :], T=T)
                for j in range(2):
                    evacuate(f"{L}cq{j}", b["CQ"][:, j, :], T=T)
                for j in range(4):
                    evacuate(f"{L}u{j}", b["U"][:, j, :], ACT.Gelu, T=T)
                for j in range(T // P):
                    evacuate(f"{L}gv{j}", b["GV"][:, j, :], ACT.Gelu)
                next_phase()
                nq = 4 * T // 512
                q = b["NQ"].rearrange("p j n -> p (j n)")
                head_norms([f"{L}hn{j}" for j in range(4 + nq)],
                           lambda i: q[:, i * 512:i * 512 + 512] if i < nq else b["NK"][:, i - nq, :])
                act.wait_ge(gv_stats, l + 1)
                mv = SM[:, 32:32 + 2 * (T // P)].rearrange("p (t s) -> p t s", s=2)[:, :, 1]
                rs = SM[:, 48:48 + T // P]
                step(act.activation(rs, mv, ACT.Ln, bias=EPS_COL))
                act.activation(rs, rs, ACT.Exp, scale=-0.5).then_inc(gv_rstd, 1)
                next_phase()
                norm(L + "n_cq", 2, lambda k: b["CQ"][:, k, :], lambda k: SQ[:, k, 0:T], T, 1.0 / 256)
                next_phase()
                norm(L + "n_ckv", 1, lambda k: b["CKV"][:, 0, :], lambda k: SQ[:, 0, :], 512, 1.0 / P)
                next_phase()
                attention(na_units(l))
                next_phase()
                ln_exp()

                def square(i):
                    Ti = T if i < MLA_H else 512
                    act.activation(SQ[0:MLA_QK, i % 2, 0:Ti], bank(f"{L}raw{i}")[0:MLA_QK, 0:Ti], ACT.Square
                                   ).then_inc(ml_sq, 1)
                square(0)
                for i in range(2 * MLA_H):
                    if i + 1 < 2 * MLA_H:
                        square(i + 1)
                    Ti = T if i < MLA_H else 512
                    if i >= 2:
                        act.wait_ge(ml_done, c["ml"] + i - 1)
                    inverse_root(f"{L}ss{i}", R[0:MLA_QK, i % 2, 0:Ti], 1.0 / MLA_QK, Ti, MLA_QK
                                 ).then_inc(ml_rstd, 1)
                c["ml"] += 2 * MLA_H
                for j in range(4):
                    evacuate(f"{L}mv{j}", b["MV"][:, j, :])
                next_phase()
                attention(mla_units(l))
                next_phase()
                merge(L, 3, T)
                next_phase()
                norm(f"{L}n2", KD, lambda k: X[:, k, 0:T], lambda k: H[:, k, 0:T], T, 1.0 / D)
                for j in range(32):
                    evacuate(f"{L}up{j}", b["HID"][:, j, :], ACT.Relu, T=T)
                next_phase()

        @block.vector
        def _(dve):
            ph = [0]
            c = dict(step=0, rstd=0, scaled=0, hn=0, ml=0, unit=0, merged=0, normed=0)

            def next_phase():
                ph[0] += 1
                dve.drain().then_inc(phase["dve"], 1)
                for e in ("pe", "act"):
                    dve.wait_ge(phase[e], ph[0])

            def step(ins):
                c["step"] += 1
                ins.then_inc(dve_step, 1)
                dve.wait_ge(dve_step, c["step"])

            def bank(name):
                dve.wait_ge(tile_ready, plan.tile_at[name] + 1)
                return bank_of(name)

            def own(name):
                dve.wait_ge(freed["dve"], plan.freed[name][1])

            def wait_rstd(n=1):
                c["rstd"] += n
                dve.wait_ge(rstd, c["rstd"])

            def norm(n, src, dst, T, gain):
                wait_rstd()
                for k in range(n):
                    dve.scalar_tensor_tensor(out=dst(k), in0=src(k), scalar=gain(k), in1=R[:, 0, 0:T],
                                             op0=ALU.mult, op1=ALU.mult).then_inc(normed, 1)
                c["normed"] += n

            def norm_modulated(T, src_norm, l, shift_tile):
                wait_rstd()
                parts = [(s, k) for k in range(KD) for s in range(T // S)]
                for s, k in parts:
                    at = slice(s * S, s * S + S)
                    dve.scalar_tensor_tensor(out=H[:, k, at], in0=X[:, k, at], scalar=MA[:, src_norm, s, k:k + 1],
                                             in1=R[:, 0, at], op0=ALU.mult, op1=ALU.mult).then_inc(scaled, 1)
                for s, k in parts:
                    at = slice(s * S, s * S + S)
                    c["scaled"] += 1
                    dve.wait_ge(scaled, c["scaled"])
                    dve.tensor_scalar(H[:, k, at], H[:, k, at], MOD[:, l, shift_tile + k, s:s + 1], None, ALU.add
                                      ).then_inc(normed, 1)

            def head_norms(n, chunk, gain):
                for i in range(n):
                    dve.wait_ge(hn_rstd, c["hn"] + 1)
                    dve.scalar_tensor_tensor(out=chunk(i), in0=chunk(i), scalar=gain(i), in1=R[:, c["hn"] % 2, :],
                                             op0=ALU.mult, op1=ALU.mult).then_inc(hn_done, 1)
                    c["hn"] += 1

            def attention(units):
                u0 = c["unit"]
                c["unit"] += len(units)

                def maxima(u):
                    g, x = u0 + u, units[u]
                    nk, s = x["nk"], att_bank("S", u0 + u)
                    m, nm = MX[:, g % N_P:g % N_P + 1], NM[:, g % N_P:g % N_P + 1]
                    dve.wait_ge(scores_ready, g + 1)
                    if x["bias"] is None:
                        step(dve.tensor_reduce(m, s[:, 0:nk], AX.X, ALU.max))
                        dve.tensor_scalar(nm, m, -x["scale"], None, ALU.mult).then_inc(negmax, 1)
                        return
                    pr = PROB[:, g % N_P, :]
                    if g >= N_P:
                        dve.wait_ge(pt_ready, g - N_P + 1)
                    nb = x["bias"].shape[-1]
                    last = dve.scalar_tensor_tensor(out=pr[:, 0:nb], in0=s[:, 0:nb], scalar=x["scale"],
                                                    in1=x["bias"], op0=ALU.mult, op1=ALU.add)
                    if nb < nk:
                        step(last)
                        last = dve.tensor_scalar(pr[:, nb:nk], s[:, nb:nk], x["scale"], None, ALU.mult)
                    if x["sink"] is not None:
                        step(last)
                        last = dve.tensor_copy(pr[:, nk:nk + 1], x["sink"])
                        nk += 1
                    step(last)
                    step(dve.tensor_reduce(m, pr[:, 0:nk], AX.X, ALU.max))
                    dve.tensor_scalar(nm, m, -1.0, None, ALU.mult).then_inc(negmax, 1)

                def normalise(u):
                    g, x = u0 + u, units[u]
                    r = RIN[:, g % N_P:g % N_P + 1]
                    dve.wait_ge(exp_done, g + 1)
                    step(dve.reciprocal(r, SUM[:, g % N_P:g % N_P + 1]))
                    dve.tensor_scalar(PROB[:, g % N_P, 0:x["nk"]], PROB[:, g % N_P, 0:x["nk"]], r, None, ALU.mult
                                      ).then_inc(probs, 1)

                def store(u):
                    g, x = u0 + u, units[u]
                    dve.wait_ge(o_ready, g + 1)
                    dve.tensor_copy(x["out"], att_bank("O", g)[x["lo"]:x["lo"] + 64, 0:P]).then_inc(o_stored, 1)
                maxima(0)
                maxima(1)
                for u in range(len(units)):
                    normalise(u)
                    if u + 2 < len(units):
                        maxima(u + 2)
                    if u:
                        store(u - 1)
                store(len(units) - 1)

            def merge(L, n, Y, T):
                for b in range(n):
                    for hf in range(2):
                        for j in range(4):
                            name = f"{L}o{b}{hf}{j}"
                            gate = f"{L}gate{b}{hf}{j}"
                            dve.wait_ge(freed["act"], plan.freed[gate][1])
                            ps, y = bank(name)[:, 0:T], Y[:, hf * 4 + j, 0:T]
                            dst = y if b == 0 else TMP[:, j % 2, 0:T]
                            dve.tensor_tensor(dst, SG[:, j, 0:T], ps, ALU.mult).then_inc(freed["dve"], 1)
                            own(name)
                            if b:
                                ins = dve.tensor_tensor(y, y, TMP[:, j % 2, 0:T], ALU.add)
                                if b == n - 1:
                                    c["merged"] += 1
                                    ins.then_inc(merged, 1)
                                    dve.wait_ge(merged, c["merged"])
                                else:
                                    step(ins)

            def route(j):
                r = TMP[:, 1, j * S:j * S + S]
                at = VEC_AT["priority"][0]
                pri8, pri4 = VEC[:, at:at + 8], VEC[:, at + 4:at + 8]
                name = f"router{j}"
                dve.tensor_copy(r[:, 0:36], bank(name)[:, 0:36]).then_inc(freed["dve"], 1)
                own(name)
                col = {n: r[:, i:i + 1] for n, i in dict(gmax=49, gw=50, best=51, m1=104, m2=105, dist=106,
                                                         ratio=107, s=108, w1=110, w2=111).items()}

                def first_of_max(out, v, m, pri, tmp):
                    step(dve.tensor_reduce(m, v, AX.X, ALU.max))
                    step(dve.scalar_tensor_tensor(out=tmp, in0=v, scalar=m, in1=pri, op0=ALU.is_equal, op1=ALU.mult))
                    step(dve.tensor_reduce(col["best"], tmp, AX.X, ALU.max))
                    step(dve.tensor_scalar(out, tmp, col["best"], None, ALU.is_equal))
                first_of_max(r[:, 52:56], r[:, 0:4], col["gmax"], pri4, r[:, 56:60])
                dve.tensor_scalar(r[:, 40:44], r[:, 0:4], col["gmax"], None, ALU.subtract).then_inc(router_group, 1)
                e8 = r[:, 64:72]
                step(dve.tensor_scalar(e8, r[:, 4:12], r[:, 52:53], None, ALU.mult))
                for g in range(1, N_GROUPS):
                    step(dve.scalar_tensor_tensor(out=e8, in0=r[:, 4 + 8 * g:12 + 8 * g], scalar=r[:, 52 + g:53 + g],
                                                  in1=e8, op0=ALU.mult, op1=ALU.add))
                oh1, oh2 = r[:, 80:88], r[:, 88:96]
                first_of_max(oh1, e8, col["m1"], pri8, r[:, 72:80])
                step(dve.scalar_tensor_tensor(out=r[:, 96:104], in0=oh1, scalar=NEG, in1=e8, op0=ALU.mult, op1=ALU.add))
                first_of_max(oh2, r[:, 96:104], col["m2"], pri8, r[:, 72:80])
                dve.tensor_tensor(col["dist"], col["m2"], col["m1"], ALU.subtract).then_inc(router_top, 1)
                dve.wait_ge(router_exp, 2 * j + 2)
                step(dve.reciprocal(col["gw"], r[:, 48:49]))
                step(dve.tensor_scalar(col["s"], col["ratio"], 1.0, None, ALU.add))
                step(dve.reciprocal(col["s"], col["s"]))
                step(dve.tensor_tensor(col["w1"], col["s"], col["gw"], ALU.mult))
                step(dve.tensor_tensor(col["w2"], col["w1"], col["ratio"], ALU.mult))
                c8 = r[:, 112:120]
                step(dve.tensor_scalar(c8, oh1, col["w1"], None, ALU.mult))
                step(dve.scalar_tensor_tensor(out=c8, in0=oh2, scalar=col["w2"], in1=c8, op0=ALU.mult, op1=ALU.add))
                for g in range(N_GROUPS):
                    ins = dve.tensor_scalar(SM[:, 64 + 32 * j + 8 * g:72 + 32 * j + 8 * g], c8, r[:, 52 + g:53 + g],
                                            None, ALU.mult)
                ins.then_inc(combined, 1)

            dve.wait_ge(loaded_in, 16 * 9)
            for l in range(2):
                for b in range(12):
                    at = VEC_AT[f"bmod_{l}"][0] + 4 * b
                    for s in range(2):
                        ins = dve.tensor_tensor(MOD[:, l, 4 * b:4 * b + 4, s],
                                                bank(f"mod{l}{b}")[:, 0:8].rearrange("p (j s) -> p j s", s=2)[:, :, s],
                                                VEC[:, at:at + 4], ALU.add)
                        if s == 0:
                            step(ins)
                        else:
                            ins.then_inc(freed["dve"], 1)

            norm(KD, lambda k: X[:, k, 0:S], lambda k: H[:, k, 0:S], S, lambda k: vec("mix_g", k))
            next_phase()
            for hd in range(RET_H):
                name = f"ret_s{hd}"
                ps = bank(name)
                if hd >= 2:
                    dve.wait_ge(tile_ready, plan.tile_at[f"ret_y{hd - 2}"] + 1)
                dve.tensor_tensor(RSM[:, hd % 2, :], BRET[:, hd, :], ps[:, 0:384], ALU.mult).then_inc(masked, 1)
                dve.wait_ge(masked, hd + 1)
                dve.nop().then_inc(freed["dve"], 1)
            yr = YR.rearrange("p h n -> p (h n)")
            for j in range(2):
                name = f"ret_mean{j}"
                at = slice(j * 512, j * 512 + 512)
                dve.scalar_tensor_tensor(out=yr[:, at], in0=bank(name), scalar=-1.0 / RET_D, in1=yr[:, at],
                                         op0=ALU.mult, op1=ALU.add).then_inc(freed["dve"], 1)
                own(name)
                dve.nop().then_inc(centred, 1)
            wait_rstd(2)
            for hd in range(RET_H):
                r = R[:, hd // 2, (hd % 2) * S:(hd % 2) * S + S]
                step(dve.scalar_tensor_tensor(out=YR[:, hd, :], in0=YR[:, hd, :], scalar=vec("ret_g", hd), in1=r,
                                              op0=ALU.mult, op1=ALU.mult))
                step(dve.scalar_tensor_tensor(out=YR[:, hd, :], in0=YR[:, hd, :], scalar=vec("ret_b", hd),
                                              in1=RG[:, hd, :], op0=ALU.add, op1=ALU.mult))
            next_phase()
            qk = QK.rearrange("p j n -> p (j n)")
            head_norms(3, lambda i: qk[:, i * 512:i * 512 + 512], lambda i: vec("qn_g" if i < 2 else "kn_g"))
            next_phase()
            attention(swa_units())
            next_phase()
            YA = BR[:, 0:KD * S].rearrange("p (k n) -> p k n", k=KD)
            merge("A", 2, YA, S)
            for j in range(KD):
                name = f"Aout{j}"
                dve.tensor_tensor(X[:, j, 0:S], X[:, j, 0:S], bank(name)[:, 0:S], ALU.add).then_inc(freed["dve"], 1)
            next_phase()
            norm(KD, lambda k: X[:, k, 0:S], lambda k: H[:, k, 0:S], S, lambda k: vec("ffn_g", k))
            for j in range(ST):
                route(j)
            dve.memset(TMP[:, 0, :], 0.0).then_inc(moe_mul, 1)
            next_phase()

            def moe_dve(e, j):
                up, sg, hid = PS[:, 2 * j + 1, :], SGM[:, j, :], HID[:, j, :].rearrange("p (f n) -> p f n", f=FT)
                dve.tensor_tensor(sg, sg, up, ALU.mult).then_inc(moe_mul, 1)
                return sg.rearrange("p (f n) -> p f n", f=FT), hid

            def weigh(e, sg, hid):
                row = A[:, bass.ds(e * S, S)]
                for f in range(FT):
                    ins = dve.tensor_tensor(hid[:, f, :], sg[:, f, :], row, ALU.mult)
                    if f == 0:
                        ins.then_inc(dve_step, 1)
                    else:
                        ins.then_inc(moe_hid, 1)
            dve.wait_ge(comb_in, 64)
            for j in range(2):
                dve.wait_ge(moe_silu, j + 1)
                sg, hid = moe_dve(j, j)
                dve.wait_ge(moe_mul, j + 2)
                weigh(j, sg, hid)
            with dve.Fori(1, N_EXP // 2) as i:
                for j in range(2):
                    dve.wait_ge(moe_silu, 2 * i + (j + 1))
                    sg, hid = moe_dve(2 * i + j, j)
                    dve.wait_ge(moe_mul, 2 * i + (j + 2))
                    dve.wait_ge(moe_down, 2 * i + (j - 1))
                    weigh(2 * i + j, sg, hid)
            c["step"] += N_EXP
            dve.wait_ge(dve_step, c["step"])
            dve.wait_ge(moe_down, N_EXP)
            for d in range(KD):
                y = PS[:, 4 + d // 2, (d % 2) * S:(d % 2) * S + S]
                dve.tensor_tensor(X[:, d, 0:S], X[:, d, 0:S], y, ALU.add).then_inc(y_done, 1)
            dve.wait_ge(y_done, KD)
            next_phase()
            norm(KD, lambda k: X[:, k, 0:S], lambda k: H[:, k, 0:S], S, lambda k: vec("pleg_g", k))
            next_phase()
            norm(KD, lambda k: PL[:, k, :], lambda k: PL[:, k, :], S, lambda k: vec("ple_g", k))
            dve.wait_ge(normed, c["normed"])
            for j in range(KD):
                dve.wait_ge(freed["act"], plan.freed[f"pleg{j}"][1])
                dve.tensor_tensor(TMP[:, j % 2, 0:S], SG[:, j % 4, 0:S], PL[:, j, :], ALU.mult).then_inc(gate_used, 1)
                dve.wait_ge(gate_used, j + 1)
                step(dve.tensor_tensor(X[:, j, 0:S], X[:, j, 0:S], TMP[:, j % 2, 0:S], ALU.add))

            def gains(l):
                for n, (g, tile) in enumerate(((f"g1_{l}", 8), (f"g2_{l}", 32))):
                    at = VEC_AT[g][0]
                    for s in range(2):
                        step(dve.scalar_tensor_tensor(out=MA[:, n, s, :], in0=MOD[:, l, tile:tile + KD, s], scalar=1.0,
                                                      in1=VEC[:, at:at + KD], op0=ALU.add, op1=ALU.mult))
            gains(0)
            next_phase()

            for l in range(2):
                L, b = f"B{l}", lens(l)
                T = b["T"]

                def residual(name, j, tile):
                    for s in range(T // S):
                        at = slice(s * S, s * S + S)
                        ins = dve.scalar_tensor_tensor(out=X[:, j, at], in0=bank(name)[:, at],
                                                       scalar=MOD[:, l, tile + j, s:s + 1], in1=X[:, j, at],
                                                       op0=ALU.mult, op1=ALU.add)
                        if s == T // S - 1:
                            ins.then_inc(freed["dve"], 1)
                        else:
                            step(ins)
                norm_modulated(512, 0, l, 0)
                next_phase()
                nq = 4 * T // 512
                q = b["NQ"].rearrange("p j n -> p (j n)")
                head_norms(4 + nq, lambda i: q[:, i * 512:i * 512 + 512] if i < nq else b["NK"][:, i - nq, :],
                           lambda i: vec(f"naq_{l}" if i < nq else f"nak_{l}"))
                mv = SM[:, 32:32 + 2 * (T // P)].rearrange("p (t s) -> p t s", s=2)
                for q_ in range(T // P):
                    step(dve.bn_stats(SM[:, 192:198], b["GV"][:, q_, :]))
                    ins = dve.bn_aggr(mv[:, q_, :], SM[:, 192:198])
                    if q_ < T // P - 1:
                        step(ins)
                    else:
                        ins.then_inc(gv_stats, 1)
                dve.wait_ge(gv_rstd, l + 1)
                if l:
                    dve.wait_ge(lc_loaded, 16)
                for q_ in range(T // P):
                    v = b["GV"][:, q_, :]
                    step(dve.tensor_scalar(v, v, mv[:, q_, 0:1], SM[:, 48 + q_:49 + q_], ALU.subtract, ALU.mult))
                    step(dve.tensor_tensor(v, v, LC[:, LC_G:LC_G + 512], ALU.mult))
                    step(dve.tensor_tensor(v, v, LC[:, LC_B:LC_B + 512], ALU.add))
                next_phase()
                norm(2, lambda k: b["CQ"][:, k, :], lambda k: b["CQ"][:, k, :], T, lambda k: vec(f"cq_{l}", k))
                next_phase()
                norm(1, lambda k: b["CKV"][:, 0, :], lambda k: b["CKV"][:, 0, :], 512, lambda k: vec(f"ckv_{l}"))
                next_phase()
                for q_ in range(T // P):
                    u = b["U"][:, :, q_ * P:q_ * P + P]
                    ps = bank(f"{L}mix{q_}").rearrange("p (g n) -> p g n", g=GM_G)
                    dve.tensor_tensor(u, u, ps, ALU.mult).then_inc(freed["dve"], 1)
                dve.wait_ge(bias_loaded, 16 * (l + 1))
                attention(na_units(l))
                next_phase()

                def head(i):
                    return b["MQ"][0:MLA_QK, i, :] if i < MLA_H else b["MK"][0:MLA_QK, i - MLA_H, :]

                def scale(i):
                    Ti = T if i < MLA_H else 512
                    name = f"{L}raw{i}"
                    dve.wait_ge(ml_sq, c["ml"] + i + 1)
                    dve.tensor_scalar(head(i)[:, 0:Ti], bank(name)[0:MLA_QK, 0:Ti],
                                      vec(f"mq_{l}" if i < MLA_H else f"mk_{l}")[0:MLA_QK], None, ALU.mult
                                      ).then_inc(freed["dve"], 1)

                def rotate(i):
                    Ti = T if i < MLA_H else 512
                    name = f"{L}rx{i}"
                    own(f"{L}raw{i}")
                    tmp, x = TMP[0:MLA_QK, i % 2, 0:S], head(i)
                    dve.tensor_tensor(tmp, SIN, bank(name)[0:MLA_QK, 0:S], ALU.mult).then_inc(freed["dve"], 1)
                    own(name)
                    step(dve.tensor_tensor(x[:, 0:S], x[:, 0:S], COS, ALU.mult))
                    step(dve.tensor_tensor(x[:, 0:S], x[:, 0:S], tmp, ALU.add))
                    dve.wait_ge(ml_rstd, c["ml"] + i + 1)
                    dve.tensor_tensor(x[:, 0:Ti], x[:, 0:Ti], R[0:MLA_QK, i % 2, 0:Ti], ALU.mult).then_inc(ml_done, 1)
                scale(0)
                for i in range(2 * MLA_H):
                    if i + 1 < 2 * MLA_H:
                        scale(i + 1)
                    rotate(i)
                c["ml"] += 2 * MLA_H
                next_phase()
                attention(mla_units(l))
                next_phase()
                merge(L, 3, b["Y"], T)
                for j in range(KD):
                    residual(f"{L}out{j}", j, 16)
                next_phase()
                norm_modulated(T, 1, l, 24)
                for j in range(32):
                    dve.wait_ge(freed["act"], plan.freed[f"{L}up{j}"][1])
                    dve.tensor_tensor(b["HID"][:, j, :], b["HID"][:, j, :], b["HID"][:, j, :], ALU.mult
                                      ).then_inc(hid_ready, 1)
                for j in range(KD):
                    residual(f"{L}down{j}", j, 40)
                if l == 0:
                    gains(1)
                next_phase()


def rows(a, n):
    return np.broadcast_to(np.asarray(a).reshape(1, -1), (n, np.asarray(a).size))


def constants():
    f = np.float32
    j = np.arange(P)
    cst = np.zeros((P, 3, P), f)
    cst[:, 0] = np.eye(P)
    cst[:, 1] = 1.0
    cst[:, 2] = (j[:, None] // 64 == j[None, :] // 64)
    lg = np.log1p(-np.exp2(-5.0 - np.arange(RET_H)))
    diff = np.arange(S)[None, :] - j[:, None]
    ret = np.where(diff[:, None, :] >= 0, np.exp(np.maximum(diff, 0)[:, None, :] * lg[None, :, None]), 0.0)
    ret = ret * RET_D ** -0.5
    ret = np.concatenate([ret, ret[:, :, 0:P]], axis=2).reshape(P, -1)
    rel = j[:, None] + P - np.arange(2 * P)[None, :]
    slopes = np.exp2(-8.0 * np.arange(1, SWA_H + 1) / SWA_H)
    swa = np.where(((rel >= 0) & (rel < P))[:, None, :], -slopes[None, :, None] * rel[:, None, :], NEG)
    mask1 = np.concatenate([ret, swa.reshape(P, -1)], axis=1).astype(f)
    tok = np.arange(S)
    freqs = (f(10000.0) ** (-np.arange(8, dtype=f) / f(8))).astype(f)
    rope = np.zeros((P, 2 * S + 2 * MLA_QK), f)
    rope[:, 0:S] = 1.0
    for axis, place in enumerate((tok // GRID_W, tok % GRID_W)):
        ang = place.astype(f)[None, :] * freqs[:, None]
        for half in range(2):
            r = MLA_NOPE + 16 * axis + 8 * half
            rope[r:r + 8, 0:S] = np.cos(ang)
            rope[r:r + 8, S:2 * S] = np.sin(ang)
        a, b = MLA_NOPE + 16 * axis + np.arange(8), MLA_NOPE + 16 * axis + 8 + np.arange(8)
        rope[b, 2 * S + a] = -1.0
        rope[a, 2 * S + b] = 1.0
    rope[np.arange(MLA_ROPE), 2 * S + MLA_QK + MLA_NOPE + np.arange(MLA_ROPE)] = 1.0
    return cst, mask1, rope


def window_bias(rpb):
    q, k = np.arange(S)[:, None], np.arange(S)[None, :]
    dr = k // GRID_W - q // GRID_W + 7
    cq, ck = q % GRID_W, k % GRID_W
    dc = np.clip(ck - cq, -(WIN_W - 1), WIN_W - 1) + WIN_W - 1
    c0 = np.clip(cq - WIN_W // 2, 0, GRID_W - WIN_W)
    inside = (ck >= c0) & (ck < c0 + WIN_W)
    out = np.where(inside[None], rpb[:, dr, dc], np.float32(NEG))
    return out.reshape(NA_H, ST, P, S).transpose(2, 1, 0, 3).reshape(P, -1)


def layout(i):
    f = np.float32
    i = {k: np.asarray(v) for k, v in i.items()}
    cst, mask1, rope = constants()

    def cols(a):
        return a.reshape(-1, P).T

    def twice(a):
        return np.concatenate([a, a]).reshape(P, 1)

    def padded(a):
        return np.concatenate([a, np.zeros(P - a.size, f)]).reshape(P, 1)
    cc = np.stack([cols(i["c_2"][0]), cols(i["c_ctx_2"])], axis=2).reshape(P, -1)
    vec = [np.full((P, 1), EPS, f), cols(i["mix_norm_g"][0]), cols(i["ffn_norm_g"][0]), cols(i["ple_gate_norm_g"][0]),
           cols(i["ple_norm_g"][0]), cols(i["ret_gn_g"][0]), cols(i["ret_gn_b"][0]), twice(i["q_norm_g"][0]),
           twice(i["k_norm_g"][0]), rows(i["attn_sinks"][0], P), cc, rows(np.arange(8, 0, -1).astype(f), P)]
    for l in range(2):
        vec += [cols(i["g_norm1_2"][l]), cols(i["g_norm2_2"][l]), twice(i["na_q_gain_2"][l]),
                twice(i["na_k_gain_2"][l]), cols(i["mla_cq_gain_2"][l]), cols(i["mla_ckv_gain_2"][l]),
                padded(i["mla_q_gain_2"][l]), padded(i["mla_k_gain_2"][l]), cols(i["b_mod_2"][l])]
    ukv = i["mla_w_ukv_2"].reshape(2, P, MLA_H, MLA_NOPE + MLA_V)
    nope = np.concatenate([ukv[..., :MLA_NOPE], np.zeros((2, P, MLA_H, MLA_ROPE), f)], axis=3)
    ukv = np.concatenate([nope.reshape(2, P, -1), ukv[..., MLA_NOPE:].reshape(2, P, -1)], axis=2)
    lc = np.stack([np.concatenate([rows(i["gm_ln_g_2"][l], P), rows(i["gm_ln_b_2"][l], P),
                                   i["gm_w_s_2"][l].transpose(2, 0, 1).reshape(P, -1),
                                   rows(i["gm_b_s_2"][l], P)], axis=1) for l in range(2)])
    return dict(
        xT=i["x"][0].T, ctxT=i["ctx_2"][0].T, pT=i["p"][0, 0].T, vec=np.concatenate(vec, axis=1), cst=cst,
        rope=rope, mask1=mask1, lc=lc, na_bias=np.stack([window_bias(i["na_rpb_2"][l]) for l in range(2)]),
        w_in=i["w_in"][0], w_ret_o=i["w_ret_o"][0], w_swa_o=i["w_swa_o"][0], w_out=i["w_out"][0],
        w_r=np.concatenate([i["w_router_group"][0], i["w_router_expert"][0]], axis=1),
        b_r=np.concatenate([i["b_router_group"][0], i["b_router_expert"][0]])[None],
        w_gate=i["w_exp_gate"][0], w_up=i["w_exp_up"][0], w_down=i["w_exp_down"][0], w_ple=i["w_ple"][0],
        w_ple_gate=i["w_ple_gate"][0], w_mod=i["w_mod_2"], w_in_2=i["w_in_2"], na_w_o=i["na_w_o_2"],
        gm_w_o=i["gm_w_o_2"], w_uq=i["mla_w_uq_2"], w_ukv=ukv, mla_w_o=i["mla_w_o_2"], w_out_2=i["w_out_2"],
        ffn_w1=i["ffn_w1_2"], ffn_w2=i["ffn_w2_2"])


def build(nc, arrays):
    t = {name: nc.dram_tensor(f"in_{name}", a.shape, F32, kind="ExternalInput").ap() for name, a in arrays.items()}
    t["comb_rows"] = nc.dram_tensor("comb_rows", (N_EXP, S), F32, kind="Internal").ap()
    program(nc, t, nc.dram_tensor("out", (D, S), F32, kind="ExternalOutput").ap())


def kernel(**inputs):
    import concourse.bacc as _bacc
    from concourse.bass_utils import run_bass_kernel_spmd as _run

    nc = _bacc.Bacc("TRN2", target_bir_lowering=False, num_devices=1)
    arrays = {k: np.ascontiguousarray(v) for k, v in layout(inputs).items()}
    build(nc, arrays)
    r = _run(nc, [{f"in_{k}": v for k, v in arrays.items()}], core_ids=[0])
    return np.ascontiguousarray(r.results[0]["out"].T)[None]
```

```python
from contextlib import ExitStack

import numpy as np

import concourse.bass as bass
from concourse import mybir

F32 = mybir.dt.float32
F32R = mybir.dt.float32r
ALU = mybir.AluOpType
ACT = mybir.ActivationFunctionType
AX = mybir.AxisListType

P = 128
D = 1024
KD = D // P
S = 256
ST = S // P
EPS = 1e-6
NEG = -1e30

RET_H, RET_D = 4, 128
SWA_H, SWA_D, SWA_KV = 8, 64, 2
N_GROUPS, PER_GROUP, FF = 4, 8, 256
N_EXP = N_GROUPS * PER_GROUP
FT = FF // P
NA_H, NA_D = 8, 64
GRID_W, WIN_W = 64, 16
GM_G = 4
MLA_H, MLA_QK, MLA_NOPE, MLA_ROPE, MLA_V = 8, 96, 64, 32, 64
FFN = 4 * D

C1 = dict(rq=0, rk=512, rv=1024, rg=1536, sq=2048, sk=2560, sv=2688, gates=2816)
C2 = dict(k=0, v=512, ckv=1024, kr=1152, q=1184, u=1696, gv=2208, cq=2720, gates=2976)

VEC_COLS = [("eps", 1), ("mix_g", 8), ("ffn_g", 8), ("pleg_g", 8), ("ple_g", 8), ("ret_g", 4), ("ret_b", 4),
            ("qn_g", 1), ("kn_g", 1), ("sinks", 8), ("priority", 8)]
for _l in (0, 1):
    VEC_COLS += [(f"{n}{_l}", w) for n, w in
                 (("g1_", 8), ("g2_", 8), ("naq_", 1), ("nak_", 1), ("cq_", 2), ("ckv_", 1), ("mq_", 1),
                  ("mk_", 1))]
VEC_COLS += [("bmod", 96)]
VEC_AT, _n = {}, 0
for _name, _w in VEC_COLS:
    VEC_AT[_name] = (_n, _w)
    _n += _w
N_VEC = _n

LC_G, LC_B, LC_WS, LC_BS, N_LC = 0, 512, 1024, 1536, 2048

RING = 3
SLOT = 2048
CHUNK = 1024
BUFS = 3
GROUPS_F = 4
GT = FFN // P // GROUPS_F
PH_END = 12
ACC = 4
N_P = 5
AHEAD = 4
MOD_COLS = 2 * 6 * D // N_EXP
MT = MOD_COLS // P


class Plan:

    def __init__(self):
        self.blocks = []
        self.block_at = {}
        self.block_end = {}
        self.landing = {}
        self.tiles = []
        self.tile_at = {}
        self.freed = {}
        self.read = {"act": 0, "dve": 0}
        self.chunks = []
        self.chunk_end = []
        self.chunk_tile = []
        self.parts = 0
        self.floor = 0
        self.floors = []
        self.att = []
        self.att_at = {}
        self.units = 0

    def block(self, name, source, kt, cols):
        self.block_at[name] = len(self.blocks)
        self.blocks.append((name, source, kt, cols))

    def tile(self, name, reader, block=None):
        self.tile_at[name] = len(self.tiles)
        self.tiles.append((name, reader))
        self.read[reader] += 1
        self.freed[name] = (reader, self.read[reader])
        if block is not None:
            self.block_end[block] = ("tile", len(self.tiles))

    def chunk(self, block, k0, kn, c0, cn, end, tile):
        self.chunks.append((self.block_at[block], k0, kn, c0, cn))
        self.chunk_end.append(end)
        self.chunk_tile.append(tile)
        self.floors.append(self.floor)
        self.block_end[block] = ("chunk", len(self.chunks))

    def fm(self, names, source, reader, behind=None):
        for i in range(0, len(names), 2):
            n = min(2, len(names) - i)
            name = "w_" + names[i]
            self.block(name, source[:, i * P:(i + n) * P], KD, n * P)
            for j in range(n):
                self.tile(names[i + j], reader)
                self.chunk(name, 0, KD, j * P, P, ("tile", len(self.tiles)), len(self.tiles))
                for extra in (behind or {}).get(i + j, []):
                    self.tile(*extra)

    def tm(self, name, source, n_tiles, cols, reader):
        t0 = len(self.tiles)
        if cols < 512:
            self.block("w_" + name, source, KD, cols)
            for j in range(n_tiles):
                self.tile(f"{name}{j}", reader)
            self.chunk("w_" + name, 0, KD, 0, cols, ("tile", len(self.tiles)), len(self.tiles))
            return
        for hf in range(2):
            self.block(f"w_{name}{hf}", source[hf * 512:hf * 512 + 512, :], 4, cols)
        for j in range(n_tiles):
            self.tile(f"{name}{j}", reader)
        for q in range(4):
            if q < 3:
                self.parts += 1
            end = ("part", self.parts) if q < 3 else ("tile", len(self.tiles))
            self.chunk(f"w_{name}{q // 2}", 2 * (q % 2), 2, 0, cols, end, t0 if q < 3 else len(self.tiles))

    def fence(self):
        self.floor = len(self.tiles)

    def finish(self):
        need, last, land = [], 0, []
        for b, (name, *_) in enumerate(self.blocks):
            last = max(last, self.landing.get(name, 0))
            if b >= RING:
                kind, count = self.block_end[self.blocks[b - RING][0]]
                if kind == "tile":
                    last = max(last, count)
            land.append(last)
        last = 0
        for i, (b, *_) in enumerate(self.chunks):
            last = max(last, land[b], self.floors[i])
            if i >= BUFS:
                last = max(last, self.chunk_tile[i - BUFS])
            need.append(last)
        self.split_by = [sum(n <= t for n in need) for t in range(len(self.tiles))]

    def attention(self, n):
        u0 = self.units
        self.units += n

        def put(kind, u):
            self.att_at[(kind, u0 + u)] = len(self.att)
            self.att.append((kind, u0 + u))
        for u in range(AHEAD):
            put("S", u)
        for u in range(n):
            put("T", u)
            if u + AHEAD < n:
                put("S", u + AHEAD)
            put("O", u)
        self.fence()


def four(name, j0=0):
    return [f"{name}{j0 + j}" for j in range(4)]


def merge_blocks(plan, L, w_in, gates, w_o, T):
    for b, w in enumerate(w_o):
        for hf in range(2):
            c = gates + b * D + hf * 512
            plan.fm(four(f"{L}gate{b}{hf}"), w_in[:, c:c + 512], "act")
            plan.block(f"{L}o{b}{hf}", w[:, hf * 512:hf * 512 + 512], 4, 512)
            for j in range(4):
                plan.tile(f"{L}o{b}{hf}{j}", "dve", f"{L}o{b}{hf}")


def out_blocks(plan, L, w):
    for q in range(4):
        plan.block(f"{L}out_w{q}", w[:, q * 256:q * 256 + 256], 8, 256)
        for j in range(2):
            plan.tile(f"{L}out{q * 2 + j}", "dve", f"{L}out_w{q}")


def norms_behind(l, name):
    first, n = {"q": (0, 4), "cq": (4, 2), "u": (6, 4 if l == 0 else 2)}[name]
    return {j: [(f"B{l}norm{first + j}", "act")] for j in range(n)}


def make_plan(t):
    plan = Plan()
    plan.tile("n_mix", "act")
    w = t["w_in"]
    at = lambda name, n=512: w[:, C1[name]:C1[name] + n]
    plan.fm(four("sq"), at("sq"), "act")
    plan.fm(["sk0", "sk1"], t["w_sk"], "act")
    plan.tm("sv", at("sv", P), ST, P, "act")
    plan.fm(four("rq"), at("rq"), "act", {j: [(f"hn1_{j}", "act")] for j in range(3)})
    plan.fm(four("rk"), at("rk"), "act")
    plan.tm("rv", at("rv"), ST, 512, "act")
    plan.fm(four("rg"), at("rg"), "act")
    for h in range(RET_H):
        plan.tile(f"ret_s{h}", "dve")
        plan.tile(f"ret_y{h}", "act")
    for j in range(2):
        plan.tile(f"ret_mean{j}", "dve")
    for j in range(2):
        plan.tile(f"ret_var{j}", "act")
    plan.attention(ST * SWA_H)
    merge_blocks(plan, "A", w, C1["gates"], [t["w_ret_o"], t["w_swa_o"]], S)
    out_blocks(plan, "A", t["w_out"])
    plan.tile("n_ffn", "act")
    plan.tm("router", t["w_r"], ST, 36, "dve")
    plan.n_before_moe = len(plan.blocks)
    plan.fence()
    plan.block("ple", t["w_ple"], 2, 1024)
    for j in range(8):
        plan.tile(f"ple{j}", "act", "ple")
    plan.tile("n_pleg", "act")
    plan.tile("n_ple", "act")
    plan.fm([f"pleg{j}" for j in range(8)], t["w_ple_gate"], "act")
    for l in range(2):
        L = f"B{l}"
        tok = 2 * S if l == 0 else S
        w = t["w_in_2"][l]
        at = lambda name, n=512: w[:, C2[name]:C2[name] + n]
        plan.tile(f"{L}n1", "act")
        plan.fm(four(L + "k"), at("k"), "act")
        plan.fm(four(L + "q"), at("q"), "act", norms_behind(l, "q"))
        plan.fm([L + "cq0", L + "cq1"], at("cq", 256), "act", norms_behind(l, "cq"))
        plan.fm([L + "ckv0", L + "kr0"], at("ckv", 256), "act")
        plan.tm(L + "gv", at("gv"), tok // P, 512, "act")
        plan.tm(L + "v", at("v"), 4, 512, "act")
        plan.fm(four(L + "u"), at("u"), "act", norms_behind(l, "u"))
        for j in range(tok // P):
            plan.tile(f"{L}mix{j}", "dve")
        plan.attention(tok // P * NA_H)
        plan.block(L + "uq", t["w_uq"][l], 2, MLA_H * MLA_QK)
        plan.block(L + "ukv", t["w_ukv"][l], 1, MLA_H * (MLA_QK + MLA_V))
        n = 2 * MLA_H

        def raw(i):
            plan.tile(f"{L}raw{i}", "dve", L + ("uq" if i < MLA_H else "ukv"))
        raw(0)
        for i in range(n):
            if i + 1 < n:
                raw(i + 1)
            plan.tile(f"{L}ss{i}", "act")
            plan.tile(f"{L}rx{i}", "dve")
        for j in range(4):
            plan.tile(f"{L}mv{j}", "act", L + "ukv")
        plan.attention(tok // P * MLA_H)
        merge_blocks(plan, L, w, C2["gates"], [t["na_w_o"][l], t["gm_w_o"][l], t["mla_w_o"][l]], tok)
        out_blocks(plan, L, t["w_out_2"][l])
        plan.tile(f"{L}n2", "act")

        def up(g):
            plan.fm([f"{L}up{g * GT + j}" for j in range(GT)], t["ffn_w1"][l][:, g * D:g * D + D], "act")

        def down(g):
            plan.fm([f"{L}down{g}_{j}" for j in range(KD)], t["ffn_w2"][l][g * D:g * D + D, :], "dve")
        for g in range(GROUPS_F):
            up(g)
            if g:
                down(g - 1)
        down(GROUPS_F - 1)
    plan.landing["w_B0up8"] = plan.tile_at["B0out7"] + 1
    plan.finish()
    return plan


def program(nc, t, out):
    plan = make_plan(t)
    ctx = ExitStack()
    with ctx:
        def sb(name, shape, dtype=F32):
            return ctx.enter_context(nc.sbuf_tensor(name, shape, dtype))

        def views(name, shape, name_r, shape_r):
            place = ExitStack()
            whole = place.enter_context(nc.sbuf_tensor(name, shape, F32))
            place.close()
            return whole, sb(name_r, shape_r, F32R)

        def sem(name):
            return ctx.enter_context(nc.semaphore(name))

        X = sb("X", [P, KD, 2 * S])
        HH = sb("HH", [P, KD, 2 * S], F32R)
        HL = sb("HL", [P, KD, 2 * S], F32R)
        ring = sb("ring", [P, RING, SLOT])
        A, AR = views("A", [P, 16384], "AR", [P, 16384])
        BR = sb("BR", [P, 4096])
        SQ = sb("SQ", [P, 2, 512])
        SCR, CR = views("SCR", [P, N_P * 520 + 1024], "CR", [P, BUFS, 2, CHUNK])
        R = sb("R", [P, 2, 512])
        TMP = sb("TMP", [P, 2, 512])
        CST = sb("CST", [P, 3, P])
        VEC = sb("VEC", [P, N_VEC])
        LC = sb("LC", [P, N_LC])
        ROPE = sb("ROPE", [P, 2 * S + 2 * MLA_QK])
        MOD = sb("MOD", [P, 2, 48, 2])
        MA = sb("MA", [P, 2, 2, KD])
        SM = sb("SM", [P, 320])
        PS = ctx.enter_context(nc.psum_tensor("PS", [P, 8, 512], F32))
        comb_rows = t["comb_rows"]

        IDENT, ONES, BLK = CST[:, 0, :], CST[:, 1, :], CST[:, 2, :]
        COS, SIN = ROPE[0:MLA_QK, 0:S], ROPE[0:MLA_QK, S:2 * S]
        ROT = ROPE[0:MLA_QK, 2 * S:2 * S + MLA_QK]
        KR_AT = ROPE[0:MLA_ROPE, 2 * S + MLA_QK:2 * S + 2 * MLA_QK]
        PROB = SCR[:, 0:N_P * 520].rearrange("p (b n) -> p b n", b=N_P)
        PT = SCR[:, N_P * 520:N_P * 520 + 1024].rearrange("p (b n) -> p b n", b=2)
        EPS_COL = VEC[:, 0:1]
        NM, SUM, RIN, MX, ESINK = (SM[:, 8 * i:8 * i + N_P] for i in range(5))

        def vec(name, k=0):
            at = VEC_AT[name][0] + k
            return VEC[:, at:at + 1]

        def cut(at, n, w):
            return A[:, at:at + n * w].rearrange("p (n w) -> p n w", n=n)

        SG = cut(10240, 4, 512)
        NS = cut(4096, KD, 512)
        RQ, RK, RV, RG = cut(0, 4, S), cut(1024, 4, S), cut(2048, ST, 512), cut(3072, 4, S)
        QK, SV, YR, YS = cut(4096, 6, S), cut(5632, ST, P), cut(5888, 4, S), cut(6912, 4, S)
        RSM = cut(7936, 2, 384)
        PIN = cut(15872, 2, S)
        BRET = BR[:, 0:1536].rearrange("p (h n) -> p h n", h=RET_H)
        BSWA = BR[:, 1536:3584].rearrange("p (h n) -> p h n", h=SWA_H)
        BCOMB = cut(0, N_EXP, S)
        SGM = cut(8192, 2, 512)
        HIDH = AR[:, 9216:10240].rearrange("p (n w) -> p n w", n=2)
        HIDL = AR[:, 10496:11520].rearrange("p (n w) -> p n w", n=2)
        CT = A[0:N_EXP, 10240:10496]
        MW = BR[:, 0:MT * D].rearrange("p (m n) -> p m n", m=MT)
        SC = cut(13568, 2, D)
        MR = SM[:, 224:224 + 2 * MT]
        JUNK = SQ[:, :, :].rearrange("p a n -> p (a n)")
        MOD_FLAT = MOD[:, :, :, :].rearrange("p l j s -> p (l j s)")
        BMOD = VEC[:, VEC_AT["bmod"][0]:VEC_AT["bmod"][0] + 96]
        PL = cut(0, KD, S)
        PLSQ = cut(2048, KD, S)

        loaded_in = sem("loaded_in")
        landed = [sem(f"weights_landed{i}") for i in range(RING)]
        loaded_x = sem("loaded_x")
        part_used, hi_done, lo_done = sem("part_used"), sem("chunk_high_done"), sem("chunk_split")
        norm_hi = sem("norm_high_done")
        tile_ready = sem("tile_ready")
        freed = {"act": sem("tile_freed_by_act"), "dve": sem("tile_freed_by_dve")}
        phase = {e: sem(f"phase_{e}") for e in ("pe", "act", "dve")}
        act_step, dve_step = sem("act_step"), sem("dve_step")
        squares, rstd, scaled, normed = sem("squares"), sem("rstd"), sem("scaled"), sem("normed")
        silu_c, modded, evac = sem("silu_c"), sem("modded"), sem("evacuated")
        masked = sem("ret_masked")
        centred, varsq = sem("ret_centred"), sem("ret_varsq")
        hn_sq, hn_rstd = sem("head_squares"), sem("head_rstd")
        scores_ready, negmax, exp_done, probs = (sem("scores_ready"), sem("negmax_ready"), sem("exp_done"),
                                                 sem("probs_ready"))
        pt_ready, pt_copied, o_ready, o_stored = (sem("pt_ready"), sem("pt_copied"), sem("o_ready"),
                                                  sem("o_stored"))
        gate_ready, merged = sem("gate_ready"), sem("merged")
        combined, comb_out, comb_t = sem("combined"), sem("comb_out"), sem("comb_t")
        comb_in = [sem(f"comb_in{i}") for i in range(2)]
        comb_turned = sem("comb_turned")
        moe_landed = {w: sem(f"moe_{w}_landed") for w in ("gate", "up", "down")}
        moe_hi, moe_lo, moe_used = sem("moe_chunk_high"), sem("moe_chunk_split"), sem("moe_chunk_used")
        moe_silu, moe_mul, moe_weighed, moe_hid_hi, moe_hid = (sem("moe_silu"), sem("moe_mul"), sem("moe_weighed"),
                                                               sem("moe_hid_high"), sem("moe_hid"))
        ml_sq, ml_rstd = sem("mla_squares"), sem("mla_rstd")
        gv_stats, gv_rstd, lc_loaded, bias_loaded = (sem("gv_stats"), sem("gv_rstd"), sem("lc_loaded"),
                                                     sem("bias_loaded"))
        hid_sq = sem("hid_square")
        hid_hi, hid_ready, x_ready, gv_ready = sem("hid_high"), sem("hid_ready"), sem("x_ready"), sem("gv_ready")
        mw_landed = [sem(f"w_mod_landed{m}") for m in range(MT)]
        mod_step, mod_acc = sem("mod_step"), sem("mod_acc")
        stored = sem("stored")
        hn_done, gate_used, ml_done = sem("head_norm_done"), sem("gate_used"), sem("mla_done")
        router_group, router_exp, router_top = sem("router_group"), sem("router_exp"), sem("router_top")

        def lens(l):
            T = 2 * S if l == 0 else S
            return dict(
                T=T, NQ=cut(0, 4, T), NK=cut(2048, 4, 512), NV=cut(4096, 4, 512), YN=cut(6144, 4, T),
                U=cut(8192, 4, T), GV=cut(10240, T // P, 512), CQ=cut(12288, 2, T), CKV=cut(13312, 1, 512),
                KR=A[0:MLA_ROPE, 13824:14336], YM=cut(14336, 4, T), MQ=cut(0, MLA_H, T), MV=cut(4096, 4, 512),
                MK=BR[:, :].rearrange("p (h n) -> p h n", h=MLA_H),
                BIAS=BR[:, :].rearrange("p (t h n) -> p t h n", t=ST, h=NA_H),
                Y=BR[:, 0:KD * T].rearrange("p (k n) -> p k n", k=KD))

        def hidden(g, j, T):
            return [AR[:, at:at + T] for at in (((g % 2) * 2 + p) * GT * 512 + j * 512 for p in range(2))]

        def chunk_views(i):
            b, k0, kn, c0, cn = plan.chunks[i]
            _, _, kt, cols = plan.blocks[b]
            src = ring[:, b % RING, 0:kt * cols].rearrange("p (k n) -> p k n", k=kt)[:, k0:k0 + kn, c0:c0 + cn]
            return [src] + [CR[:, i % BUFS, p, 0:kn * cn].rearrange("p (k n) -> p k n", k=kn) for p in range(2)]

        MOE_CHUNKS = 6 * N_EXP

        def moe_chunk(q, c):
            w, half = ("gate", "up", "down")[c // 2], c % 2
            raw = ring[:, c // 2, :]
            if w == "down":
                return raw[:, half * CHUNK:half * CHUNK + CHUNK], CR[:, q % BUFS, 0, :], CR[:, q % BUFS, 1, :]
            raw = raw.rearrange("p (k n) -> p k n", k=KD)[:, :, half * P:half * P + P]
            return [raw] + [CR[:, q % BUFS, p, :].rearrange("p (k n) -> p k n", k=KD) for p in range(2)]

        class Expert:

            def __init__(self, base, i=None):
                self.base, self.i, self.j = base, i, base % 2

            def at(self, m, k=0):
                return m * self.base + k if self.i is None else (2 * m) * self.i + (m * self.base + k)

        def experts(eng, body):
            for e in (1, 2):
                body(Expert(e))
            with eng.Fori(1, N_EXP // 2 - 1) as i:
                for base in (1, 2):
                    body(Expert(base, i))
            body(Expert(N_EXP - 1))

        def wait_after(eng, semaphore, count):
            if not isinstance(count, int) or count > 0:
                eng.wait_ge(semaphore, count)

        def bank_of(name):
            return PS[:, plan.tile_at[name] % ACC, :]

        def att_bank(kind, u):
            return PS[:, plan.att_at[(kind, u)] % 8, :]

        def swa_units():
            units = []
            for qt in range(ST):
                for h in range(SWA_H):
                    lo, kv = 64 * (h % 2), h // (SWA_H // SWA_KV)
                    keys = [(QK[lo:lo + 64, 4 + kv, (qt - 1) * P if qt else 0:(qt + 1) * P])]
                    nk = P if qt == 0 else 2 * P
                    units.append(dict(
                        q=QK[lo:lo + 64, h // 2, qt * P:qt * P + P], k=keys[0], nk=nk,
                        bias=BSWA[:, h, 2 * P - nk:2 * P], sink=vec("sinks", h),
                        v=[SV[:, j, kv * 64:kv * 64 + 64] for j in range(qt + 1 - nk // P, qt + 1)],
                        out=YS[lo:lo + 64, h // 2, qt * P:qt * P + P], lo=lo))
            return units

        def dense_units(q, k, v, y, T, bias):
            units = []
            for qt in range(T // P):
                k0, nk = (0, 512) if qt < ST else (S, S)
                for h in range(8):
                    lo = 64 * (h % 2)
                    units.append(dict(
                        q=q(h, qt * P), k=k(h, k0, nk), nk=nk,
                        bias=bias[:, qt, h, :] if bias is not None and qt < ST else None, sink=None,
                        v=[v[:, j, h * 64:h * 64 + 64] for j in range(k0 // P, (k0 + nk) // P)],
                        out=y[lo:lo + 64, h // 2, qt * P:qt * P + P], lo=lo))
            return units

        def na_units(l):
            b = lens(l)
            return dense_units(
                lambda h, c: b["NQ"][64 * (h % 2):64 * (h % 2) + 64, h // 2, c:c + P],
                lambda h, c, n: b["NK"][64 * (h % 2):64 * (h % 2) + 64, h // 2, c:c + n],
                b["NV"], b["YN"], b["T"], b["BIAS"])

        def mla_units(l):
            b = lens(l)
            return dense_units(lambda h, c: b["MQ"][0:MLA_QK, h, c:c + P],
                               lambda h, c, n: b["MK"][0:MLA_QK, h, c:c + n],
                               b["MV"], b["YM"], b["T"], None)

        r0 = plan.tile_at["router0"]
        GU_BANKS = [((r0 + 2) % ACC, (r0 + 3) % ACC), (r0 % ACC, (r0 + 1) % ACC)]

        def norm_items(l):
            b = lens(l)
            T = b["T"]
            nq = 4 * T // 512
            q = b["NQ"].rearrange("p j n -> p (j n)")
            items = [([b["NK"][:, i, :]], [SQ[:, i % 2, :]], BLK, 1.0 / NA_D, [f"nak_{l}"]) for i in range(4)]
            items += [([q[:, i * 512:i * 512 + 512]], [SQ[:, i % 2, :]], BLK, 1.0 / NA_D, [f"naq_{l}"])
                      for i in range(nq)]
            items.append(([b["CQ"][:, k, :] for k in range(2)], [TMP[:, k, 0:T] for k in range(2)], ONES,
                          1.0 / 256, [(f"cq_{l}", 0), (f"cq_{l}", 1)]))
            items.append(([b["CKV"][:, 0, :]], [SQ[:, (4 + nq + 1) % 2, :]], ONES, 1.0 / P, [f"ckv_{l}"]))
            return [(x, sq, lhs, inv, [g if isinstance(g, tuple) else (g, 0) for g in gains])
                    for x, sq, lhs, inv, gains in items]

        block = ctx.enter_context(nc.Block())

        @block.sync
        def _(sp):
            for dst, src in ((X[:, :, 0:S], t["xT"].rearrange("(k p) n -> p k n", p=P)),
                             (VEC[:, :], t["vec"]), (CST[:, :, :], t["cst"])):
                sp.dma_start(dst, src).then_inc(loaded_x, 16)

            def after(n):
                for e in ("pe", "act", "dve"):
                    sp.wait_ge(phase[e], n)

            def wait_used(n):
                kind, count = plan.block_end[plan.blocks[n][0]]
                sp.wait_ge(tile_ready if kind == "tile" else lo_done, count)

            def load_block(n, fresh=False):
                name, src, kt, cols = plan.blocks[n]
                if n >= RING and not fresh:
                    wait_used(n - RING)
                sp.dma_start(ring[:, n % RING, 0:kt * cols].rearrange("p (k n) -> p k n", k=kt),
                             src.rearrange("(k p) n -> p k n", p=P)).then_inc(landed[n % RING], 16)

            for n in range(RING):
                load_block(n)
            for dst, src in ((BR[:, 0:3584], t["mask1"]), (SM[0:1, 256:256 + 36], t["b_r"]),
                             (A[:, 13568:13568 + 2 * D], t["c_rows"]),
                             (X[:, :, S:2 * S], t["ctxT"].rearrange("(k p) n -> p k n", p=P)),
                             (ROPE[:, :], t["rope"]), (PIN, t["pT"].rearrange("(k p) n -> p k n", p=P)),
                             (LC[:, :], t["lc"][0])):
                sp.dma_start(dst, src).then_inc(loaded_in, 16)
            for n in range(RING, plan.n_before_moe):
                load_block(n)

            def load_expert(which, e):
                w, slot, kt = {"gate": (t["w_gate"], 0, KD), "up": (t["w_up"], 1, KD),
                               "down": (t["w_down"], 2, FT)}[which]
                sp.dma_start(ring[:, slot, :].rearrange("p (k n) -> p k n", k=kt),
                             w[bass.ds(e, 1)].rearrange("e (k p) n -> p (e k) n", p=P)
                             ).then_inc(moe_landed[which], 16)

            def load_mod(m, e):
                sp.dma_start(MW[:, m, :], t["w_mod"][bass.ds(e, 1)][:, m * P:m * P + P, :].rearrange("e p k -> p (e k)")
                             ).then_inc(mw_landed[m], 16)
            for n in range(plan.n_before_moe - RING, plan.n_before_moe):
                wait_used(n)
            for which in ("gate", "up", "down"):
                load_expert(which, 0)
            for m in range(MT):
                load_mod(m, 0)
            sp.wait_ge(comb_t, 1)
            sp.dma_start(comb_rows, CT).then_inc(comb_out, 16)
            sp.wait_ge(moe_lo, 2)
            load_expert("gate", 1)
            sp.wait_ge(comb_out, 16)
            flat = comb_rows.rearrange("e n -> (e n)")
            for q, (lo, hi) in enumerate(((0, 2 * S), (2 * S, N_EXP * S))):
                sp.dma_start(A[:, lo:hi], flat[lo:hi].rearrange("(o n) -> o n", o=1).broadcast_to([P, hi - lo])
                             ).then_inc(comb_in[q], 16)
            sp.wait_ge(moe_lo, 4)
            load_expert("up", 1)

            def refill(x, last=False):
                for m, which in enumerate(("gate", "up", "down")):
                    sp.wait_ge(moe_lo, x.at(6, 2 * m))
                    if which == "down":
                        load_expert(which, x.at(1))
                    elif not last:
                        load_expert(which, x.at(1, 1))
                    sp.wait_ge(mod_step, x.at(6, 2 * m - 4))
                    load_mod(m, x.at(1))
            for e in (1, 2):
                refill(Expert(e))
            with sp.Fori(1, N_EXP // 2 - 1) as i:
                for base in (1, 2):
                    refill(Expert(base, i))
            refill(Expert(N_EXP - 1), last=True)
            sp.wait_ge(moe_lo, MOE_CHUNKS)
            n0 = plan.n_before_moe
            for n in range(n0, plan.block_at["w_B0gv0"]):
                load_block(n, fresh=n < n0 + RING)
            sp.wait_ge(mod_acc, N_EXP)
            sp.dma_start(BR[:, :], t["na_bias"][0]).then_inc(bias_loaded, 16)
            for n in range(plan.block_at["w_B0gv0"], plan.block_at["w_B0up8"]):
                load_block(n)
            sp.wait_ge(tile_ready, plan.tile_at["B0out7"] + 1)
            sp.dma_start(LC[:, :], t["lc"][1]).then_inc(lc_loaded, 16)
            sp.dma_start(BR[:, :], t["na_bias"][1]).then_inc(bias_loaded, 16)
            for n in range(plan.block_at["w_B0up8"], len(plan.blocks)):
                load_block(n)
            after(PH_END)
            sp.dma_start(out.rearrange("(k p) n -> p k n", p=P), X[:, :, 0:S]).then_inc(stored, 16)
            sp.wait_ge(stored, 16)

        @block.tensor
        def _(pe):
            ph = [0]
            c = dict(squares=0, normed=0, evac=0, hn=0, ml=0, unit=0, merged=0, chunk=0)
            waits = []

            def next_phase():
                ph[0] += 1
                pe.drain().then_inc(phase["pe"], 1)
                for e in ("act", "dve"):
                    pe.wait_ge(phase[e], ph[0])

            def open_tile(name):
                n = plan.tile_at[name]
                if n >= ACC:
                    reader, count = plan.freed[plan.tiles[n - ACC][0]]
                    pe.wait_ge(freed[reader], count)
                return PS[:, n % ACC, :]

            def weights(name):
                n = plan.block_at[name]
                _, _, kt, cols = plan.blocks[n]
                pe.wait_ge(landed[n % RING], 16 * (n // RING + 1))
                return ring[:, n % RING, 0:kt * cols].rearrange("p (k n) -> p k n", k=kt)

            def fm(W, tile, c0, M, rhs, kt, T):
                bank = open_tile(tile)
                for k in range(kt):
                    mm = pe.matmul(bank[0:M, 0:T], W[:, k, c0:c0 + M], rhs(k), start=(k == 0), stop=(k == kt - 1))
                mm.then_inc(tile_ready, 1)

            def split_weights():
                i = c["chunk"]
                c["chunk"] += 1
                pe.wait_ge(lo_done, i + 1)
                return chunk_views(i)[1:]

            def product(bank, w, x, k, start, stop):
                (wh, wl), (xh, xl) = w, x
                if waits and k < len(waits):
                    pe.wait_ge(normed, waits[k])
                pe.matmul(bank, wh, xh, start=start, stop=False)
                pe.matmul(bank, wh, xl, start=False, stop=False)
                return pe.matmul(bank, wl, xh, start=False, stop=stop)

            def fm3(tile, T, x=None):
                bank = open_tile(tile)
                W = split_weights()
                for k in range(KD):
                    rhs = x(k) if x else (HH[:, k, 0:T], HL[:, k, 0:T])
                    mm = product(bank[:, 0:T], [w[:, k, :] for w in W], rhs, k, k == 0, k == KD - 1)
                waits.clear()
                mm.then_inc(tile_ready, 1)

            def tm3(name, n, cols):
                banks = [open_tile(f"{name}{j}") for j in range(n)]
                for q in range(4):
                    W = split_weights()
                    for j in range(n):
                        at = slice(j * P, j * P + P)
                        for kk in range(2):
                            k = 2 * q + kk
                            mm = product(banks[j][:, 0:cols], (HH[:, k, at], HL[:, k, at]),
                                         [w[:, kk, :] for w in W], k, k == 0, k == KD - 1)
                        if q == 3:
                            mm.then_inc(tile_ready, 1)
                    if q < 3:
                        mm.then_inc(part_used, 1)

            def tm3_small(name, n, cols, bias=None):
                W = split_weights()
                for j in range(n):
                    at = slice(j * P, j * P + P)
                    bank = open_tile(f"{name}{j}")
                    for k in range(KD):
                        mm = product(bank[:, 0:cols], (HH[:, k, at], HL[:, k, at]), [w[:, k, :] for w in W], k,
                                     k == 0, k == KD - 1 and bias is None)
                    waits.clear()
                    if bias is not None:
                        mm = pe.matmul(bank[:, 0:cols], ONES[0:1, :], bias, start=False, stop=True)
                    mm.then_inc(tile_ready, 1)

            def norm_sums(tile, n, sq, T, lhs=None):
                bank = open_tile(tile)
                for k in range(n):
                    c["squares"] += 1
                    pe.wait_ge(squares, c["squares"])
                    mm = pe.matmul(bank[:, 0:T], ONES, sq(k), start=(k == 0), stop=(k == n - 1))
                mm.then_inc(tile_ready, 1)

            def h_ready(streams):
                for k in range(KD):
                    c["normed"] += streams
                    waits.append(c["normed"])

            def ns(T):
                return lambda k: NS[:, k, 0:T]

            def head_sums(tiles):
                for name in tiles:
                    bank = open_tile(name)
                    pe.wait_ge(hn_sq, c["hn"] + 1)
                    pe.matmul(bank[:, :], BLK, SQ[:, c["hn"] % 2, :], start=True, stop=True).then_inc(tile_ready, 1)
                    c["hn"] += 1

            def attention(units):
                u0 = c["unit"]
                c["unit"] += len(units)

                def open_att(kind, u):
                    m = plan.att_at[(kind, u0 + u)]
                    if m >= 8:
                        kd, old = plan.att[m - 8]
                        pe.wait_ge({"S": exp_done, "T": pt_copied, "O": o_stored}[kd], old + 1)
                    return PS[:, m % 8, :]

                def scores(u):
                    bank, x = open_att("S", u), units[u]
                    bias = x["bias"]
                    mm = pe.matmul(bank[:, 0:x["nk"]], x["q"], x["k"], start=True, stop=bias is None)
                    if bias is not None:
                        mm = pe.matmul(bank[:, 0:bias.shape[-1]], IDENT, bias, start=False, stop=True)
                    mm.then_inc(scores_ready, 1)

                def turn(u):
                    bank, x = open_att("T", u), units[u]
                    pe.wait_ge(probs, u0 + u + 1)
                    n = x["nk"] // P
                    for j in range(n):
                        mm = pe.transpose(bank[:, j * P:j * P + P], PROB[:, (u0 + u) % N_P, j * P:j * P + P], IDENT)
                    mm.then_inc(pt_ready, 1)

                def values(u):
                    bank, x = open_att("O", u), units[u]
                    pe.wait_ge(pt_copied, u0 + u + 1)
                    n = x["nk"] // P
                    for j in range(n):
                        mm = pe.matmul(bank[x["lo"]:x["lo"] + 64, 0:P], x["v"][j],
                                       PT[:, (u0 + u) % 2, j * P:j * P + P], start=(j == 0), stop=(j == n - 1))
                    mm.then_inc(o_ready, 1)

                for u in range(AHEAD):
                    scores(u)
                for u in range(len(units)):
                    turn(u)
                    if u + AHEAD < len(units):
                        scores(u + AHEAD)
                    values(u)

            def merge(L, ys, T):
                for b, y in enumerate(ys):
                    for hf in range(2):
                        for j in range(4):
                            fm3(f"{L}gate{b}{hf}{j}", T)
                        W = weights(f"{L}o{b}{hf}")
                        for j in range(4):
                            fm(W, f"{L}o{b}{hf}{j}", j * P, P, lambda k: y[:, k, 0:T], 4, T)

            def project_out(L, Y, T):
                c["merged"] += KD
                pe.wait_ge(merged, c["merged"])
                for q in range(4):
                    W = weights(f"{L}out_w{q}")
                    for j in range(2):
                        fm(W, f"{L}out{q * 2 + j}", j * P, P, lambda k: Y[:, k, 0:T], KD, T)

            pe.wait_ge(loaded_x, 48)
            norm_sums("n_mix", KD, ns(S), S)
            h_ready(1)
            for j in range(4):
                fm3(f"sq{j}", S)
            for j in range(SWA_KV):
                fm3(f"sk{j}", S)
            tm3_small("sv", ST, P)
            for j in range(4):
                fm3(f"rq{j}", S)
                if j < 3:
                    head_sums([f"hn1_{j}"])
            for j in range(4):
                fm3(f"rk{j}", S)
            tm3("rv", ST, 512)
            for j in range(4):
                fm3(f"rg{j}", S)
            next_phase()
            pe.wait_ge(loaded_in, 16 * 7)
            for hd in range(RET_H):
                bank = open_tile(f"ret_s{hd}")
                pe.matmul(bank[:, 0:S], RK[:, hd, 0:P], RQ[:, hd, :], start=True, stop=True)
                pe.matmul(bank[:, S:S + P], RK[:, hd, P:S], RQ[:, hd, P:S], start=True, stop=True
                          ).then_inc(tile_ready, 1)
                bank = open_tile(f"ret_y{hd}")
                pe.wait_ge(masked, hd + 1)
                pe.matmul(bank[:, 0:S], RV[:, 0, hd * P:hd * P + P], RSM[:, hd % 2, 0:S], start=True, stop=False)
                pe.matmul(bank[:, P:S], RV[:, 1, hd * P:hd * P + P], RSM[:, hd % 2, S:S + P], start=False, stop=True
                          ).then_inc(tile_ready, 1)
            pe.wait_ge(evac, 1)
            yr = YR.rearrange("p h n -> p (h n)")
            for j in range(2):
                pe.matmul(open_tile(f"ret_mean{j}"), ONES, yr[:, j * 512:j * 512 + 512], start=True, stop=True
                          ).then_inc(tile_ready, 1)
            for j in range(2):
                bank = open_tile(f"ret_var{j}")
                pe.wait_ge(varsq, j + 1)
                pe.matmul(bank, ONES, SQ[:, j, :], start=True, stop=True).then_inc(tile_ready, 1)
            next_phase()
            attention(swa_units())
            next_phase()
            merge("A", [YR, YS], S)
            project_out("A", BR[:, 0:KD * S].rearrange("p (k n) -> p k n", k=KD), S)
            norm_sums("n_ffn", KD, ns(S), S)
            h_ready(1)
            tm3_small("router", ST, 36, SM[0:1, 256:256 + 36])
            Y = [PS[:, 4 + d // 2, (d % 2) * S:(d % 2) * S + S] for d in range(KD)]

            def gate_up(x, q0, q_mod):
                for q in range(4):
                    pe.wait_ge(moe_lo, q0 + q + 1 if isinstance(q0, int) else q0(q + 1))
                    W = moe_chunk(q_mod + q, q)[1:]
                    bank = PS[:, GU_BANKS[x.j][q // 2], (q % 2) * S:(q % 2) * S + S]
                    for k in range(KD):
                        mm = product(bank, [w[:, k, :] for w in W], (HH[:, k, 0:S], HL[:, k, 0:S]), k, k == 0,
                                     k == KD - 1)
                    mm.then_inc(moe_used, 1)

            def down(j, q0, q_mod):
                for f in range(FT):
                    pe.wait_ge(moe_lo, q0(f + 1))
                    W = moe_chunk(q_mod + f, 4 + f)[1:]
                    at = slice(f * S, f * S + S)
                    for d in range(KD):
                        for w, x in ((0, HIDH), (0, HIDL), (1, HIDH)):
                            mm = pe.matmul(Y[d], W[w][:, d * P:d * P + P], x[:, j, at], start=False, stop=False,
                                           skip_group_check=True)
                    mm.then_inc(moe_used, 1)

            gate_up(Expert(0), 0, 0)
            pe.wait_ge(combined, ST)
            for j in range(ST):
                mm = pe.transpose(PS[0:N_EXP, 4, j * P:j * P + P], SM[:, 64 + 32 * j:96 + 32 * j], IDENT)
            mm.then_inc(comb_turned, 1)
            pe.wait_ge(comb_t, 1)
            for b in range(4):
                pe.matmul(PS[:, 4 + b, :], TMP[:, 0, 0:P], TMP[:, 0, :], start=True, stop=False,
                          skip_group_check=True)

            def expert(x):
                wait_after(pe, moe_mul, x.at(1, -1))
                gate_up(x, lambda n: x.at(6, n - 2), 4)
                pe.wait_ge(moe_hid, x.at(1))
                down(1 - x.j, lambda n: x.at(6, n + 2), 2)
            experts(pe, expert)
            pe.wait_ge(moe_hid, N_EXP)
            down((N_EXP - 1) % 2, lambda n: MOE_CHUNKS - 2 + n, 1)

            W = weights("ple")
            for j in range(8):
                fm(W, f"ple{j}", j * P, P, lambda k: PIN[:, k, :], 2, S)
            norm_sums("n_pleg", KD, ns(S), S)
            h_ready(1)
            norm_sums("n_ple", KD, lambda k: PLSQ[:, k, :], S)
            c["normed"] += KD
            for j in range(KD):
                fm3(f"pleg{j}", S)

            for l in range(2):
                L, b = f"B{l}", lens(l)
                T = b["T"]
                norm_sums(f"{L}n1", KD, ns(512), 512)
                h_ready(2)
                items = norm_items(l)

                def project(name, T, n=4):
                    behind = norms_behind(l, name) if name in ("q", "cq", "u") else {}
                    for j in range(n):
                        fm3(f"{L}{name}{j}", T)
                        for norm_tile, _ in behind.get(j, []):
                            _, sq, lhs, _, _ = items[int(norm_tile[6:])]
                            bank = open_tile(norm_tile)
                            for k, x in enumerate(sq):
                                c["hn"] += 1
                                pe.wait_ge(hn_sq, c["hn"])
                                mm = pe.matmul(bank[:, 0:x.shape[-1]], lhs, x, start=(k == 0),
                                               stop=(k == len(sq) - 1))
                            mm.then_inc(tile_ready, 1)
                project("k", 512)
                project("q", T)
                project("cq", T, 2)
                project("ckv", 512, 1)
                project("kr", 512, 1)
                tm3(L + "gv", T // P, 512)
                tm3(L + "v", 4, 512)
                project("u", T)
                pe.wait_ge(gv_ready, l + 1)
                for q in range(T // P):
                    bank = open_tile(f"{L}mix{q}")
                    for g in range(GM_G):
                        pe.matmul(bank[:, g * P:g * P + P], b["GV"][:, q, g * P:g * P + P],
                                  LC[:, LC_WS + g * P:LC_WS + g * P + P], start=True, stop=False)
                        mm = pe.matmul(bank[:, g * P:g * P + P], ONES[0:1, :],
                                       LC[0:1, LC_BS + g * P:LC_BS + g * P + P], start=False, stop=True)
                    mm.then_inc(tile_ready, 1)
                next_phase()
                pe.wait_ge(bias_loaded, 16 * (l + 1))
                attention(na_units(l))
                next_phase()
                Wq, Wk = weights(L + "uq"), weights(L + "ukv")

                def raw(i):
                    bank, hd = open_tile(f"{L}raw{i}"), i % MLA_H
                    if i < MLA_H:
                        for k in range(2):
                            mm = pe.matmul(bank[0:MLA_QK, 0:T], Wq[:, k, hd * MLA_QK:hd * MLA_QK + MLA_QK],
                                           b["CQ"][:, k, 0:T], start=(k == 0), stop=(k == 1))
                    else:
                        pe.matmul(bank[0:MLA_QK, :], Wk[:, 0, hd * MLA_QK:hd * MLA_QK + MLA_QK], b["CKV"][:, 0, :],
                                  start=True, stop=False)
                        mm = pe.matmul(bank[0:MLA_QK, :], KR_AT, b["KR"], start=False, stop=True)
                    mm.then_inc(tile_ready, 1)
                raw(0)
                for i in range(2 * MLA_H):
                    if i + 1 < 2 * MLA_H:
                        raw(i + 1)
                    Ti = T if i < MLA_H else 512
                    bank = open_tile(f"{L}ss{i}")
                    pe.wait_ge(ml_sq, c["ml"] + i + 1)
                    pe.matmul(bank[0:MLA_QK, 0:Ti], ONES[0:MLA_QK, 0:MLA_QK], SQ[0:MLA_QK, i % 2, 0:Ti], start=True,
                              stop=True).then_inc(tile_ready, 1)
                    bank = open_tile(f"{L}rx{i}")
                    pe.wait_ge(freed["dve"], plan.freed[f"{L}raw{i}"][1])
                    src = b["MQ"][0:MLA_QK, i, 0:S] if i < MLA_H else b["MK"][0:MLA_QK, i - MLA_H, 0:S]
                    pe.matmul(bank[0:MLA_QK, 0:S], ROT, src, start=True, stop=True).then_inc(tile_ready, 1)
                c["ml"] += 2 * MLA_H
                for j in range(4):
                    bank = open_tile(f"{L}mv{j}")
                    pe.matmul(bank, b["CKV"][:, 0, j * P:j * P + P],
                              Wk[:, 0, MLA_H * MLA_QK:MLA_H * MLA_QK + 512], start=True, stop=True
                              ).then_inc(tile_ready, 1)
                next_phase()
                attention(mla_units(l))
                next_phase()
                merge(L, [b["YN"], b["U"], b["YM"]], T)
                project_out(L, b["Y"], T)
                norm_sums(f"{L}n2", KD, ns(T), T)
                h_ready(T // S)

                def up(g):
                    for j in range(GT):
                        fm3(f"{L}up{g * GT + j}", T)

                def down_group(g):
                    pe.wait_ge(hid_ready, FFN // P * l + GT * g + GT)
                    for j in range(KD):
                        fm3(f"{L}down{g}_{j}", T, lambda k: hidden(g, k, T))
                for g in range(GROUPS_F):
                    up(g)
                    if g:
                        down_group(g - 1)
                down_group(GROUPS_F - 1)
            next_phase()

        @block.scalar
        def _(act):
            ph = [0]
            c = dict(step=0, squares=0, rstd=0, hn=0, hnr=0, ml=0, unit=0, gate=0, x=0, chunk=0, scaled=0)

            def next_phase():
                ph[0] += 1
                act.drain().then_inc(phase["act"], 1)
                for e in ("pe", "dve"):
                    act.wait_ge(phase[e], ph[0])

            def step(ins):
                c["step"] += 1
                ins.then_inc(act_step, 1)
                act.wait_ge(act_step, c["step"])

            def split(name):
                while c["chunk"] < plan.split_by[plan.tile_at[name]]:
                    i = c["chunk"]
                    c["chunk"] += 1
                    b = plan.chunks[i][0]
                    act.wait_ge(landed[b % RING], 16 * (b // RING + 1))
                    if i >= BUFS:
                        kind, count = plan.chunk_end[i - BUFS]
                        act.wait_ge(tile_ready if kind == "tile" else part_used, count)
                    src, hi, _ = chunk_views(i)
                    act.activation(hi, src, ACT.Copy).then_inc(hi_done, 1)

            def bank(name):
                split(name)
                act.wait_ge(tile_ready, plan.tile_at[name] + 1)
                return bank_of(name)

            def inverse_root(name, r, inv, T, M=P):
                act.activation(r, bank(name)[0:M, 0:T], ACT.Ln, bias=VEC[0:M, 0:1], scale=inv
                               ).then_inc(freed["act"], 1)
                act.wait_ge(freed["act"], plan.freed[name][1])
                return act.activation(r, r, ACT.Exp, scale=-0.5)

            def ln_exp():
                act.preload_act_table_set("natural_log_exp_and_others")

            def norm(tile, n, src, sq, T, inv, x_tiles=None, r=0):
                ln_exp()
                for k in range(n):
                    if x_tiles:
                        split(x_tiles(k))
                        c["x"] += 1
                        act.wait_ge(x_ready, c["x"])
                    act.activation(sq(k), src(k), ACT.Square).then_inc(squares, 1)
                inverse_root(tile, R[:, r, 0:T], inv, T).then_inc(rstd, 1)

            def norm_high(T, shift=None):
                for k in range(KD):
                    for st in range(T // S):
                        at = slice(st * S, st * S + S)
                        c["scaled"] += 1
                        act.wait_ge(scaled, c["scaled"])
                        if shift is None:
                            act.activation(HH[:, k, at], NS[:, k, at], ACT.Copy).then_inc(norm_hi, 1)
                        else:
                            act.activation(HH[:, k, at], NS[:, k, at], ACT.Identity, bias=shift(st, k)
                                           ).then_inc(norm_hi, 1)

            def evacuate(name, dst, func=ACT.Copy, M=P, T=512):
                act.activation(dst, bank(name)[0:M, 0:T], func).then_inc(freed["act"], 1)

            def attention(units):
                u0 = c["unit"]
                c["unit"] += len(units)
                ln_exp()

                def expo(u):
                    g, x = u0 + u, units[u]
                    act.wait_ge(negmax, g + 1)
                    if g >= N_P:
                        act.wait_ge(pt_ready, g - N_P + 1)
                    nm = NM[:, g % N_P:g % N_P + 1]
                    if x["sink"] is not None:
                        act.activation(ESINK[:, g % N_P:g % N_P + 1], x["sink"], ACT.Exp, bias=nm)
                    act.activation(PROB[:, g % N_P, 0:x["nk"]], att_bank("S", g)[:, 0:x["nk"]], ACT.Exp, bias=nm,
                                   accum_out=SUM[:, g % N_P:g % N_P + 1]).then_inc(exp_done, 1)

                def copy_turned(u):
                    g, x = u0 + u, units[u]
                    act.wait_ge(pt_ready, g + 1)
                    if g >= 2:
                        act.wait_ge(o_ready, g - 1)
                    act.activation(PT[:, g % 2, 0:x["nk"]], att_bank("T", g)[:, 0:x["nk"]], ACT.Copy
                                   ).then_inc(pt_copied, 1)

                def store(u):
                    g, x = u0 + u, units[u]
                    act.wait_ge(o_ready, g + 1)
                    act.activation(x["out"], att_bank("O", g)[x["lo"]:x["lo"] + 64, 0:P], ACT.Copy
                                   ).then_inc(o_stored, 1)
                for u in range(AHEAD - 1):
                    expo(u)
                for u in range(len(units)):
                    copy_turned(u)
                    if u + AHEAD - 1 < len(units):
                        expo(u + AHEAD - 1)
                    if u:
                        store(u - 1)
                store(len(units) - 1)

            def merge(L, n, T):
                for b in range(n):
                    for hf in range(2):
                        for j in range(4):
                            split(f"{L}gate{b}{hf}{j}")
                            if b or hf:
                                prev = f"{L}o{b if hf else b - 1}{1 - hf}{j}"
                                act.wait_ge(freed["dve"], plan.freed[prev][1])
                            name = f"{L}gate{b}{hf}{j}"
                            evacuate(name, SG[:, j, 0:T], ACT.Sigmoid, T=T)

            act.wait_ge(loaded_x, 48)
            norm("n_mix", KD, lambda k: X[:, k, 0:S], lambda k: NS[:, k, 0:S], S, 1.0 / D)
            norm_high(S)
            for j in range(4):
                evacuate(f"sq{j}", QK[:, j, :], T=S)
            for j in range(SWA_KV):
                evacuate(f"sk{j}", QK[:, 4 + j, :], T=S)
            for j in range(ST):
                evacuate(f"sv{j}", SV[:, j, :], T=P)
            act.wait_ge(freed["act"], plan.freed[f"sk{SWA_KV - 1}"][1])
            qk = QK.rearrange("p j n -> p (j n)")
            for j in range(4):
                if j < 3:
                    act.activation(SQ[:, j % 2, :], qk[:, j * 512:j * 512 + 512], ACT.Square).then_inc(hn_sq, 1)
                evacuate(f"rq{j}", RQ[:, j, :], T=S)
                if j < 3:
                    if j == 2:
                        act.wait_ge(hn_done, 1)
                    inverse_root(f"hn1_{j}", R[:, 1 - j % 2, :], 1.0 / 64, 512).then_inc(hn_rstd, 1)
            c["hn"] = 3
            for j in range(4):
                evacuate(f"rk{j}", RK[:, j, :], T=S)
            for j in range(ST):
                evacuate(f"rv{j}", RV[:, j, :])
            for j in range(4):
                evacuate(f"rg{j}", RG[:, j, :], ACT.Silu, T=S)
            act.wait_ge(loaded_in, 16 * 7)
            act.activation(SC, SC, ACT.Silu).then_inc(silu_c, 1)
            next_phase()
            ln_exp()
            for hd in range(RET_H):
                act.activation(YR[:, hd, :], bank(f"ret_y{hd}")[:, 0:S], ACT.Copy).then_inc(freed["act"], 1)
            act.drain().then_inc(evac, 1)
            yr = YR.rearrange("p h n -> p (h n)")
            for j in range(2):
                act.wait_ge(centred, j + 1)
                act.activation(SQ[:, j, :], yr[:, j * 512:j * 512 + 512], ACT.Square).then_inc(varsq, 1)
            for j in range(2):
                inverse_root(f"ret_var{j}", R[:, j, :], 1.0 / RET_D, 512).then_inc(rstd, 1)
            next_phase()
            attention(swa_units())
            next_phase()
            merge("A", 2, S)
            norm("n_ffn", KD, lambda k: X[:, k, 0:S], lambda k: NS[:, k, 0:S], S, 1.0 / D, lambda k: f"Aout{k}")
            norm_high(S)

            def moe_high(which, count, c_, q_mod, free):
                act.wait_ge(moe_landed[which], count)
                if free is not None:
                    act.wait_ge(moe_used, free)
                src, hi, _ = moe_chunk(q_mod, c_)
                act.activation(hi, src, ACT.Copy).then_inc(moe_hi, 1)
            split("router1")
            act.wait_ge(tile_ready, plan.tile_at["router1"] + 1)
            for q in range(3):
                moe_high(("gate", "up")[q // 2], 16, q, q, None)
            for j in range(ST):
                r = TMP[:, 1, j * S:j * S + S]
                act.wait_ge(router_group, j + 1)
                act.activation(r[:, 44:48], r[:, 40:44], ACT.Exp, accum_out=r[:, 48:49]).then_inc(router_exp, 1)
                act.wait_ge(router_top, j + 1)
                act.activation(r[:, 107:108], r[:, 106:107], ACT.Exp).then_inc(router_exp, 1)
                if j == 0:
                    moe_high("up", 16, 3, 3, 1)
            act.wait_ge(comb_turned, 1)
            act.activation(CT, PS[0:N_EXP, 4, 0:S], ACT.Copy).then_inc(comb_t, 1)

            def hidden_silu(x, used):
                wait_after(act, moe_used, used)
                act.activation(SGM[:, x, :], PS[:, GU_BANKS[x][0], :], ACT.Silu).then_inc(moe_silu, 1)

            def hidden_high(x, count):
                act.wait_ge(moe_weighed, count)
                act.activation(HIDH[:, x, :], SGM[:, x, :], ACT.Copy).then_inc(moe_hid_hi, 1)

            def expert(x):
                j = 1 - x.j
                hidden_silu(j, x.at(6, -6))
                for q in range(2):
                    moe_high("gate", x.at(16, 16), q, 4 + q, x.at(6, q - 4))
                for q in range(2, 4):
                    moe_high("up", x.at(16, 16), q, 4 + q, x.at(6, q - 4))
                    if q == 2:
                        hidden_high(j, x.at(1))
                for q in range(4, 6):
                    moe_high("down", x.at(16), q, 4 + q, x.at(6, q - 4))
            experts(act, expert)
            j = (N_EXP - 1) % 2
            hidden_silu(j, 6 * N_EXP - 4)
            hidden_high(j, N_EXP)
            for q in range(4, 6):
                moe_high("down", 16 * N_EXP, q, MOE_CHUNKS - 6 + q, MOE_CHUNKS - 8 + q)
            act.wait_ge(moe_hid, N_EXP)
            act.wait_ge(moe_used, MOE_CHUNKS)
            for j in range(8):
                evacuate(f"ple{j}", PL[:, j, :], T=S)
            norm("n_pleg", KD, lambda k: X[:, k, 0:S], lambda k: NS[:, k, 0:S], S, 1.0 / D, lambda k: "ple7")
            norm_high(S)
            act.wait_ge(freed["act"], plan.freed["ple7"][1])
            norm("n_ple", KD, lambda k: PL[:, k, :], lambda k: PLSQ[:, k, :], S, 1.0 / D, r=1)
            for j in range(8):
                name = f"pleg{j}"
                split(name)
                if j >= 4:
                    act.wait_ge(gate_used, j - 3)
                evacuate(name, SG[:, j % 4, 0:S], ACT.Sigmoid, T=S)

            for l in range(2):
                L, b = f"B{l}", lens(l)
                T = b["T"]
                norm(f"{L}n1", KD, lambda k: X[:, k, :], lambda k: NS[:, k, :], 512, 1.0 / D,
                     lambda k: f"pleg{k}" if l == 0 else f"B0down{GROUPS_F - 1}_{k}")
                norm_high(512, lambda st, k: MOD[:, l, k, st:st + 1])
                items, h0 = norm_items(l), c["hn"]

                def square_items(i):
                    for x, sq in zip(items[i][0], items[i][1]):
                        act.activation(sq, x, ACT.Square).then_inc(hn_sq, 1)

                def project(name, dst, T, n=4, func=ACT.Copy):
                    behind = norms_behind(l, name) if name in ("q", "cq", "u") else {}
                    for j in range(n):
                        norms = [int(tile[6:]) for tile, _ in behind.get(j, [])]
                        for i in norms:
                            square_items(i)
                        evacuate(f"{L}{name}{j}", dst[:, j, :], func, T=T)
                        for i in norms:
                            T_i = items[i][1][0].shape[-1]
                            if i >= 2:
                                act.wait_ge(hn_done, h0 + i - 1)
                            ln_exp()
                            inverse_root(f"{L}norm{i}", R[:, 1 - i % 2, 0:T_i], items[i][3], T_i
                                         ).then_inc(hn_rstd, 1)
                project("k", b["NK"], 512)
                act.wait_ge(freed["act"], plan.freed[L + "k3"][1])
                project("q", b["NQ"], T)
                act.wait_ge(freed["act"], plan.freed[f"{L}norm3"][1])
                project("cq", b["CQ"], T, 2)
                evacuate(L + "ckv0", b["CKV"][:, 0, :])
                evacuate(L + "kr0", b["KR"], M=MLA_ROPE)
                for j in range(T // P):
                    evacuate(f"{L}gv{j}", b["GV"][:, j, :], ACT.Gelu)
                for j in range(4):
                    evacuate(f"{L}v{j}", b["NV"][:, j, :])
                ln_exp()
                act.wait_ge(gv_stats, l + 1)
                mv = SM[:, 40:40 + 2 * (T // P)].rearrange("p (t s) -> p t s", s=2)[:, :, 1]
                rs = SM[:, 56:56 + T // P]
                step(act.activation(rs, mv, ACT.Ln, bias=EPS_COL))
                act.activation(rs, rs, ACT.Exp, scale=-0.5).then_inc(gv_rstd, 1)
                act.wait_ge(freed["act"], plan.freed[L + "v3"][1])
                project("u", b["U"], T, func=ACT.Gelu)
                c["hn"] += len(items)
                next_phase()
                attention(na_units(l))
                next_phase()
                ln_exp()

                def square(i):
                    Ti = T if i < MLA_H else 512
                    act.activation(SQ[0:MLA_QK, i % 2, 0:Ti], bank(f"{L}raw{i}")[0:MLA_QK, 0:Ti], ACT.Square
                                   ).then_inc(ml_sq, 1)
                square(0)
                for i in range(2 * MLA_H):
                    if i + 1 < 2 * MLA_H:
                        square(i + 1)
                    Ti = T if i < MLA_H else 512
                    if i >= 2:
                        act.wait_ge(ml_done, c["ml"] + i - 1)
                    inverse_root(f"{L}ss{i}", R[0:MLA_QK, i % 2, 0:Ti], 1.0 / MLA_QK, Ti, MLA_QK
                                 ).then_inc(ml_rstd, 1)
                c["ml"] += 2 * MLA_H
                for j in range(4):
                    evacuate(f"{L}mv{j}", b["MV"][:, j, :])
                next_phase()
                attention(mla_units(l))
                next_phase()
                merge(L, 3, T)
                norm(f"{L}n2", KD, lambda k: X[:, k, 0:T], lambda k: NS[:, k, 0:T], T, 1.0 / D,
                     lambda k: f"{L}out{k}")
                norm_high(T, lambda st, k: MOD[:, l, 24 + k, st:st + 1])

                def up(g):
                    for j in range(GT):
                        name = f"{L}up{g * GT + j}"
                        split(name)
                        n = FFN // P * l + g * GT + j
                        if g * GT + j >= 2:
                            act.wait_ge(hid_ready, n - 1)
                        relu = TMP[:, j % 2, 0:T]
                        evacuate(name, relu, ACT.Relu, T=T)
                        act.wait_ge(freed["act"], plan.freed[name][1])
                        act.activation(hidden(g, j, T)[0], relu, ACT.Square).then_inc(hid_hi, 1)

                def down(g):
                    for j in range(KD):
                        split(f"{L}down{g}_{j}")
                for g in range(GROUPS_F):
                    up(g)
                    if g:
                        down(g - 1)
                if l:
                    down(GROUPS_F - 1)
            next_phase()

        @block.vector
        def _(dve):
            ph = [0]
            c = dict(step=0, rstd=0, scaled=0, hn=0, ml=0, unit=0, merged=0, normed=0, x=0, chunk=0, nh=0)

            def next_phase():
                ph[0] += 1
                dve.drain().then_inc(phase["dve"], 1)
                for e in ("pe", "act"):
                    dve.wait_ge(phase[e], ph[0])

            def step(ins):
                c["step"] += 1
                ins.then_inc(dve_step, 1)
                dve.wait_ge(dve_step, c["step"])

            def split(name):
                while c["chunk"] < plan.split_by[plan.tile_at[name]]:
                    c["chunk"] += 1
                    dve.wait_ge(hi_done, c["chunk"])
                    src, hi, lo = chunk_views(c["chunk"] - 1)
                    dve.tensor_tensor(lo, src, hi, ALU.subtract).then_inc(lo_done, 1)

            def bank(name):
                split(name)
                dve.wait_ge(tile_ready, plan.tile_at[name] + 1)
                return bank_of(name)

            def own(name):
                dve.wait_ge(freed["dve"], plan.freed[name][1])

            def wait_rstd(n=1):
                c["rstd"] += n
                dve.wait_ge(rstd, c["rstd"])

            def norm(n, src, dst, T, gain, r=0):
                wait_rstd()
                for k in range(n):
                    dve.scalar_tensor_tensor(out=dst(k), in0=src(k), scalar=gain(k), in1=R[:, r, 0:T],
                                             op0=ALU.mult, op1=ALU.mult).then_inc(normed, 1)
                c["normed"] += n

            def norm_split(T, gain, shift=None):
                wait_rstd()
                parts = [(st, k) for k in range(KD) for st in range(T // S)]

                def scale(st, k):
                    at = slice(st * S, st * S + S)
                    dve.scalar_tensor_tensor(out=NS[:, k, at], in0=X[:, k, at], scalar=gain(st, k), in1=R[:, 0, at],
                                             op0=ALU.mult, op1=ALU.mult).then_inc(scaled, 1)

                def rest(st, k):
                    at = slice(st * S, st * S + S)
                    c["nh"] += 1
                    dve.wait_ge(norm_hi, c["nh"])
                    if shift is None:
                        ins = dve.tensor_tensor(HL[:, k, at], NS[:, k, at], HH[:, k, at], ALU.subtract)
                    else:
                        ins = dve.scalar_tensor_tensor(out=HL[:, k, at], in0=NS[:, k, at], scalar=shift(st, k),
                                                       in1=HH[:, k, at], op0=ALU.add, op1=ALU.subtract)
                    ins.then_inc(normed, 1)
                for i, part in enumerate(parts):
                    scale(*part)
                    if i >= 2:
                        rest(*parts[i - 2])
                for part in parts[-2:]:
                    rest(*part)
                c["normed"] += len(parts)

            def norm_modulated(T, n, l, shift_tile):
                norm_split(T, lambda st, k: MA[:, n, st, k:k + 1],
                           lambda st, k: MOD[:, l, shift_tile + k, st:st + 1])

            def attention(units):
                u0 = c["unit"]
                c["unit"] += len(units)

                def maxima(u):
                    g, x = u0 + u, units[u]
                    s = att_bank("S", g)[:, 0:x["nk"]]
                    m, nm = MX[:, g % N_P:g % N_P + 1], NM[:, g % N_P:g % N_P + 1]
                    dve.wait_ge(scores_ready, g + 1)
                    if x["sink"] is None:
                        dve.tensor_reduce(nm, s, AX.X, ALU.max, negate=True).then_inc(negmax, 1)
                        return
                    step(dve.tensor_reduce(m, s, AX.X, ALU.max))
                    dve.tensor_scalar(nm, m, x["sink"], -1.0, ALU.max, ALU.mult).then_inc(negmax, 1)

                def normalise(u):
                    g, x = u0 + u, units[u]
                    r = RIN[:, g % N_P:g % N_P + 1]
                    total = SUM[:, g % N_P:g % N_P + 1]
                    dve.wait_ge(exp_done, g + 1)
                    if x["sink"] is not None:
                        step(dve.tensor_tensor(total, total, ESINK[:, g % N_P:g % N_P + 1], ALU.add))
                    step(dve.reciprocal(r, total))
                    dve.tensor_scalar(PROB[:, g % N_P, 0:x["nk"]], PROB[:, g % N_P, 0:x["nk"]], r, None, ALU.mult
                                      ).then_inc(probs, 1)

                for u in range(AHEAD):
                    maxima(u)
                normalise(0)
                for u in range(len(units)):
                    if u + 1 < len(units):
                        normalise(u + 1)
                    if u + AHEAD < len(units):
                        maxima(u + AHEAD)

            def merge(L, n, Y, T):
                for b in range(n):
                    for hf in range(2):
                        for j in range(4):
                            name = f"{L}o{b}{hf}{j}"
                            gate = f"{L}gate{b}{hf}{j}"
                            split(name)
                            dve.wait_ge(freed["act"], plan.freed[gate][1])
                            ps, y = bank(name)[:, 0:T], Y[:, hf * 4 + j, 0:T]
                            dst = y if b == 0 else TMP[:, j % 2, 0:T]
                            dve.tensor_tensor(dst, SG[:, j, 0:T], ps, ALU.mult).then_inc(freed["dve"], 1)
                            own(name)
                            if b:
                                ins = dve.tensor_tensor(y, y, TMP[:, j % 2, 0:T], ALU.add)
                                if b == n - 1:
                                    c["merged"] += 1
                                    ins.then_inc(merged, 1)
                                    dve.wait_ge(merged, c["merged"])
                                else:
                                    step(ins)

            def route(j):
                r = TMP[:, 1, j * S:j * S + S]
                at = VEC_AT["priority"][0]
                pri8, pri4 = VEC[:, at:at + 8], VEC[:, at + 4:at + 8]
                name = f"router{j}"
                dve.tensor_copy(r[:, 0:36], bank(name)[:, 0:36]).then_inc(freed["dve"], 1)
                own(name)
                col = {n: r[:, i:i + 1] for n, i in dict(gmax=49, gw=50, best=51, m1=104, m2=105, dist=106,
                                                         ratio=107, s=108, w1=110, w2=111).items()}

                def first_of_max(out, v, m, pri, tmp):
                    step(dve.tensor_reduce(m, v, AX.X, ALU.max))
                    step(dve.scalar_tensor_tensor(out=tmp, in0=v, scalar=m, in1=pri, op0=ALU.is_equal, op1=ALU.mult))
                    step(dve.tensor_reduce(col["best"], tmp, AX.X, ALU.max))
                    step(dve.tensor_scalar(out, tmp, col["best"], None, ALU.is_equal))
                first_of_max(r[:, 52:56], r[:, 0:4], col["gmax"], pri4, r[:, 56:60])
                dve.tensor_scalar(r[:, 40:44], r[:, 0:4], col["gmax"], None, ALU.subtract).then_inc(router_group, 1)
                e8 = r[:, 64:72]
                step(dve.tensor_scalar(e8, r[:, 4:12], r[:, 52:53], None, ALU.mult))
                for g in range(1, N_GROUPS):
                    step(dve.scalar_tensor_tensor(out=e8, in0=r[:, 4 + 8 * g:12 + 8 * g], scalar=r[:, 52 + g:53 + g],
                                                  in1=e8, op0=ALU.mult, op1=ALU.add))
                oh1, oh2 = r[:, 80:88], r[:, 88:96]
                first_of_max(oh1, e8, col["m1"], pri8, r[:, 72:80])
                step(dve.scalar_tensor_tensor(out=r[:, 96:104], in0=oh1, scalar=NEG, in1=e8, op0=ALU.mult, op1=ALU.add))
                first_of_max(oh2, r[:, 96:104], col["m2"], pri8, r[:, 72:80])
                dve.tensor_tensor(col["dist"], col["m2"], col["m1"], ALU.subtract).then_inc(router_top, 1)
                dve.wait_ge(router_exp, 2 * j + 2)
                step(dve.reciprocal(col["gw"], r[:, 48:49]))
                step(dve.tensor_scalar(col["s"], col["ratio"], 1.0, None, ALU.add))
                step(dve.reciprocal(col["s"], col["s"]))
                step(dve.tensor_tensor(col["w1"], col["s"], col["gw"], ALU.mult))
                step(dve.tensor_tensor(col["w2"], col["w1"], col["ratio"], ALU.mult))
                c8 = r[:, 112:120]
                step(dve.tensor_scalar(c8, oh1, col["w1"], None, ALU.mult))
                step(dve.scalar_tensor_tensor(out=c8, in0=oh2, scalar=col["w2"], in1=c8, op0=ALU.mult, op1=ALU.add))
                for g in range(N_GROUPS):
                    ins = dve.tensor_scalar(SM[:, 64 + 32 * j + 8 * g:72 + 32 * j + 8 * g], c8, r[:, 52 + g:53 + g],
                                            None, ALU.mult)
                ins.then_inc(combined, 1)

            dve.wait_ge(loaded_x, 48)
            for name, dim in (("qn_g", SWA_D), ("naq_0", NA_D), ("naq_1", NA_D), ("mq_0", MLA_QK), ("mq_1", MLA_QK)):
                step(dve.tensor_scalar(vec(name), vec(name), dim ** -0.5, None, ALU.mult))
            norm_split(S, lambda st, k: vec("mix_g", k))
            for j in range(4):
                split(f"sq{j}")
            for j in range(SWA_KV):
                split(f"sk{j}")
            for j in range(ST):
                split(f"sv{j}")
            qk = QK.rearrange("p j n -> p (j n)")
            for i in range(3):
                split(f"hn1_{i}")
                dve.wait_ge(hn_rstd, i + 1)
                x = qk[:, i * 512:i * 512 + 512]
                dve.scalar_tensor_tensor(out=x, in0=x, scalar=vec("qn_g" if i < 2 else "kn_g"), in1=R[:, 1 - i % 2, :],
                                         op0=ALU.mult, op1=ALU.mult).then_inc(hn_done, 1)
            c["hn"] = 3
            for name in four("rq") + four("rk") + ["rv0", "rv1"] + four("rg"):
                split(name)
            next_phase()
            dve.wait_ge(loaded_in, 16 * 7)
            for hd in range(RET_H):
                name = f"ret_s{hd}"
                ps = bank(name)
                if hd >= 2:
                    dve.wait_ge(tile_ready, plan.tile_at[f"ret_y{hd - 2}"] + 1)
                dve.tensor_tensor(RSM[:, hd % 2, :], BRET[:, hd, :], ps[:, 0:384], ALU.mult).then_inc(masked, 1)
                dve.wait_ge(masked, hd + 1)
                dve.nop().then_inc(freed["dve"], 1)
            yr = YR.rearrange("p h n -> p (h n)")
            for j in range(2):
                name = f"ret_mean{j}"
                at = slice(j * 512, j * 512 + 512)
                dve.scalar_tensor_tensor(out=yr[:, at], in0=bank(name), scalar=-1.0 / RET_D, in1=yr[:, at],
                                         op0=ALU.mult, op1=ALU.add).then_inc(freed["dve"], 1)
                own(name)
                dve.nop().then_inc(centred, 1)
            wait_rstd(2)
            for hd in range(RET_H):
                r = R[:, hd // 2, (hd % 2) * S:(hd % 2) * S + S]
                step(dve.scalar_tensor_tensor(out=YR[:, hd, :], in0=YR[:, hd, :], scalar=vec("ret_g", hd), in1=r,
                                              op0=ALU.mult, op1=ALU.mult))
                step(dve.scalar_tensor_tensor(out=YR[:, hd, :], in0=YR[:, hd, :], scalar=vec("ret_b", hd),
                                              in1=RG[:, hd, :], op0=ALU.add, op1=ALU.mult))
            next_phase()
            attention(swa_units())
            next_phase()
            YA = BR[:, 0:KD * S].rearrange("p (k n) -> p k n", k=KD)
            merge("A", 2, YA, S)
            for j in range(KD):
                name = f"Aout{j}"
                dve.tensor_tensor(X[:, j, 0:S], X[:, j, 0:S], bank(name)[:, 0:S], ALU.add).then_inc(freed["dve"], 1)
                own(name)
                c["x"] += 1
                dve.nop().then_inc(x_ready, 1)
            split("n_ffn")
            norm_split(S, lambda st, k: vec("ffn_g", k))
            step(dve.memset(TMP[:, 0, :], 0.0))

            def moe_rest(count, c_, q_mod):
                dve.wait_ge(moe_hi, count)
                src, hi, lo = moe_chunk(q_mod, c_)
                dve.tensor_tensor(lo, src, hi, ALU.subtract).then_inc(moe_lo, 1)
            split("router1")
            for q in range(3):
                moe_rest(q + 1, q, q)
            route(0)
            moe_rest(4, 3, 3)
            route(1)

            def weigh(x, e):
                sg = SGM[:, x, :]
                dve.tensor_tensor(sg, sg, PS[:, GU_BANKS[x][1], :], ALU.mult).then_inc(moe_mul, 1)
                dve.wait_ge(moe_mul, e(1))
                sg = sg.rearrange("p (f n) -> p f n", f=FT)
                row = A[:, bass.ds(e(0) * S, S)]
                for f in range(FT):
                    ins = dve.tensor_tensor(sg[:, f, :], sg[:, f, :], row, ALU.mult)
                ins.then_inc(moe_weighed, 1)

            def hidden_rest(x, count):
                dve.wait_ge(moe_hid_hi, count)
                dve.tensor_tensor(HIDL[:, x, :], SGM[:, x, :], HIDH[:, x, :], ALU.subtract).then_inc(moe_hid, 1)

            def modulation(q, landed_count, steps):
                m, st = q // 2, q % 2
                if st == 0:
                    dve.wait_ge(mw_landed[m], landed_count)
                wait_after(dve, mod_step, steps)
                dve.tensor_tensor_reduce(out=JUNK, in0=MW[:, m, :], in1=SC[:, st, :], scale=1.0, scalar=0.0,
                                         op0=ALU.mult, op1=ALU.add, accum_out=MR[:, q:q + 1]).then_inc(mod_step, 1)

            def modulated(e, steps):
                dve.wait_ge(mod_step, steps)
                for st in range(2):
                    dst = MOD_FLAT[:, bass.ds(e * (2 * MT), 2 * MT)].rearrange("p (m s) -> p m s", s=2)[:, :, st]
                    src = MR.rearrange("p (m s) -> p m s", s=2)[:, :, st]
                    ins = dve.tensor_tensor(dst, src, BMOD[:, bass.ds(e * MT, MT)], ALU.add)
                ins.then_inc(mod_acc, 1)

            dve.wait_ge(silu_c, 1)
            for q in range(2):
                dve.wait_ge(comb_in[q], 16)

            def expert(x):
                j = 1 - x.j
                for q in range(6):
                    moe_rest(x.at(6, q - 1), q, 4 + q)
                    if q == 0:
                        wait_after(dve, mod_acc, x.at(1, -1))
                    if q == 1:
                        dve.wait_ge(moe_silu, x.at(1))
                        dve.wait_ge(moe_used, x.at(6, -4))
                        weigh(j, lambda n: x.at(1, n - 1) if n == 0 else x.at(1))
                    if q == 2:
                        hidden_rest(j, x.at(1))
                    modulation(q, x.at(16), x.at(6, q - 6))
                modulated(x.at(1, -1), x.at(6))
            experts(dve, expert)
            j = (N_EXP - 1) % 2
            dve.wait_ge(moe_silu, N_EXP)
            dve.wait_ge(moe_used, 6 * N_EXP - 2)
            weigh(j, lambda n: N_EXP - 1 if n == 0 else N_EXP)
            hidden_rest(j, N_EXP)
            for q in range(4, 6):
                moe_rest(MOE_CHUNKS - 5 + q, q, MOE_CHUNKS - 6 + q)
            dve.wait_ge(mod_acc, N_EXP - 1)
            for q in range(6):
                modulation(q, 16 * N_EXP, 6 * (N_EXP - 1) + q)
            modulated(N_EXP - 1, 6 * N_EXP)
            dve.wait_ge(mod_acc, N_EXP)
            dve.wait_ge(moe_used, MOE_CHUNKS)
            for d in range(KD):
                y = PS[:, 4 + d // 2, (d % 2) * S:(d % 2) * S + S]
                dve.tensor_tensor(X[:, d, 0:S], X[:, d, 0:S], y, ALU.add).then_inc(x_ready, 1)
            c["x"] += KD
            dve.wait_ge(x_ready, c["x"])
            split("n_pleg")
            norm_split(S, lambda st, k: vec("pleg_g", k))
            norm(KD, lambda k: PL[:, k, :], lambda k: PL[:, k, :], S, lambda k: vec("ple_g", k), r=1)
            dve.wait_ge(normed, c["normed"])
            for j in range(KD):
                split(f"pleg{j}")
                dve.wait_ge(freed["act"], plan.freed[f"pleg{j}"][1])
                dve.tensor_tensor(TMP[:, j % 2, 0:S], SG[:, j % 4, 0:S], PL[:, j, :], ALU.mult).then_inc(gate_used, 1)
                dve.wait_ge(gate_used, j + 1)
                dve.tensor_tensor(X[:, j, 0:S], X[:, j, 0:S], TMP[:, j % 2, 0:S], ALU.add).then_inc(x_ready, 1)
                c["x"] += 1
                dve.wait_ge(x_ready, c["x"])

            def gains(l):
                for n, (g, tile) in enumerate(((f"g1_{l}", 8), (f"g2_{l}", 32))):
                    at = VEC_AT[g][0]
                    for s in range(2):
                        step(dve.scalar_tensor_tensor(out=MA[:, n, s, :], in0=MOD[:, l, tile:tile + KD, s], scalar=1.0,
                                                      in1=VEC[:, at:at + KD], op0=ALU.add, op1=ALU.mult))
            gains(0)

            for l in range(2):
                L, b = f"B{l}", lens(l)
                T = b["T"]

                def residual(name, j, tile, last=True):
                    for s in range(T // S):
                        at = slice(s * S, s * S + S)
                        ins = dve.scalar_tensor_tensor(out=X[:, j, at], in0=bank(name)[:, at],
                                                       scalar=MOD[:, l, tile + j, s:s + 1], in1=X[:, j, at],
                                                       op0=ALU.mult, op1=ALU.add)
                        if s < T // S - 1:
                            step(ins)
                    ins.then_inc(freed["dve"], 1)
                    if last:
                        own(name)
                        c["x"] += 1
                        dve.nop().then_inc(x_ready, 1)
                split(f"{L}n1")
                norm_modulated(512, 0, l, 0)
                items = norm_items(l)
                mv = SM[:, 40:40 + 2 * (T // P)].rearrange("p (t s) -> p t s", s=2)

                def project(name, n=4):
                    behind = norms_behind(l, name) if name in ("q", "cq", "u") else {}
                    for j in range(n):
                        split(f"{L}{name}{j}")
                        for tile, _ in behind.get(j, []):
                            i = int(tile[6:])
                            split(tile)
                            dve.wait_ge(hn_rstd, c["hn"] + 1)
                            for x, (gain, k) in zip(items[i][0], items[i][4]):
                                w = x.shape[-1]
                                ins = dve.scalar_tensor_tensor(out=x, in0=x, scalar=vec(gain, k),
                                                               in1=R[:, 1 - i % 2, 0:w], op0=ALU.mult, op1=ALU.mult)
                            ins.then_inc(hn_done, 1)
                            c["hn"] += 1
                project("k")
                project("q")
                project("cq", 2)
                project("ckv", 1)
                project("kr", 1)
                for q_ in range(T // P):
                    split(f"{L}gv{q_}")
                    dve.wait_ge(freed["act"], plan.freed[f"{L}gv{q_}"][1])
                    step(dve.bn_stats(SM[:, 192:198], b["GV"][:, q_, :]))
                    ins = dve.bn_aggr(mv[:, q_, :], SM[:, 192:198])
                    if q_ < T // P - 1:
                        step(ins)
                    else:
                        ins.then_inc(gv_stats, 1)
                for j in range(4):
                    split(f"{L}v{j}")
                if l:
                    dve.wait_ge(lc_loaded, 16)

                def gating_norm(q_):
                    v = b["GV"][:, q_, :]
                    step(dve.tensor_scalar(v, v, mv[:, q_, 0:1], SM[:, 56 + q_:57 + q_], ALU.subtract, ALU.mult))
                    step(dve.tensor_tensor(v, v, LC[:, LC_G:LC_G + 512], ALU.mult))
                    ins = dve.tensor_tensor(v, v, LC[:, LC_B:LC_B + 512], ALU.add)
                    if q_ < T // P - 1:
                        step(ins)
                    else:
                        ins.then_inc(gv_ready, 1)
                split(f"{L}u0")
                dve.wait_ge(gv_rstd, l + 1)
                for q_ in range(T // P):
                    gating_norm(q_)
                    if q_ == 1:
                        split(f"{L}u0")
                project("u")
                for j in range(4):
                    dve.wait_ge(freed["act"], plan.freed[f"{L}u{j}"][1])
                for q_ in range(T // P):
                    u = b["U"][:, :, q_ * P:q_ * P + P]
                    ps = bank(f"{L}mix{q_}").rearrange("p (g n) -> p g n", g=GM_G)
                    dve.tensor_tensor(u, u, ps, ALU.mult).then_inc(freed["dve"], 1)
                next_phase()
                attention(na_units(l))
                next_phase()

                def head(i):
                    return b["MQ"][0:MLA_QK, i, :] if i < MLA_H else b["MK"][0:MLA_QK, i - MLA_H, :]

                def scale(i):
                    Ti = T if i < MLA_H else 512
                    name = f"{L}raw{i}"
                    dve.wait_ge(ml_sq, c["ml"] + i + 1)
                    dve.tensor_scalar(head(i)[:, 0:Ti], bank(name)[0:MLA_QK, 0:Ti],
                                      vec(f"mq_{l}" if i < MLA_H else f"mk_{l}")[0:MLA_QK], None, ALU.mult
                                      ).then_inc(freed["dve"], 1)

                def rotate(i):
                    Ti = T if i < MLA_H else 512
                    name = f"{L}rx{i}"
                    own(f"{L}raw{i}")
                    tmp, x = TMP[0:MLA_QK, i % 2, 0:S], head(i)
                    dve.tensor_tensor(tmp, SIN, bank(name)[0:MLA_QK, 0:S], ALU.mult).then_inc(freed["dve"], 1)
                    own(name)
                    step(dve.tensor_tensor(x[:, 0:S], x[:, 0:S], COS, ALU.mult))
                    step(dve.tensor_tensor(x[:, 0:S], x[:, 0:S], tmp, ALU.add))
                    dve.wait_ge(ml_rstd, c["ml"] + i + 1)
                    dve.tensor_tensor(x[:, 0:Ti], x[:, 0:Ti], R[0:MLA_QK, i % 2, 0:Ti], ALU.mult).then_inc(ml_done, 1)
                scale(0)
                for i in range(2 * MLA_H):
                    if i + 1 < 2 * MLA_H:
                        scale(i + 1)
                    rotate(i)
                c["ml"] += 2 * MLA_H
                next_phase()
                attention(mla_units(l))
                next_phase()
                merge(L, 3, b["Y"], T)
                for j in range(KD):
                    residual(f"{L}out{j}", j, 16)
                split(f"{L}n2")
                norm_modulated(T, 1, l, 24)
                hid0 = FFN // P * l

                def up(g):
                    def rest(j):
                        dve.wait_ge(hid_sq, hid0 + g * GT + j + 1)
                        dve.wait_ge(hid_hi, hid0 + g * GT + j + 1)
                        hi, lo = hidden(g, j, T)
                        dve.tensor_tensor(lo, SQ[:, j % 2, 0:T], hi, ALU.subtract).then_inc(hid_ready, 1)
                    for j in range(GT):
                        name = f"{L}up{g * GT + j}"
                        split(name)
                        dve.wait_ge(freed["act"], plan.freed[name][1])
                        if g * GT + j >= 2:
                            dve.wait_ge(hid_ready, hid0 + g * GT + j - 1)
                        relu = TMP[:, j % 2, 0:T]
                        dve.tensor_tensor(SQ[:, j % 2, 0:T], relu, relu, ALU.mult).then_inc(hid_sq, 1)
                        if j:
                            rest(j - 1)
                    rest(GT - 1)

                def down(g):
                    for j in range(KD):
                        if g:
                            own(f"{L}down{g - 1}_{j}")
                        residual(f"{L}down{g}_{j}", j, 40, last=g == GROUPS_F - 1)
                for g in range(GROUPS_F):
                    up(g)
                    if g:
                        down(g - 1)
                down(GROUPS_F - 1)
                if l == 0:
                    gains(1)
            next_phase()


def rows(a, n):
    return np.broadcast_to(np.asarray(a).reshape(1, -1), (n, np.asarray(a).size))


def constants():
    f = np.float32
    j = np.arange(P)
    cst = np.zeros((P, 3, P), f)
    cst[:, 0] = np.eye(P)
    cst[:, 1] = 1.0
    cst[:, 2] = (j[:, None] // 64 == j[None, :] // 64)
    lg = np.log1p(-np.exp2(-5.0 - np.arange(RET_H)))
    diff = np.arange(S)[None, :] - j[:, None]
    ret = np.where(diff[:, None, :] >= 0, np.exp(np.maximum(diff, 0)[:, None, :] * lg[None, :, None]), 0.0)
    ret = ret * RET_D ** -0.5
    ret = np.concatenate([ret, ret[:, :, 0:P]], axis=2).reshape(P, -1)
    rel = j[:, None] + P - np.arange(2 * P)[None, :]
    slopes = np.exp2(-8.0 * np.arange(1, SWA_H + 1) / SWA_H)
    swa = np.where(((rel >= 0) & (rel < P))[:, None, :], -slopes[None, :, None] * rel[:, None, :], NEG)
    mask1 = np.concatenate([ret, swa.reshape(P, -1)], axis=1).astype(f)
    tok = np.arange(S)
    freqs = (f(10000.0) ** (-np.arange(8, dtype=f) / f(8))).astype(f)
    rope = np.zeros((P, 2 * S + 2 * MLA_QK), f)
    rope[:, 0:S] = 1.0
    for axis, place in enumerate((tok // GRID_W, tok % GRID_W)):
        ang = place.astype(f)[None, :] * freqs[:, None]
        for half in range(2):
            r = MLA_NOPE + 16 * axis + 8 * half
            rope[r:r + 8, 0:S] = np.cos(ang)
            rope[r:r + 8, S:2 * S] = np.sin(ang)
        a, b = MLA_NOPE + 16 * axis + np.arange(8), MLA_NOPE + 16 * axis + 8 + np.arange(8)
        rope[b, 2 * S + a] = -1.0
        rope[a, 2 * S + b] = 1.0
    rope[np.arange(MLA_ROPE), 2 * S + MLA_QK + MLA_NOPE + np.arange(MLA_ROPE)] = 1.0
    return cst, mask1, rope


def window_bias(rpb):
    q, k = np.arange(S)[:, None], np.arange(S)[None, :]
    dr = k // GRID_W - q // GRID_W + 7
    cq, ck = q % GRID_W, k % GRID_W
    dc = np.clip(ck - cq, -(WIN_W - 1), WIN_W - 1) + WIN_W - 1
    c0 = np.clip(cq - WIN_W // 2, 0, GRID_W - WIN_W)
    inside = (ck >= c0) & (ck < c0 + WIN_W)
    out = np.where(inside[None], rpb[:, dr, dc], np.float32(NEG))
    return out.reshape(NA_H, ST, P, S).transpose(2, 1, 0, 3).reshape(P, -1)


def layout(i):
    f = np.float32
    i = {k: np.asarray(v) for k, v in i.items()}
    cst, mask1, rope = constants()

    def cols(a):
        return a.reshape(-1, P).T

    def twice(a):
        return np.concatenate([a, a]).reshape(P, 1)

    def padded(a):
        return np.concatenate([a, np.zeros(P - a.size, f)]).reshape(P, 1)
    vec = [np.full((P, 1), EPS, f), cols(i["mix_norm_g"][0]), cols(i["ffn_norm_g"][0]), cols(i["ple_gate_norm_g"][0]),
           cols(i["ple_norm_g"][0]), cols(i["ret_gn_g"][0]), cols(i["ret_gn_b"][0]), twice(i["q_norm_g"][0]),
           twice(i["k_norm_g"][0]), rows(i["attn_sinks"][0], P), rows(np.arange(8, 0, -1).astype(f), P)]
    for l in range(2):
        vec += [cols(i["g_norm1_2"][l]), cols(i["g_norm2_2"][l]), twice(i["na_q_gain_2"][l]),
                twice(i["na_k_gain_2"][l]), cols(i["mla_cq_gain_2"][l]), cols(i["mla_ckv_gain_2"][l]),
                padded(i["mla_q_gain_2"][l]), padded(i["mla_k_gain_2"][l])]
    vec.append(cols(i["b_mod_2"].reshape(-1)))
    ukv = i["mla_w_ukv_2"].reshape(2, P, MLA_H, MLA_NOPE + MLA_V)
    nope = np.concatenate([ukv[..., :MLA_NOPE], np.zeros((2, P, MLA_H, MLA_ROPE), f)], axis=3)
    ukv = np.concatenate([nope.reshape(2, P, -1), ukv[..., MLA_NOPE:].reshape(2, P, -1)], axis=2)
    lc = np.stack([np.concatenate([rows(i["gm_ln_g_2"][l], P), rows(i["gm_ln_b_2"][l], P),
                                   i["gm_w_s_2"][l].transpose(2, 0, 1).reshape(P, -1),
                                   rows(i["gm_b_s_2"][l], P)], axis=1) for l in range(2)])
    return dict(
        xT=i["x"][0].T, ctxT=i["ctx_2"][0].T, pT=i["p"][0, 0].T, vec=np.concatenate(vec, axis=1), cst=cst,
        rope=rope, mask1=mask1, lc=lc, na_bias=np.stack([window_bias(i["na_rpb_2"][l]) for l in range(2)]),
        w_in=i["w_in"][0],
        w_sk=np.concatenate([i["w_in"][0][:, C1["sk"] + 64 * (j // 2):C1["sk"] + 64 * (j // 2) + 64]
                             for j in range(4)], axis=1), w_ret_o=i["w_ret_o"][0], w_swa_o=i["w_swa_o"][0], w_out=i["w_out"][0],
        w_r=np.concatenate([i["w_router_group"][0], i["w_router_expert"][0]], axis=1),
        b_r=np.concatenate([i["b_router_group"][0], i["b_router_expert"][0]])[None],
        w_gate=i["w_exp_gate"][0], w_up=i["w_exp_up"][0], w_down=i["w_exp_down"][0], w_ple=i["w_ple"][0],
        w_ple_gate=i["w_ple_gate"][0], 
        w_mod=i["w_mod_2"].transpose(0, 2, 1).reshape(N_EXP, MOD_COLS, D),
        c_rows=np.concatenate([rows(i["c_2"], P), rows(i["c_ctx_2"], P)], axis=1),
         w_in_2=i["w_in_2"], na_w_o=i["na_w_o_2"],
        gm_w_o=i["gm_w_o_2"], w_uq=i["mla_w_uq_2"], w_ukv=ukv, mla_w_o=i["mla_w_o_2"], w_out_2=i["w_out_2"],
        ffn_w1=i["ffn_w1_2"], ffn_w2=i["ffn_w2_2"])


def build(nc, arrays):
    t = {name: nc.dram_tensor(f"in_{name}", a.shape, F32, kind="ExternalInput").ap() for name, a in arrays.items()}
    t["comb_rows"] = nc.dram_tensor("comb_rows", (N_EXP, S), F32, kind="Internal").ap()
    program(nc, t, nc.dram_tensor("out", (D, S), F32, kind="ExternalOutput").ap())


def kernel(**inputs):
    import concourse.bacc as _bacc
    from concourse.bass_utils import run_bass_kernel_spmd as _run

    nc = _bacc.Bacc("TRN2", target_bir_lowering=False, num_devices=1)
    arrays = {k: np.ascontiguousarray(v) for k, v in layout(inputs).items()}
    build(nc, arrays)
    r = _run(nc, [{f"in_{k}": v for k, v in arrays.items()}], core_ids=[0])
    return np.ascontiguousarray(r.results[0]["out"].T)[None]
```

```python
from contextlib import ExitStack

import numpy as np

import concourse.bass as bass
from concourse import mybir

F32 = mybir.dt.float32
F32R = mybir.dt.float32r
ALU = mybir.AluOpType
ACT = mybir.ActivationFunctionType
AX = mybir.AxisListType

P = 128
D = 1024
KD = D // P
S = 256
ST = S // P
EPS = 1e-6
NEG = -1e30

RET_H, RET_D = 4, 128
SWA_H, SWA_D, SWA_KV = 8, 64, 2
N_GROUPS, PER_GROUP, FF = 4, 8, 256
N_EXP = N_GROUPS * PER_GROUP
FT = FF // P
NA_H, NA_D = 8, 64
GRID_W, WIN_W = 64, 16
GM_G = 4
MLA_H, MLA_QK, MLA_NOPE, MLA_ROPE, MLA_V = 8, 96, 64, 32, 64
FFN = 4 * D

C1 = dict(rq=0, rk=512, rv=1024, rg=1536, sq=2048, sk=2560, sv=2688, gates=2816)
C2 = dict(k=0, v=512, ckv=1024, kr=1152, q=1184, u=1696, gv=2208, cq=2720, gates=2976)

VEC_COLS = [("eps", 1), ("mix_g", 8), ("ffn_g", 8), ("pleg_g", 8), ("ple_g", 8), ("ret_g", 4), ("ret_b", 4),
            ("qn_g", 1), ("kn_g", 1), ("sinks", 8), ("priority", 8)]
for _l in (0, 1):
    VEC_COLS += [(f"{n}{_l}", w) for n, w in
                 (("g1_", 8), ("g2_", 8), ("naq_", 1), ("nak_", 1), ("cq_", 2), ("ckv_", 1), ("mq_", 1),
                  ("mk_", 1))]
VEC_COLS += [("bmod", 96)]
VEC_AT, _n = {}, 0
for _name, _w in VEC_COLS:
    VEC_AT[_name] = (_n, _w)
    _n += _w
N_VEC = _n

LC_G, LC_B, LC_WS, LC_BS, N_LC = 0, 512, 1024, 1536, 2048

RING = 3
SLOT = 2048
CHUNK = 1024
BUFS = 3
FIRST = 2
GROUPS_F = 4
GT = FFN // P // GROUPS_F
X_UPDATES = 7 * KD
ACC = 4
N_P = 5
AHEAD = 4
MOD_COLS = 6 * D // (N_EXP // 2)
MT = MOD_COLS // P
MOD_TILES = 6 * KD


class Plan:

    def __init__(self):
        self.blocks = []
        self.block_at = {}
        self.block_end = {}
        self.tiles = []
        self.tile_at = {}
        self.freed = {}
        self.read = {"act": 0, "dve": 0}
        self.chunks = []
        self.chunk_end = []
        self.chunk_tile = []
        self.parts = 0
        self.floor = 0
        self.floors = []
        self.att = []
        self.att_at = {}
        self.units = 0

    def block(self, name, source, kt, cols):
        self.block_at[name] = len(self.blocks)
        self.blocks.append((name, source, kt, cols))

    def tile(self, name, reader, block=None):
        self.tile_at[name] = len(self.tiles)
        self.tiles.append((name, reader))
        self.read[reader] += 1
        self.freed[name] = (reader, self.read[reader])
        if block is not None:
            self.block_end[block] = ("tile", len(self.tiles))

    def chunk(self, block, k0, kn, c0, cn, end, tile):
        self.chunks.append((self.block_at[block], k0, kn, c0, cn))
        self.chunk_end.append(end)
        self.chunk_tile.append(tile)
        self.floors.append(self.floor)
        self.block_end[block] = ("chunk", len(self.chunks))

    def fm(self, names, source, reader, behind=None):
        for i in range(0, len(names), 2):
            n = min(2, len(names) - i)
            name = "w_" + names[i]
            self.block(name, source[:, i * P:(i + n) * P], KD, n * P)
            for j in range(n):
                self.tile(names[i + j], reader)
                self.chunk(name, 0, KD, j * P, P, ("tile", len(self.tiles)), len(self.tiles))
                for extra in (behind or {}).get(i + j, []):
                    self.tile(*extra)

    def fm_half(self, names, source, reader):
        name = "w_" + names[0]
        self.block(name, source, KD // 2, 4 * P)
        for c in range(2):
            for j in range(2):
                self.tile(names[2 * c + j], reader)
            self.chunk(name, 0, KD // 2, c * 2 * P, 2 * P, ("tile", len(self.tiles)), len(self.tiles))

    def tm(self, name, source, n_tiles, cols, reader):
        t0 = len(self.tiles)
        if cols < 512:
            self.block("w_" + name, source, KD, cols)
            for j in range(n_tiles):
                self.tile(f"{name}{j}", reader)
            self.chunk("w_" + name, 0, KD, 0, cols, ("tile", len(self.tiles)), len(self.tiles))
            return
        for hf in range(2):
            self.block(f"w_{name}{hf}", source[hf * 512:hf * 512 + 512, :], 4, cols)
        for j in range(n_tiles):
            self.tile(f"{name}{j}", reader)
        for q in range(4):
            if q < 3:
                self.parts += 1
            end = ("part", self.parts) if q < 3 else ("tile", len(self.tiles))
            self.chunk(f"w_{name}{q // 2}", 2 * (q % 2), 2, 0, cols, end, t0 if q < 3 else len(self.tiles))

    def fence(self):
        self.floor = len(self.tiles)

    def finish(self):
        need, last, land = [], 0, []
        for b, (name, *_) in enumerate(self.blocks):
            if b >= RING:
                kind, count = self.block_end[self.blocks[b - RING][0]]
                if kind == "tile":
                    last = max(last, count)
            land.append(last)
        last = 0
        for i, (b, *_) in enumerate(self.chunks):
            last = max(last, land[b], self.floors[i])
            if i >= BUFS:
                last = max(last, self.chunk_tile[i - BUFS])
            need.append(last)
        self.split_by = [sum(n <= t for n in need) for t in range(len(self.tiles))]

    def attention(self, n):
        u0 = self.units
        self.units += n

        def put(kind, u):
            self.att_at[(kind, u0 + u)] = len(self.att)
            self.att.append((kind, u0 + u))
        for u in range(AHEAD):
            put("S", u)
        for u in range(n):
            put("T", u)
            if u + AHEAD < n:
                put("S", u + AHEAD)
            if u:
                put("O", u - 1)
        put("O", n - 1)
        self.fence()


def four(name, j0=0):
    return [f"{name}{j0 + j}" for j in range(4)]


def merge_blocks(plan, L, w_in, gates, w_o, T):
    for b, w in enumerate(w_o):
        for hf in range(2):
            c = gates + b * D + hf * 512
            plan.fm(four(f"{L}gate{b}{hf}"), w_in[:, c:c + 512], "act")
            plan.fm_half(four(f"{L}o{b}{hf}"), w[:, hf * 512:hf * 512 + 512], "dve")


def out_blocks(plan, L, w):
    plan.fm([f"{L}out{j}" for j in range(KD)], w, "dve")


def norms_behind(l, name):
    first, n = {"q": (0, 4), "cq": (4, 2), "u": (6, 4 if l == 0 else 2)}[name]
    return {j: [(f"B{l}norm{first + j}", "act")] for j in range(n)}


def make_plan(t):
    plan = Plan()
    plan.tile("n_mix", "act")
    w = t["w_in"]
    at = lambda name, n=512: w[:, C1[name]:C1[name] + n]
    plan.fm(four("sq"), at("sq"), "act")
    plan.fm(["sk0", "sk1"], t["w_sk"], "act")
    plan.tm("sv", at("sv", P), ST, P, "act")
    plan.fm(four("rq"), at("rq"), "act", {j: [(f"hn1_{j}", "act")] for j in range(3)})
    plan.fm(four("rk"), at("rk"), "act")
    plan.tm("rv", at("rv"), ST, 512, "act")
    plan.fm(four("rg"), at("rg"), "act")
    plan.tile("ret_s0", "dve")
    for h in range(RET_H):
        if h + 1 < RET_H:
            plan.tile(f"ret_s{h + 1}", "dve")
        plan.tile(f"ret_y{h}", "act")
    for j in range(2):
        plan.tile(f"ret_mean{j}", "dve")
    for j in range(2):
        plan.tile(f"ret_var{j}", "act")
    plan.attention(ST * SWA_H)
    merge_blocks(plan, "A", w, C1["gates"], [t["w_ret_o"], t["w_swa_o"]], S)
    out_blocks(plan, "A", t["w_out"])
    plan.tile("n_ffn", "act")
    plan.tm("router", t["w_r"], ST, 36, "dve")
    plan.n_before_moe = len(plan.blocks)
    plan.fence()
    plan.block("ple", t["w_ple"], 2, 1024)
    for j in range(8):
        plan.tile(f"ple{j}", "act", "ple")
    plan.tile("n_pleg", "act")
    plan.fm([f"pleg{j}" for j in range(8)], t["w_ple_gate"], "act", {1: [("n_ple", "act")]})
    for l in range(2):
        L = f"B{l}"
        tok = 2 * S if l == 0 else S
        w = t["w_in_2"][l]
        at = lambda name, n=512: w[:, C2[name]:C2[name] + n]
        plan.tile(f"{L}n1", "act")
        plan.fm(four(L + "k"), at("k"), "act")
        plan.fm(four(L + "q"), at("q"), "act", norms_behind(l, "q"))
        plan.fm([L + "cq0", L + "cq1"], at("cq", 256), "act", norms_behind(l, "cq"))
        plan.fm([L + "ckv0", L + "kr0"], at("ckv", 256), "act")
        plan.tm(L + "gv", at("gv"), tok // P, 512, "act")
        plan.tm(L + "v", at("v"), 4, 512, "act")
        plan.fm(four(L + "u"), at("u"), "act", norms_behind(l, "u"))
        for j in range(tok // P):
            plan.tile(f"{L}mix{j}", "dve")
        plan.attention(tok // P * NA_H)
        plan.block(L + "uq", t["w_uq"][l], 2, MLA_H * MLA_QK)
        plan.block(L + "ukv", t["w_ukv"][l], 1, MLA_H * (MLA_QK + MLA_V))
        n = 2 * MLA_H

        def raw(i):
            plan.tile(f"{L}raw{i}", "dve", L + ("uq" if i < MLA_H else "ukv"))
        raw(0)
        for i in range(n):
            if i + 1 < n:
                raw(i + 1)
            plan.tile(f"{L}ss{i}", "act")
            plan.tile(f"{L}rx{i}", "dve")
        for j in range(4):
            plan.tile(f"{L}mv{j}", "act", L + "ukv")
        plan.attention(tok // P * MLA_H)
        merge_blocks(plan, L, w, C2["gates"], [t["na_w_o"][l], t["gm_w_o"][l], t["mla_w_o"][l]], tok)
        out_blocks(plan, L, t["w_out_2"][l])
        plan.tile(f"{L}n2", "act")

        def up(g):
            plan.fm([f"{L}up{g * GT + j}" for j in range(GT)], t["ffn_w1"][l][:, g * D:g * D + D], "act")

        def down(g):
            plan.fm([f"{L}down{g}_{j}" for j in range(KD)], t["ffn_w2"][l][g * D:g * D + D, :], "dve")
        for g in range(GROUPS_F):
            up(g)
            if g:
                down(g - 1)
        down(GROUPS_F - 1)
    plan.finish()
    return plan


def program(nc, t, out):
    plan = make_plan(t)
    ctx = ExitStack()
    with ctx:
        def sb(name, shape, dtype=F32):
            return ctx.enter_context(nc.sbuf_tensor(name, shape, dtype))

        def views(name, shape, name_r, shape_r):
            place = ExitStack()
            whole = place.enter_context(nc.sbuf_tensor(name, shape, F32))
            place.close()
            return whole, sb(name_r, shape_r, F32R)

        def sem(name):
            return ctx.enter_context(nc.semaphore(name))

        X = sb("X", [P, KD, 2 * S])
        HH = sb("HH", [P, KD, 2 * S], F32R)
        HL = sb("HL", [P, KD, 2 * S], F32R)
        ring = sb("ring", [P, RING, SLOT])
        A, AR = views("A", [P, 16384], "AR", [P, 16384])
        BR = sb("BR", [P, 4096])
        SQ = sb("SQ", [P, 2, 512])
        SCR, CR = views("SCR", [P, N_P * 520 + 1024], "CR", [P, BUFS, 2, CHUNK])
        R = sb("R", [P, 2, 512])
        TMP = sb("TMP", [P, 2, 512])
        CST = sb("CST", [P, 3, P])
        VEC = sb("VEC", [P, N_VEC])
        LC = sb("LC", [P, N_LC])
        ROPE = sb("ROPE", [P, 2 * S + 2 * MLA_QK])
        MOD = sb("MOD", [P, 2, 48, 2])
        MA = sb("MA", [P, 2, 2, KD])
        SM = sb("SM", [P, 320])
        JUNK = sb("JUNK", [P, D])
        PS = ctx.enter_context(nc.psum_tensor("PS", [P, 8, 512], F32))
        comb_rows = t["comb_rows"]

        IDENT, ONES, BLK = CST[:, 0, :], CST[:, 1, :], CST[:, 2, :]
        COS, SIN = ROPE[0:MLA_QK, 0:S], ROPE[0:MLA_QK, S:2 * S]
        ROT = ROPE[0:MLA_QK, 2 * S:2 * S + MLA_QK]
        KR_AT = ROPE[0:MLA_ROPE, 2 * S + MLA_QK:2 * S + 2 * MLA_QK]
        PROB = SCR[:, 0:N_P * 520].rearrange("p (b n) -> p b n", b=N_P)
        PT = SCR[:, N_P * 520:N_P * 520 + 1024].rearrange("p (b n) -> p b n", b=2)
        EPS_COL = VEC[:, 0:1]
        NM, SUM, RIN, MX, ESINK = (SM[:, 8 * i:8 * i + N_P] for i in range(5))

        def vec(name, k=0):
            at = VEC_AT[name][0] + k
            return VEC[:, at:at + 1]

        def cut(at, n, w):
            return A[:, at:at + n * w].rearrange("p (n w) -> p n w", n=n)

        SG = cut(10240, 4, 512)
        NS = cut(4096, KD, 512)
        NS2 = cut(0, KD, 512)
        RQ, RK, RV, RG = cut(0, 4, S), cut(1024, 4, S), cut(2048, ST, 512), cut(3072, 4, S)
        QK, SV, YR, YS = cut(4096, 6, S), cut(5632, ST, P), cut(5888, 4, S), cut(6912, 4, S)
        RSM = cut(7936, 2, 384)
        PIN = cut(15872, 2, S)
        BRET = BR[:, 0:1536].rearrange("p (h n) -> p h n", h=RET_H)
        BSWA = BR[:, 1536:3584].rearrange("p (h n) -> p h n", h=SWA_H)
        BCOMB = cut(0, N_EXP, S)
        SGM = cut(8192, 2, 512)
        HIDH = AR[:, 9216:10240].rearrange("p (n w) -> p n w", n=2)
        HIDL = AR[:, 10496:11520].rearrange("p (n w) -> p n w", n=2)
        CT = A[0:N_EXP, 10240:10496]
        MW = BR[:, 0:MT * D].rearrange("p (m n) -> p m n", m=MT)
        SC = cut(13568, 2, D)
        MR = SM[:, 224:224 + 2 * MT]
        MW2 = BR[:, 0:2 * D].rearrange("p (b n) -> p b n", b=2)
        SC2 = BR[:, 2 * D:4 * D].rearrange("p (s n) -> p s n", s=2)
        MOD_FLAT = MOD[:, :, :, :].rearrange("p l j s -> p (l j s)")
        BMOD = VEC[:, VEC_AT["bmod"][0]:VEC_AT["bmod"][0] + 96]
        PL = cut(0, KD, S)
        PLSQ = cut(2048, KD, S)

        loaded_in = sem("loaded_in")
        landed = [sem(f"weights_landed{i}") for i in range(RING)]
        loaded_x = sem("loaded_x")
        part_used, hi_done, lo_done = sem("part_used"), sem("chunk_high_done"), sem("chunk_split")
        norm_hi = sem("norm_high_done")
        tile_ready = sem("tile_ready")
        freed = {"act": sem("tile_freed_by_act"), "dve": sem("tile_freed_by_dve")}
        phase = {e: sem(f"phase_{e}") for e in ("pe", "act", "dve")}
        act_step, dve_step = sem("act_step"), sem("dve_step")
        squares, rstd, scaled, normed = sem("squares"), sem("rstd"), sem("scaled"), sem("normed")
        silu_c, modded, evac = sem("silu_c"), sem("modded"), sem("evacuated")
        masked = sem("ret_masked")
        ret_done = sem("retention_done")
        centred, varsq = sem("ret_centred"), sem("ret_varsq")
        hn_sq, hn_rstd = sem("head_squares"), sem("head_rstd")
        scores_ready, negmax, exp_done, probs = (sem("scores_ready"), sem("negmax_ready"), sem("exp_done"),
                                                 sem("probs_ready"))
        pt_ready, pt_copied, o_ready, o_stored = (sem("pt_ready"), sem("pt_copied"), sem("o_ready"),
                                                  sem("o_stored"))
        branch_hi, branch_split = sem("branch_high"), sem("branch_split")
        merged, merged_hi, merged_split = sem("merged"), sem("merged_high"), sem("merged_split")
        combined, comb_out, comb_t = sem("combined"), sem("comb_out"), sem("comb_t")
        comb_in = [sem(f"comb_in{i}") for i in range(2)]
        comb_turned = sem("comb_turned")
        moe_landed = {w: sem(f"moe_{w}_landed") for w in ("gate", "up", "down")}
        moe_hi, moe_lo, moe_used = sem("moe_chunk_high"), sem("moe_chunk_split"), sem("moe_chunk_used")
        moe_silu, moe_mul, moe_weighed, moe_hid_hi, moe_hid = (sem("moe_silu"), sem("moe_mul"), sem("moe_weighed"),
                                                               sem("moe_hid_high"), sem("moe_hid"))
        ml_sq, ml_rstd = sem("mla_squares"), sem("mla_rstd")
        gv_stats, gv_rstd, lc_loaded, bias_loaded = (sem("gv_stats"), sem("gv_rstd"), sem("lc_loaded"),
                                                     sem("bias_loaded"))
        hid_sq = sem("hid_square")
        hid_hi, hid_ready, x_ready, gv_ready = sem("hid_high"), sem("hid_ready"), sem("x_ready"), sem("gv_ready")
        mw_landed = [sem(f"w_mod_landed{m}") for m in range(MT)]
        mod_step, mod_acc = sem("mod_step"), sem("mod_acc")
        bias1_loaded = sem("bias1_loaded")
        c_again, silu_again, mod2_used, mod2_step = (sem("c_loaded_again"), sem("silu_c_again"), sem("w_mod2_used"),
                                                     sem("mod2_step"))
        mw2_landed = [sem(f"w_mod2_landed{i}") for i in range(2)]
        stored = sem("stored")
        hn_done, gate_used, ml_done = sem("head_norm_done"), sem("gate_used"), sem("mla_done")
        router_group, router_exp, router_top = sem("router_group"), sem("router_exp"), sem("router_top")

        def lens(l):
            T = 2 * S if l == 0 else S
            return dict(
                T=T, NQ=cut(0, 4, T), NK=cut(2048, 4, 512), NV=cut(4096, 4, 512), YN=cut(6144, 4, T),
                U=cut(8192, 4, T), GV=cut(10240, T // P, 512), CQ=cut(12288, 2, T), CKV=cut(13312, 1, 512),
                KR=A[0:MLA_ROPE, 13824:14336], YM=cut(14336, 4, T), MQ=cut(0, MLA_H, T), MV=cut(4096, 4, 512),
                MK=BR[:, :].rearrange("p (h n) -> p h n", h=MLA_H),
                BIAS=BR[:, :].rearrange("p (t h n) -> p t h n", t=ST, h=NA_H),
                Y=BR[:, 0:KD * T].rearrange("p (k n) -> p k n", k=KD))

        def part(at, n, T):
            return AR[:, at:at + n * T].rearrange("p (n w) -> p n w", n=n)

        def branch_parts(b, T):
            if T == S:
                hi = {0: 0, 1: 2048, 2: 0}[b]
                return part(hi, 4, T), part(hi + 1024, 4, T)
            return part({0: 0, 1: 4096, 2: 0}[b], 4, T), part({0: 2048, 1: 12288, 2: 2048}[b], 4, T)

        def merged_parts(k, T):
            lo = 4096 if T == S else (8192 if k < 4 else 12288 - 4 * T)
            hi = 8192 if T == S else 4096
            return AR[:, hi + k * T:hi + k * T + T], AR[:, lo + k * T:lo + k * T + T]

        def hidden(g, j, T):
            return [AR[:, at:at + T] for at in (((g % 2) * 2 + p) * GT * 512 + j * 512 for p in range(2))]

        def chunk_views(i):
            b, k0, kn, c0, cn = plan.chunks[i]
            _, _, kt, cols = plan.blocks[b]
            src = ring[:, b % RING, 0:kt * cols].rearrange("p (k n) -> p k n", k=kt)[:, k0:k0 + kn, c0:c0 + cn]
            return [src] + [CR[:, i % BUFS, p, 0:kn * cn].rearrange("p (k n) -> p k n", k=kn) for p in range(2)]

        MOE_CHUNKS = 6 * N_EXP

        def moe_chunk(q, c):
            w, half = ("gate", "up", "down")[c // 2], c % 2
            raw = ring[:, c // 2, :]
            if w == "down":
                return raw[:, half * CHUNK:half * CHUNK + CHUNK], CR[:, q % BUFS, 0, :], CR[:, q % BUFS, 1, :]
            raw = raw.rearrange("p (k n) -> p k n", k=KD)[:, :, half * P:half * P + P]
            return [raw] + [CR[:, q % BUFS, p, :].rearrange("p (k n) -> p k n", k=KD) for p in range(2)]

        class Expert:

            def __init__(self, base, i=None):
                self.base, self.i, self.j = base, i, base % 2

            def at(self, m, k=0):
                return m * self.base + k if self.i is None else (2 * m) * self.i + (m * self.base + k)

            def pair(self, m, k=0):
                p = (self.base - 1) // 2
                return m * p + k if self.i is None else m * self.i + (m * p + k)

        def experts(eng, body):
            for e in (1, 2):
                body(Expert(e))
            with eng.Fori(1, N_EXP // 2 - 1) as i:
                for base in (1, 2):
                    body(Expert(base, i))
            body(Expert(N_EXP - 1))

        def wait_after(eng, semaphore, count):
            if not isinstance(count, int) or count > 0:
                eng.wait_ge(semaphore, count)

        def bank_of(name):
            return PS[:, plan.tile_at[name] % ACC, :]

        def att_bank(kind, u):
            return PS[:, plan.att_at[(kind, u)] % 8, :]

        def swa_units():
            units = []
            for qt in range(ST):
                for h in range(SWA_H):
                    lo, kv = 64 * (h % 2), h // (SWA_H // SWA_KV)
                    keys = [(QK[lo:lo + 64, 4 + kv, (qt - 1) * P if qt else 0:(qt + 1) * P])]
                    nk = P if qt == 0 else 2 * P
                    units.append(dict(
                        q=QK[lo:lo + 64, h // 2, qt * P:qt * P + P], k=keys[0], nk=nk,
                        bias=BSWA[:, h, 2 * P - nk:2 * P], sink=vec("sinks", h),
                        v=[SV[:, j, kv * 64:kv * 64 + 64] for j in range(qt + 1 - nk // P, qt + 1)],
                        out=YS[lo:lo + 64, h // 2, qt * P:qt * P + P], lo=lo))
            return units

        def dense_units(q, k, v, y, T, bias):
            units = []
            for qt in range(T // P):
                k0, nk = (0, 512) if qt < ST else (S, S)
                for h in range(8):
                    lo = 64 * (h % 2)
                    units.append(dict(
                        q=q(h, qt * P), k=k(h, k0, nk), nk=nk,
                        bias=bias[:, qt, h, :] if bias is not None and qt < ST else None, sink=None,
                        v=[v[:, j, h * 64:h * 64 + 64] for j in range(k0 // P, (k0 + nk) // P)],
                        out=y[lo:lo + 64, h // 2, qt * P:qt * P + P], lo=lo))
            return units

        def na_units(l):
            b = lens(l)
            return dense_units(
                lambda h, c: b["NQ"][64 * (h % 2):64 * (h % 2) + 64, h // 2, c:c + P],
                lambda h, c, n: b["NK"][64 * (h % 2):64 * (h % 2) + 64, h // 2, c:c + n],
                b["NV"], b["YN"], b["T"], b["BIAS"])

        def mla_units(l):
            b = lens(l)
            return dense_units(lambda h, c: b["MQ"][0:MLA_QK, h, c:c + P],
                               lambda h, c, n: b["MK"][0:MLA_QK, h, c:c + n],
                               b["MV"], b["YM"], b["T"], None)

        r0 = plan.tile_at["router0"]
        GU_BANKS = [((r0 + 2) % ACC, (r0 + 3) % ACC), (r0 % ACC, (r0 + 1) % ACC)]

        def norm_items(l):
            b = lens(l)
            T = b["T"]
            nq = 4 * T // 512
            q = b["NQ"].rearrange("p j n -> p (j n)")
            items = [([b["NK"][:, i, :]], [SQ[:, i % 2, :]], BLK, 1.0 / NA_D, [f"nak_{l}"]) for i in range(4)]
            items += [([q[:, i * 512:i * 512 + 512]], [SQ[:, i % 2, :]], BLK, 1.0 / NA_D, [f"naq_{l}"])
                      for i in range(nq)]
            items.append(([b["CQ"][:, k, :] for k in range(2)], [TMP[:, k, 0:T] for k in range(2)], ONES,
                          1.0 / 256, [(f"cq_{l}", 0), (f"cq_{l}", 1)]))
            items.append(([b["CKV"][:, 0, :]], [SQ[:, (4 + nq + 1) % 2, :]], ONES, 1.0 / P, [f"ckv_{l}"]))
            return [(x, sq, lhs, inv, [g if isinstance(g, tuple) else (g, 0) for g in gains])
                    for x, sq, lhs, inv, gains in items]

        block = ctx.enter_context(nc.Block())

        @block.sync
        def _(sp):
            for dst, src in ((X[:, :, 0:S], t["xT"].rearrange("(k p) n -> p k n", p=P)),
                             (VEC[:, :], t["vec"]), (CST[:, :, :], t["cst"])):
                sp.dma_start(dst, src).then_inc(loaded_x, 16)

            def wait_used(n):
                kind, count = plan.block_end[plan.blocks[n][0]]
                sp.wait_ge(tile_ready if kind == "tile" else lo_done, count)

            def load_block(n, fresh=False):
                name, src, kt, cols = plan.blocks[n]
                if n >= RING and not fresh:
                    wait_used(n - RING)
                sp.dma_start(ring[:, n % RING, 0:kt * cols].rearrange("p (k n) -> p k n", k=kt),
                             src.rearrange("(k p) n -> p k n", p=P)).then_inc(landed[n % RING], 16)

            for n in range(RING):
                load_block(n)
            for dst, src in ((BR[:, 0:3584], t["mask1"]), (SM[0:1, 256:256 + 36], t["b_r"]),
                             (A[:, 13568:13568 + 2 * D], t["c_rows"]),
                             (X[:, :, S:2 * S], t["ctxT"].rearrange("(k p) n -> p k n", p=P)),
                             (ROPE[:, :], t["rope"]), (PIN, t["pT"].rearrange("(k p) n -> p k n", p=P)),
                             (LC[:, :], t["lc"][0])):
                sp.dma_start(dst, src).then_inc(loaded_in, 16)
            for n in range(RING, plan.n_before_moe):
                load_block(n)

            def load_expert(which, e):
                w, slot, kt = {"gate": (t["w_gate"], 0, KD), "up": (t["w_up"], 1, KD),
                               "down": (t["w_down"], 2, FT)}[which]
                sp.dma_start(ring[:, slot, :].rearrange("p (k n) -> p k n", k=kt),
                             w[bass.ds(e, 1)].rearrange("e (k p) n -> p (e k) n", p=P)
                             ).then_inc(moe_landed[which], 16)

            def load_mod(m, e):
                sp.dma_start(MW[:, m, :], t["w_mod"][bass.ds(e, 1)][:, m * P:m * P + P, :].rearrange("e p k -> p (e k)")
                             ).then_inc(mw_landed[m], 16)
            for n in range(plan.n_before_moe - RING, plan.n_before_moe):
                wait_used(n)
            for which in ("gate", "up", "down"):
                load_expert(which, 0)
            for m in range(MT):
                load_mod(m, 0)
            sp.wait_ge(comb_t, 1)
            sp.dma_start(comb_rows, CT).then_inc(comb_out, 16)
            sp.wait_ge(moe_lo, 2)
            load_expert("gate", 1)
            sp.wait_ge(comb_out, 16)
            flat = comb_rows.rearrange("e n -> (e n)")

            def combine_rows(q, lo, hi):
                sp.dma_start(A[:, lo:hi], flat[lo:hi].rearrange("(o n) -> o n", o=1).broadcast_to([P, hi - lo])
                             ).then_inc(comb_in[q], 16)
            combine_rows(0, 0, 2 * S)
            sp.wait_ge(moe_lo, 4)
            load_expert("up", 1)
            combine_rows(1, 2 * S, N_EXP * S)

            def refill(x, last=False):
                def next_mod(m):
                    sp.wait_ge(mod_step, x.pair(2 * MT, 2 * m + 2))
                    load_mod(m, x.pair(1, 1))
                sp.wait_ge(moe_lo, x.at(6))
                if not last:
                    load_expert("gate", x.at(1, 1))
                    if x.j == 0:
                        next_mod(1)
                sp.wait_ge(moe_lo, x.at(6, 2))
                if not last:
                    load_expert("up", x.at(1, 1))
                    if x.j == 1:
                        next_mod(0)
                sp.wait_ge(moe_lo, x.at(6, 4))
                load_expert("down", x.at(1))
                if x.j == 0:
                    next_mod(2)
            for e in (1, 2):
                refill(Expert(e))
            with sp.Fori(1, N_EXP // 2 - 1) as i:
                for base in (1, 2):
                    refill(Expert(base, i))
            refill(Expert(N_EXP - 1), last=True)
            sp.wait_ge(moe_lo, MOE_CHUNKS)
            n0 = plan.n_before_moe
            for n in range(n0, plan.block_at["w_B0gv0"]):
                load_block(n, fresh=n < n0 + RING)
            sp.wait_ge(mod_acc, N_EXP // 2)
            sp.dma_start(BR[:, :], t["na_bias"][0]).then_inc(bias_loaded, 16)
            for n in range(plan.block_at["w_B0gv0"], len(plan.blocks)):
                load_block(n)
            for k in range(0, KD, 2):
                sp.wait_ge(x_ready, X_UPDATES - KD + k + 2)
                sp.dma_start(out[k * P:k * P + 2 * P].rearrange("(k p) n -> p k n", p=P), X[:, k:k + 2, 0:S]
                             ).then_inc(stored, 16)
            sp.wait_ge(stored, 16 * KD // 2)

        @block.gpsimd
        def _(gp):
            gp.wait_ge(tile_ready, plan.tile_at["B0out7"] + 1)
            gp.dma_start(BR[:, 2 * D:4 * D], t["c_rows"]).then_inc(c_again, 16)
            gp.dma_start(LC[:, :], t["lc"][1]).then_inc(lc_loaded, 16)
            for n in range(MOD_TILES):
                if n >= 2:
                    gp.wait_ge(mod2_used, n - 1)
                gp.dma_start(MW2[:, n % 2, :], t["w_mod2"][n]).then_inc(mw2_landed[n % 2], 16)
            gp.wait_ge(mod2_used, MOD_TILES)
            gp.dma_start(BR[:, :], t["na_bias"][1]).then_inc(bias1_loaded, 16)

        @block.tensor
        def _(pe):
            ph = [0]
            c = dict(squares=0, normed=0, evac=0, hn=0, ml=0, unit=0, merged=0, chunk=0, branch=0)
            out_waits = []
            waits = []

            def next_phase():
                ph[0] += 1
                pe.drain().then_inc(phase["pe"], 1)
                for e in ("act", "dve"):
                    pe.wait_ge(phase[e], ph[0])

            def open_tile(name):
                n = plan.tile_at[name]
                if n >= ACC:
                    reader, count = plan.freed[plan.tiles[n - ACC][0]]
                    pe.wait_ge(freed[reader], count)
                return PS[:, n % ACC, :]

            def weights(name):
                n = plan.block_at[name]
                _, _, kt, cols = plan.blocks[n]
                pe.wait_ge(landed[n % RING], 16 * (n // RING + 1))
                return ring[:, n % RING, 0:kt * cols].rearrange("p (k n) -> p k n", k=kt)

            def fm(W, tile, c0, M, rhs, kt, T):
                bank = open_tile(tile)
                for k in range(kt):
                    mm = pe.matmul(bank[0:M, 0:T], W[:, k, c0:c0 + M], rhs(k), start=(k == 0), stop=(k == kt - 1))
                mm.then_inc(tile_ready, 1)

            def split_weights():
                i = c["chunk"]
                c["chunk"] += 1
                pe.wait_ge(lo_done, i + 1)
                return chunk_views(i)[1:]

            def product(bank, w, x, k, start, stop):
                (wh, wl), (xh, xl) = w, x
                pe.matmul(bank, wh, xh, start=start, stop=False)
                pe.matmul(bank, wh, xl, start=False, stop=False)
                return pe.matmul(bank, wl, xh, start=False, stop=stop)

            def fm3(tile, T, x=None):
                bank = open_tile(tile)
                W = split_weights()
                for k in range(KD):
                    if out_waits:
                        pe.wait_ge(merged_split, out_waits.pop(0))
                    rhs = x(k) if x else (HH[:, k, 0:T], HL[:, k, 0:T])
                    mm = product(bank[:, 0:T], [w[:, k, :] for w in W], rhs, k, k == 0, k == KD - 1)
                mm.then_inc(tile_ready, 1)

            def fm3_first(tiles, T):
                banks = [open_tile(tile) for tile in tiles]
                W = [split_weights() for _ in tiles]
                for k in range(KD):
                    pe.wait_ge(normed, waits.pop(0))
                    for bank, w in zip(banks, W):
                        mm = product(bank[:, 0:T], [part[:, k, :] for part in w], (HH[:, k, 0:T], HL[:, k, 0:T]),
                                     k, k == 0, k == KD - 1)
                        if k == KD - 1:
                            mm.then_inc(tile_ready, 1)

            def tm3(name, n, cols):
                banks = [open_tile(f"{name}{j}") for j in range(n)]
                for q in range(4):
                    W = split_weights()
                    for j in range(n):
                        at = slice(j * P, j * P + P)
                        for kk in range(2):
                            k = 2 * q + kk
                            mm = product(banks[j][:, 0:cols], (HH[:, k, at], HL[:, k, at]),
                                         [w[:, kk, :] for w in W], k, k == 0, k == KD - 1)
                        if q == 3:
                            mm.then_inc(tile_ready, 1)
                    if q < 3:
                        mm.then_inc(part_used, 1)

            def tm3_small(name, n, cols, bias=None):
                W = split_weights()
                for j in range(n):
                    at = slice(j * P, j * P + P)
                    bank = open_tile(f"{name}{j}")
                    for k in range(KD):
                        if waits:
                            pe.wait_ge(normed, waits.pop(0))
                        mm = product(bank[:, 0:cols], (HH[:, k, at], HL[:, k, at]), [w[:, k, :] for w in W], k,
                                     k == 0, k == KD - 1 and bias is None)
                    if bias is not None:
                        mm = pe.matmul(bank[:, 0:cols], ONES[0:1, :], bias, start=False, stop=True)
                    mm.then_inc(tile_ready, 1)

            def norm_sums(tile, n, sq, T, lhs=None):
                bank = open_tile(tile)
                for k in range(n):
                    c["squares"] += 1
                    pe.wait_ge(squares, c["squares"])
                    mm = pe.matmul(bank[:, 0:T], ONES, sq(k), start=(k == 0), stop=(k == n - 1))
                mm.then_inc(tile_ready, 1)

            def h_ready(streams):
                for k in range(KD):
                    c["normed"] += streams
                    waits.append(c["normed"])

            def ns(T, where=NS):
                return lambda k: where[:, k, 0:T]

            def head_sums(tiles):
                for name in tiles:
                    bank = open_tile(name)
                    pe.wait_ge(hn_sq, c["hn"] + 1)
                    pe.matmul(bank[:, :], BLK, SQ[:, c["hn"] % 2, :], start=True, stop=True).then_inc(tile_ready, 1)
                    c["hn"] += 1

            def attention(units):
                u0 = c["unit"]
                c["unit"] += len(units)

                def open_att(kind, u):
                    m = plan.att_at[(kind, u0 + u)]
                    if m >= 8:
                        kd, old = plan.att[m - 8]
                        pe.wait_ge({"S": exp_done, "T": pt_copied, "O": o_stored}[kd], old + 1)
                    return PS[:, m % 8, :]

                def scores(u):
                    bank, x = open_att("S", u), units[u]
                    bias = x["bias"]
                    mm = pe.matmul(bank[:, 0:x["nk"]], x["q"], x["k"], start=True, stop=bias is None)
                    if bias is not None:
                        mm = pe.matmul(bank[:, 0:bias.shape[-1]], IDENT, bias, start=False, stop=True)
                    mm.then_inc(scores_ready, 1)

                def turn(u):
                    bank, x = open_att("T", u), units[u]
                    pe.wait_ge(probs, u0 + u + 1)
                    n = x["nk"] // P
                    for j in range(n):
                        mm = pe.transpose(bank[:, j * P:j * P + P], PROB[:, (u0 + u) % N_P, j * P:j * P + P], IDENT)
                    mm.then_inc(pt_ready, 1)

                def values(u):
                    bank, x = open_att("O", u), units[u]
                    pe.wait_ge(pt_copied, u0 + u + 1)
                    n = x["nk"] // P
                    for j in range(n):
                        mm = pe.matmul(bank[x["lo"]:x["lo"] + 64, 0:P], x["v"][j],
                                       PT[:, (u0 + u) % 2, j * P:j * P + P], start=(j == 0), stop=(j == n - 1))
                    mm.then_inc(o_ready, 1)

                for u in range(AHEAD):
                    scores(u)
                for u in range(len(units)):
                    turn(u)
                    if u + AHEAD < len(units):
                        scores(u + AHEAD)
                    if u:
                        values(u - 1)
                values(len(units) - 1)

            def merge(L, n, T):
                for b in range(n):
                    yh, yl = branch_parts(b, T)
                    for hf in range(2):
                        for j in range(4):
                            fm3(f"{L}gate{b}{hf}{j}", T)
                        for j in range(4):
                            bank = open_tile(f"{L}o{b}{hf}{j}")
                            if j % 2 == 0:
                                W = split_weights()
                            at = slice((j % 2) * P, (j % 2) * P + P)
                            for k in range(4):
                                if hf == 0 and j == 0:
                                    c["branch"] += 1
                                    pe.wait_ge(branch_split, c["branch"])
                                mm = product(bank[:, 0:T], [w[:, k, at] for w in W], (yh[:, k, :], yl[:, k, :]), k,
                                             k == 0, k == 3)
                            mm.then_inc(tile_ready, 1)

            def project_out(L, T):
                for j in range(KD):
                    if j == 0:
                        for k in range(KD):
                            c["merged"] += 1
                            out_waits.append(c["merged"])
                    fm3(f"{L}out{j}", T, lambda k: merged_parts(k, T))

            pe.wait_ge(loaded_x, 48)
            norm_sums("n_mix", KD, ns(S), S)
            h_ready(1)
            fm3_first([f"sq{j}" for j in range(FIRST)], S)
            for j in range(FIRST, 4):
                fm3(f"sq{j}", S)
            for j in range(SWA_KV):
                fm3(f"sk{j}", S)
            tm3_small("sv", ST, P)
            for j in range(4):
                fm3(f"rq{j}", S)
                if j < 3:
                    head_sums([f"hn1_{j}"])
            for j in range(4):
                fm3(f"rk{j}", S)
            tm3("rv", ST, 512)
            for j in range(4):
                fm3(f"rg{j}", S)
            next_phase()
            pe.wait_ge(loaded_in, 16 * 7)
            def ret_scores(hd):
                bank = open_tile(f"ret_s{hd}")
                pe.matmul(bank[:, 0:S], RK[:, hd, 0:P], RQ[:, hd, :], start=True, stop=True)
                pe.matmul(bank[:, S:S + P], RK[:, hd, P:S], RQ[:, hd, P:S], start=True, stop=True
                          ).then_inc(tile_ready, 1)
            ret_scores(0)
            for hd in range(RET_H):
                if hd + 1 < RET_H:
                    ret_scores(hd + 1)
                bank = open_tile(f"ret_y{hd}")
                pe.wait_ge(masked, hd + 1)
                pe.matmul(bank[:, 0:S], RV[:, 0, hd * P:hd * P + P], RSM[:, hd % 2, 0:S], start=True, stop=False)
                pe.matmul(bank[:, P:S], RV[:, 1, hd * P:hd * P + P], RSM[:, hd % 2, S:S + P], start=False, stop=True
                          ).then_inc(tile_ready, 1)
            pe.wait_ge(evac, 1)
            yr = YR.rearrange("p h n -> p (h n)")
            for j in range(2):
                pe.matmul(open_tile(f"ret_mean{j}"), ONES, yr[:, j * 512:j * 512 + 512], start=True, stop=True
                          ).then_inc(tile_ready, 1)
            for j in range(2):
                bank = open_tile(f"ret_var{j}")
                pe.wait_ge(varsq, j + 1)
                pe.matmul(bank, ONES, SQ[:, j, :], start=True, stop=True).then_inc(tile_ready, 1)
            next_phase()
            attention(swa_units())
            next_phase()
            merge("A", 2, S)
            project_out("A", S)
            norm_sums("n_ffn", KD, ns(S, NS2), S)
            h_ready(1)
            tm3_small("router", ST, 36, SM[0:1, 256:256 + 36])
            Y = [PS[:, 4 + d // 2, (d % 2) * S:(d % 2) * S + S] for d in range(KD)]

            def gate_up(x, q0, q_mod):
                for q in range(4):
                    pe.wait_ge(moe_lo, q0 + q + 1 if isinstance(q0, int) else q0(q + 1))
                    W = moe_chunk(q_mod + q, q)[1:]
                    bank = PS[:, GU_BANKS[x.j][q // 2], (q % 2) * S:(q % 2) * S + S]
                    for k in range(KD):
                        mm = product(bank, [w[:, k, :] for w in W], (HH[:, k, 0:S], HL[:, k, 0:S]), k, k == 0,
                                     k == KD - 1)
                    mm.then_inc(moe_used, 1)

            def down(j, q0, q_mod):
                for f in range(FT):
                    pe.wait_ge(moe_lo, q0(f + 1))
                    W = moe_chunk(q_mod + f, 4 + f)[1:]
                    at = slice(f * S, f * S + S)
                    for d in range(KD):
                        for w, x in ((0, HIDH), (0, HIDL), (1, HIDH)):
                            mm = pe.matmul(Y[d], W[w][:, d * P:d * P + P], x[:, j, at], start=False, stop=False,
                                           skip_group_check=True)
                    mm.then_inc(moe_used, 1)

            gate_up(Expert(0), 0, 0)
            pe.wait_ge(combined, ST)
            for j in range(ST):
                mm = pe.transpose(PS[0:N_EXP, 4, j * P:j * P + P], SM[:, 64 + 32 * j:96 + 32 * j], IDENT)
            mm.then_inc(comb_turned, 1)
            pe.wait_ge(comb_t, 1)
            for b in range(4):
                pe.matmul(PS[:, 4 + b, :], TMP[:, 0, 0:P], TMP[:, 0, :], start=True, stop=False,
                          skip_group_check=True)

            def expert(x):
                wait_after(pe, moe_mul, x.at(1, -1))
                gate_up(x, lambda n: x.at(6, n - 2), 4)
                pe.wait_ge(moe_hid, x.at(1))
                down(1 - x.j, lambda n: x.at(6, n + 2), 2)
            experts(pe, expert)
            pe.wait_ge(moe_hid, N_EXP)
            down((N_EXP - 1) % 2, lambda n: MOE_CHUNKS - 2 + n, 1)

            W = weights("ple")
            for j in range(8):
                fm(W, f"ple{j}", j * P, P, lambda k: PIN[:, k, :], 2, S)
            norm_sums("n_pleg", KD, ns(S), S)
            h_ready(1)
            fm3_first(["pleg0", "pleg1"], S)
            for j in range(1, KD):
                if j > 1:
                    fm3(f"pleg{j}", S)
                if j == 1:
                    norm_sums("n_ple", KD, lambda k: PLSQ[:, k, :], S)
                    c["normed"] += KD

            for l in range(2):
                L, b = f"B{l}", lens(l)
                T = b["T"]
                norm_sums(f"{L}n1", KD, ns(512), 512)
                h_ready(2)
                items = norm_items(l)

                def project(name, T, n=4):
                    behind = norms_behind(l, name) if name in ("q", "cq", "u") else {}
                    for j in range(n):
                        fm3(f"{L}{name}{j}", T)
                        for norm_tile, _ in behind.get(j, []):
                            _, sq, lhs, _, _ = items[int(norm_tile[6:])]
                            bank = open_tile(norm_tile)
                            for k, x in enumerate(sq):
                                c["hn"] += 1
                                pe.wait_ge(hn_sq, c["hn"])
                                mm = pe.matmul(bank[:, 0:x.shape[-1]], lhs, x, start=(k == 0),
                                               stop=(k == len(sq) - 1))
                            mm.then_inc(tile_ready, 1)
                fm3_first([f"{L}k{j}" for j in range(FIRST)], 512)
                for j in range(FIRST, 4):
                    fm3(f"{L}k{j}", 512)
                project("q", T)
                project("cq", T, 2)
                project("ckv", 512, 1)
                project("kr", 512, 1)
                tm3(L + "gv", T // P, 512)
                tm3(L + "v", 4, 512)
                project("u", T)
                pe.wait_ge(gv_ready, l + 1)
                for q in range(T // P):
                    bank = open_tile(f"{L}mix{q}")
                    for g in range(GM_G):
                        pe.matmul(bank[:, g * P:g * P + P], b["GV"][:, q, g * P:g * P + P],
                                  LC[:, LC_WS + g * P:LC_WS + g * P + P], start=True, stop=False)
                        mm = pe.matmul(bank[:, g * P:g * P + P], ONES[0:1, :],
                                       LC[0:1, LC_BS + g * P:LC_BS + g * P + P], start=False, stop=True)
                    mm.then_inc(tile_ready, 1)
                next_phase()
                pe.wait_ge((bias_loaded, bias1_loaded)[l], 16)
                attention(na_units(l))
                next_phase()
                Wq, Wk = weights(L + "uq"), weights(L + "ukv")

                def raw(i):
                    bank, hd = open_tile(f"{L}raw{i}"), i % MLA_H
                    if i < MLA_H:
                        for k in range(2):
                            mm = pe.matmul(bank[0:MLA_QK, 0:T], Wq[:, k, hd * MLA_QK:hd * MLA_QK + MLA_QK],
                                           b["CQ"][:, k, 0:T], start=(k == 0), stop=(k == 1))
                    else:
                        pe.matmul(bank[0:MLA_QK, :], Wk[:, 0, hd * MLA_QK:hd * MLA_QK + MLA_QK], b["CKV"][:, 0, :],
                                  start=True, stop=False)
                        mm = pe.matmul(bank[0:MLA_QK, :], KR_AT, b["KR"], start=False, stop=True)
                    mm.then_inc(tile_ready, 1)
                raw(0)
                for i in range(2 * MLA_H):
                    if i + 1 < 2 * MLA_H:
                        raw(i + 1)
                    Ti = T if i < MLA_H else 512
                    bank = open_tile(f"{L}ss{i}")
                    pe.wait_ge(ml_sq, c["ml"] + i + 1)
                    pe.matmul(bank[0:MLA_QK, 0:Ti], ONES[0:MLA_QK, 0:MLA_QK], SQ[0:MLA_QK, i % 2, 0:Ti], start=True,
                              stop=True).then_inc(tile_ready, 1)
                    bank = open_tile(f"{L}rx{i}")
                    pe.wait_ge(freed["dve"], plan.freed[f"{L}raw{i}"][1])
                    src = b["MQ"][0:MLA_QK, i, 0:S] if i < MLA_H else b["MK"][0:MLA_QK, i - MLA_H, 0:S]
                    pe.matmul(bank[0:MLA_QK, 0:S], ROT, src, start=True, stop=True).then_inc(tile_ready, 1)
                c["ml"] += 2 * MLA_H
                for j in range(4):
                    bank = open_tile(f"{L}mv{j}")
                    pe.matmul(bank, b["CKV"][:, 0, j * P:j * P + P],
                              Wk[:, 0, MLA_H * MLA_QK:MLA_H * MLA_QK + 512], start=True, stop=True
                              ).then_inc(tile_ready, 1)
                next_phase()
                attention(mla_units(l))
                next_phase()
                merge(L, 3, T)
                project_out(L, T)
                norm_sums(f"{L}n2", KD, ns(T, NS2), T)
                h_ready(T // S)

                def up(g):
                    if g == 0:
                        fm3_first([f"{L}up{j}" for j in range(FIRST)], T)
                    for j in range(0 if g else FIRST, GT):
                        fm3(f"{L}up{g * GT + j}", T)

                def down_group(g):
                    pe.wait_ge(hid_ready, FFN // P * l + GT * g + GT)
                    for j in range(KD):
                        fm3(f"{L}down{g}_{j}", T, lambda k: hidden(g, k, T))
                for g in range(GROUPS_F):
                    up(g)
                    if g:
                        down_group(g - 1)
                down_group(GROUPS_F - 1)
            next_phase()

        @block.scalar
        def _(act):
            ph = [0]
            c = dict(step=0, squares=0, rstd=0, hn=0, hnr=0, ml=0, unit=0, gate=0, x=0, chunk=0, scaled=0, merged=0)

            def next_phase():
                ph[0] += 1
                act.drain().then_inc(phase["act"], 1)
                for e in ("pe", "dve"):
                    act.wait_ge(phase[e], ph[0])

            def step(ins):
                c["step"] += 1
                ins.then_inc(act_step, 1)
                act.wait_ge(act_step, c["step"])

            def split(name):
                while c["chunk"] < plan.split_by[plan.tile_at[name]]:
                    i = c["chunk"]
                    c["chunk"] += 1
                    b = plan.chunks[i][0]
                    act.wait_ge(landed[b % RING], 16 * (b // RING + 1))
                    if i >= BUFS:
                        kind, count = plan.chunk_end[i - BUFS]
                        act.wait_ge(tile_ready if kind == "tile" else part_used, count)
                    src, hi, _ = chunk_views(i)
                    act.activation(hi, src, ACT.Copy).then_inc(hi_done, 1)

            def bank(name):
                split(name)
                act.wait_ge(tile_ready, plan.tile_at[name] + 1)
                return bank_of(name)

            def inverse_root(name, r, inv, T, M=P):
                act.activation(r, bank(name)[0:M, 0:T], ACT.Ln, bias=VEC[0:M, 0:1], scale=inv
                               ).then_inc(freed["act"], 1)
                act.wait_ge(freed["act"], plan.freed[name][1])
                return act.activation(r, r, ACT.Exp, scale=-0.5)

            def ln_exp():
                act.preload_act_table_set("natural_log_exp_and_others")

            def norm(tile, n, src, sq, T, inv, x_tiles=None, r=0):
                ln_exp()
                for k in range(n):
                    if x_tiles:
                        split(x_tiles(k))
                        c["x"] += 1
                        act.wait_ge(x_ready, c["x"])
                    act.activation(sq(k), src(k), ACT.Square).then_inc(squares, 1)
                inverse_root(tile, R[:, r, 0:T], inv, T).then_inc(rstd, 1)

            def norm_high(T, shift=None, where=NS):
                for k in range(KD):
                    for st in range(T // S):
                        at = slice(st * S, st * S + S)
                        c["scaled"] += 1
                        act.wait_ge(scaled, c["scaled"])
                        if shift is None:
                            act.activation(HH[:, k, at], where[:, k, at], ACT.Copy).then_inc(norm_hi, 1)
                        else:
                            act.activation(HH[:, k, at], where[:, k, at], ACT.Identity, bias=shift(st, k)
                                           ).then_inc(norm_hi, 1)

            def evacuate(name, dst, func=ACT.Copy, M=P, T=512):
                act.activation(dst, bank(name)[0:M, 0:T], func).then_inc(freed["act"], 1)

            def attention(units):
                u0 = c["unit"]
                c["unit"] += len(units)
                ln_exp()

                def expo(u):
                    g, x = u0 + u, units[u]
                    act.wait_ge(negmax, g + 1)
                    if g >= N_P:
                        act.wait_ge(pt_ready, g - N_P + 1)
                    nm = NM[:, g % N_P:g % N_P + 1]
                    if x["sink"] is not None:
                        act.activation(ESINK[:, g % N_P:g % N_P + 1], x["sink"], ACT.Exp, bias=nm)
                    act.activation(PROB[:, g % N_P, 0:x["nk"]], att_bank("S", g)[:, 0:x["nk"]], ACT.Exp, bias=nm,
                                   accum_out=SUM[:, g % N_P:g % N_P + 1]).then_inc(exp_done, 1)

                def copy_turned(u):
                    g, x = u0 + u, units[u]
                    act.wait_ge(pt_ready, g + 1)
                    if g >= 2:
                        act.wait_ge(o_ready, g - 1)
                    act.activation(PT[:, g % 2, 0:x["nk"]], att_bank("T", g)[:, 0:x["nk"]], ACT.Copy
                                   ).then_inc(pt_copied, 1)

                def store(u):
                    g, x = u0 + u, units[u]
                    act.wait_ge(o_ready, g + 1)
                    act.activation(x["out"], att_bank("O", g)[x["lo"]:x["lo"] + 64, 0:P], ACT.Copy
                                   ).then_inc(o_stored, 1)
                for u in range(AHEAD - 1):
                    expo(u)
                for u in range(len(units)):
                    copy_turned(u)
                    if u + AHEAD - 1 < len(units):
                        expo(u + AHEAD - 1)
                    if u:
                        store(u - 1)
                store(len(units) - 1)

            def merge(L, ys, Y, T):
                n = len(ys)

                def merged_high(k):
                    c["merged"] += 1
                    act.wait_ge(merged, c["merged"])
                    act.activation(merged_parts(k, T)[0], Y[:, k, 0:T], ACT.Copy).then_inc(merged_hi, 1)
                for b in range(n):
                    for hf in range(2):
                        for j in range(4):
                            split(f"{L}gate{b}{hf}{j}")
                            if hf == 0:
                                if L == "A" and b == 0:
                                    act.wait_ge(ret_done, j + 1)
                                act.activation(branch_parts(b, T)[0][:, j, :], ys[b][:, j, 0:T], ACT.Copy
                                               ).then_inc(branch_hi, 1)
                            if b or hf:
                                prev = f"{L}o{b if hf else b - 1}{1 - hf}{j}"
                                act.wait_ge(freed["dve"], plan.freed[prev][1])
                            evacuate(f"{L}gate{b}{hf}{j}", SG[:, j, 0:T], ACT.Sigmoid, T=T)
                            if b == n - 1 and hf:
                                merged_high(j)
                for j in range(4):
                    split(f"{L}o{n - 1}1{j}")
                    merged_high(4 + j)

            act.wait_ge(loaded_x, 48)
            norm("n_mix", KD, lambda k: X[:, k, 0:S], lambda k: NS[:, k, 0:S], S, 1.0 / D)
            norm_high(S)
            for j in range(4):
                evacuate(f"sq{j}", QK[:, j, :], T=S)
            for j in range(SWA_KV):
                evacuate(f"sk{j}", QK[:, 4 + j, :], T=S)
            for j in range(ST):
                evacuate(f"sv{j}", SV[:, j, :], T=P)
            act.wait_ge(freed["act"], plan.freed[f"sk{SWA_KV - 1}"][1])
            qk = QK.rearrange("p j n -> p (j n)")
            for j in range(4):
                if j < 3:
                    act.activation(SQ[:, j % 2, :], qk[:, j * 512:j * 512 + 512], ACT.Square).then_inc(hn_sq, 1)
                evacuate(f"rq{j}", RQ[:, j, :], T=S)
                if j < 3:
                    if j == 2:
                        act.wait_ge(hn_done, 1)
                    inverse_root(f"hn1_{j}", R[:, 1 - j % 2, :], 1.0 / 64, 512).then_inc(hn_rstd, 1)
            c["hn"] = 3
            for j in range(4):
                evacuate(f"rk{j}", RK[:, j, :], T=S)
            for j in range(ST):
                evacuate(f"rv{j}", RV[:, j, :])
            for j in range(4):
                evacuate(f"rg{j}", RG[:, j, :], ACT.Silu, T=S)
            next_phase()
            ln_exp()
            for hd in range(RET_H):
                act.activation(YR[:, hd, :], bank(f"ret_y{hd}")[:, 0:S], ACT.Copy).then_inc(freed["act"], 1)
            act.drain().then_inc(evac, 1)
            yr = YR.rearrange("p h n -> p (h n)")
            for j in range(2):
                act.wait_ge(centred, j + 1)
                act.activation(SQ[:, j, :], yr[:, j * 512:j * 512 + 512], ACT.Square).then_inc(varsq, 1)
            for j in range(2):
                inverse_root(f"ret_var{j}", R[:, j, :], 1.0 / RET_D, 512).then_inc(rstd, 1)
            next_phase()
            attention(swa_units())
            next_phase()
            merge("A", [YR, YS], BR[:, 0:KD * S].rearrange("p (k n) -> p k n", k=KD), S)
            norm("n_ffn", KD, lambda k: X[:, k, 0:S], lambda k: NS2[:, k, 0:S], S, 1.0 / D, lambda k: f"Aout{k}")
            norm_high(S, where=NS2)

            def moe_high(which, count, c_, q_mod, free):
                act.wait_ge(moe_landed[which], count)
                if free is not None:
                    act.wait_ge(moe_used, free)
                src, hi, _ = moe_chunk(q_mod, c_)
                act.activation(hi, src, ACT.Copy).then_inc(moe_hi, 1)
            split("router1")
            act.wait_ge(tile_ready, plan.tile_at["router1"] + 1)
            for q in range(3):
                moe_high(("gate", "up")[q // 2], 16, q, q, None)
            for j in range(ST):
                r = TMP[:, 1, j * S:j * S + S]
                act.wait_ge(router_group, j + 1)
                act.activation(r[:, 44:48], r[:, 40:44], ACT.Exp, accum_out=r[:, 48:49]).then_inc(router_exp, 1)
                act.wait_ge(router_top, j + 1)
                act.activation(r[:, 107:108], r[:, 106:107], ACT.Exp).then_inc(router_exp, 1)
                if j == 0:
                    moe_high("up", 16, 3, 3, 1)
            act.wait_ge(comb_turned, 1)
            act.activation(CT, PS[0:N_EXP, 4, 0:S], ACT.Copy).then_inc(comb_t, 1)
            act.wait_ge(loaded_in, 16 * 7)
            act.activation(SC, SC, ACT.Silu).then_inc(silu_c, 1)

            def hidden_silu(x, used):
                wait_after(act, moe_used, used)
                act.activation(SGM[:, x, :], PS[:, GU_BANKS[x][0], :], ACT.Silu).then_inc(moe_silu, 1)

            def hidden_high(x, count):
                act.wait_ge(moe_weighed, count)
                act.activation(HIDH[:, x, :], SGM[:, x, :], ACT.Copy).then_inc(moe_hid_hi, 1)

            def expert(x):
                j = 1 - x.j
                hidden_silu(j, x.at(6, -6))
                for q in range(2):
                    moe_high("gate", x.at(16, 16), q, 4 + q, x.at(6, q - 4))
                for q in range(2, 4):
                    moe_high("up", x.at(16, 16), q, 4 + q, x.at(6, q - 4))
                    if q == 2:
                        hidden_high(j, x.at(1))
                for q in range(4, 6):
                    moe_high("down", x.at(16), q, 4 + q, x.at(6, q - 4))
            experts(act, expert)
            j = (N_EXP - 1) % 2
            hidden_silu(j, 6 * N_EXP - 4)
            hidden_high(j, N_EXP)
            for q in range(4, 6):
                moe_high("down", 16 * N_EXP, q, MOE_CHUNKS - 6 + q, MOE_CHUNKS - 8 + q)
            act.wait_ge(moe_hid, N_EXP)
            act.wait_ge(moe_used, MOE_CHUNKS)
            for j in range(8):
                evacuate(f"ple{j}", PL[:, j, :], T=S)
            norm("n_pleg", KD, lambda k: X[:, k, 0:S], lambda k: NS[:, k, 0:S], S, 1.0 / D, lambda k: "ple7")
            norm_high(S)
            act.wait_ge(freed["act"], plan.freed["ple7"][1])
            for k in range(KD):
                act.activation(PLSQ[:, k, :], PL[:, k, :], ACT.Square).then_inc(squares, 1)
            for j in range(8):
                if j == 2:
                    ln_exp()
                    inverse_root("n_ple", R[:, 1, 0:S], 1.0 / D, S).then_inc(rstd, 1)
                name = f"pleg{j}"
                split(name)
                if j >= 4:
                    act.wait_ge(gate_used, j - 3)
                evacuate(name, SG[:, j % 4, 0:S], ACT.Sigmoid, T=S)

            for l in range(2):
                L, b = f"B{l}", lens(l)
                T = b["T"]
                norm(f"{L}n1", KD, lambda k: X[:, k, :], lambda k: NS[:, k, :], 512, 1.0 / D,
                     lambda k: f"pleg{k}" if l == 0 else f"B0down{GROUPS_F - 1}_{k}")
                norm_high(512, lambda st, k: MOD[:, l, k, st:st + 1])
                items, h0 = norm_items(l), c["hn"]

                def square_items(i):
                    for x, sq in zip(items[i][0], items[i][1]):
                        act.activation(sq, x, ACT.Square).then_inc(hn_sq, 1)

                def project(name, dst, T, n=4, func=ACT.Copy):
                    behind = norms_behind(l, name) if name in ("q", "cq", "u") else {}
                    for j in range(n):
                        norms = [int(tile[6:]) for tile, _ in behind.get(j, [])]
                        for i in norms:
                            square_items(i)
                        evacuate(f"{L}{name}{j}", dst[:, j, :], func, T=T)
                        for i in norms:
                            T_i = items[i][1][0].shape[-1]
                            if i >= 2:
                                act.wait_ge(hn_done, h0 + i - 1)
                            ln_exp()
                            inverse_root(f"{L}norm{i}", R[:, 1 - i % 2, 0:T_i], items[i][3], T_i
                                         ).then_inc(hn_rstd, 1)
                project("k", b["NK"], 512)
                act.wait_ge(freed["act"], plan.freed[L + "k3"][1])
                project("q", b["NQ"], T)
                act.wait_ge(freed["act"], plan.freed[f"{L}norm3"][1])
                project("cq", b["CQ"], T, 2)
                evacuate(L + "ckv0", b["CKV"][:, 0, :])
                evacuate(L + "kr0", b["KR"], M=MLA_ROPE)
                for j in range(T // P):
                    evacuate(f"{L}gv{j}", b["GV"][:, j, :], ACT.Gelu)
                for j in range(4):
                    evacuate(f"{L}v{j}", b["NV"][:, j, :])
                ln_exp()
                act.wait_ge(gv_stats, l + 1)
                mv = SM[:, 40:40 + 2 * (T // P)].rearrange("p (t s) -> p t s", s=2)[:, :, 1]
                rs = SM[:, 56:56 + T // P]
                step(act.activation(rs, mv, ACT.Ln, bias=EPS_COL))
                act.activation(rs, rs, ACT.Exp, scale=-0.5).then_inc(gv_rstd, 1)
                act.wait_ge(freed["act"], plan.freed[L + "v3"][1])
                project("u", b["U"], T, func=ACT.Gelu)
                c["hn"] += len(items)
                next_phase()
                attention(na_units(l))
                next_phase()
                ln_exp()

                def square(i):
                    Ti = T if i < MLA_H else 512
                    act.activation(SQ[0:MLA_QK, i % 2, 0:Ti], bank(f"{L}raw{i}")[0:MLA_QK, 0:Ti], ACT.Square
                                   ).then_inc(ml_sq, 1)
                square(0)
                for i in range(2 * MLA_H):
                    if i + 1 < 2 * MLA_H:
                        square(i + 1)
                    Ti = T if i < MLA_H else 512
                    if i >= 2:
                        act.wait_ge(ml_done, c["ml"] + i - 1)
                    inverse_root(f"{L}ss{i}", R[0:MLA_QK, i % 2, 0:Ti], 1.0 / MLA_QK, Ti, MLA_QK
                                 ).then_inc(ml_rstd, 1)
                c["ml"] += 2 * MLA_H
                for j in range(4):
                    evacuate(f"{L}mv{j}", b["MV"][:, j, :])
                next_phase()
                attention(mla_units(l))
                next_phase()
                merge(L, [b["YN"], b["U"], b["YM"]], b["Y"], T)
                norm(f"{L}n2", KD, lambda k: X[:, k, 0:T], lambda k: NS2[:, k, 0:T], T, 1.0 / D,
                     lambda k: f"{L}out{k}")
                norm_high(T, lambda st, k: MOD[:, l, 24 + k, st:st + 1], NS2)
                if l == 0:
                    act.wait_ge(c_again, 16)
                    act.activation(SC2, SC2, ACT.Silu).then_inc(silu_again, 1)

                def up(g):
                    for j in range(GT):
                        name = f"{L}up{g * GT + j}"
                        split(name)
                        n = FFN // P * l + g * GT + j
                        if g * GT + j >= 2:
                            act.wait_ge(hid_ready, n - 1)
                        relu = TMP[:, j % 2, 0:T]
                        evacuate(name, relu, ACT.Relu, T=T)
                        act.wait_ge(freed["act"], plan.freed[name][1])
                        act.activation(hidden(g, j, T)[0], relu, ACT.Square).then_inc(hid_hi, 1)

                def down(g):
                    for j in range(KD):
                        split(f"{L}down{g}_{j}")
                for g in range(GROUPS_F):
                    up(g)
                    if g:
                        down(g - 1)
                if l:
                    down(GROUPS_F - 1)
            next_phase()

        @block.vector
        def _(dve):
            ph = [0]
            c = dict(step=0, rstd=0, scaled=0, hn=0, ml=0, unit=0, merged=0, merged_hi=0, branch=0, normed=0, x=0, chunk=0, nh=0, mod2=0)

            def next_phase():
                ph[0] += 1
                dve.drain().then_inc(phase["dve"], 1)
                for e in ("pe", "act"):
                    dve.wait_ge(phase[e], ph[0])

            def step(ins):
                c["step"] += 1
                ins.then_inc(dve_step, 1)
                dve.wait_ge(dve_step, c["step"])

            def split(name):
                while c["chunk"] < plan.split_by[plan.tile_at[name]]:
                    c["chunk"] += 1
                    dve.wait_ge(hi_done, c["chunk"])
                    src, hi, lo = chunk_views(c["chunk"] - 1)
                    dve.tensor_tensor(lo, src, hi, ALU.subtract).then_inc(lo_done, 1)

            def bank(name):
                split(name)
                dve.wait_ge(tile_ready, plan.tile_at[name] + 1)
                return bank_of(name)

            def own(name):
                dve.wait_ge(freed["dve"], plan.freed[name][1])

            def wait_rstd(n=1):
                c["rstd"] += n
                dve.wait_ge(rstd, c["rstd"])

            def norm(n, src, dst, T, gain, r=0):
                wait_rstd()
                for k in range(n):
                    dve.scalar_tensor_tensor(out=dst(k), in0=src(k), scalar=gain(k), in1=R[:, r, 0:T],
                                             op0=ALU.mult, op1=ALU.mult).then_inc(normed, 1)
                c["normed"] += n

            def norm_split(T, gain, shift=None, where=NS):
                wait_rstd()
                parts = [(st, k) for k in range(KD) for st in range(T // S)]

                def scale(st, k):
                    at = slice(st * S, st * S + S)
                    dve.scalar_tensor_tensor(out=where[:, k, at], in0=X[:, k, at], scalar=gain(st, k), in1=R[:, 0, at],
                                             op0=ALU.mult, op1=ALU.mult).then_inc(scaled, 1)

                def rest(st, k):
                    at = slice(st * S, st * S + S)
                    c["nh"] += 1
                    dve.wait_ge(norm_hi, c["nh"])
                    if shift is None:
                        ins = dve.tensor_tensor(HL[:, k, at], where[:, k, at], HH[:, k, at], ALU.subtract)
                    else:
                        ins = dve.scalar_tensor_tensor(out=HL[:, k, at], in0=where[:, k, at], scalar=shift(st, k),
                                                       in1=HH[:, k, at], op0=ALU.add, op1=ALU.subtract)
                    ins.then_inc(normed, 1)
                for i, part in enumerate(parts):
                    scale(*part)
                    if i >= 2:
                        rest(*parts[i - 2])
                for part in parts[-2:]:
                    rest(*part)
                c["normed"] += len(parts)

            def norm_modulated(T, n, l, shift_tile, where=NS):
                norm_split(T, lambda st, k: MA[:, n, st, k:k + 1],
                           lambda st, k: MOD[:, l, shift_tile + k, st:st + 1], where)

            def attention(units):
                u0 = c["unit"]
                c["unit"] += len(units)

                def maxima(u):
                    g, x = u0 + u, units[u]
                    s = att_bank("S", g)[:, 0:x["nk"]]
                    m, nm = MX[:, g % N_P:g % N_P + 1], NM[:, g % N_P:g % N_P + 1]
                    dve.wait_ge(scores_ready, g + 1)
                    if x["sink"] is None:
                        dve.tensor_reduce(nm, s, AX.X, ALU.max, negate=True).then_inc(negmax, 1)
                        return
                    step(dve.tensor_reduce(m, s, AX.X, ALU.max))
                    dve.tensor_scalar(nm, m, x["sink"], -1.0, ALU.max, ALU.mult).then_inc(negmax, 1)

                def normalise(u):
                    g, x = u0 + u, units[u]
                    r = RIN[:, g % N_P:g % N_P + 1]
                    total = SUM[:, g % N_P:g % N_P + 1]
                    dve.wait_ge(exp_done, g + 1)
                    if x["sink"] is not None:
                        step(dve.tensor_tensor(total, total, ESINK[:, g % N_P:g % N_P + 1], ALU.add))
                    step(dve.reciprocal(r, total))
                    dve.tensor_scalar(PROB[:, g % N_P, 0:x["nk"]], PROB[:, g % N_P, 0:x["nk"]], r, None, ALU.mult
                                      ).then_inc(probs, 1)

                for u in range(AHEAD):
                    maxima(u)
                normalise(0)
                for u in range(len(units)):
                    if u + 1 < len(units):
                        normalise(u + 1)
                    if u + AHEAD < len(units):
                        maxima(u + AHEAD)

            def merge(L, ys, Y, T):
                n = len(ys)

                def merged_rest(k):
                    c["merged_hi"] += 1
                    dve.wait_ge(merged_hi, c["merged_hi"])
                    hi, lo = merged_parts(k, T)
                    dve.tensor_tensor(lo, Y[:, k, 0:T], hi, ALU.subtract).then_inc(merged_split, 1)
                for b in range(n):
                    for j in range(4):
                        split(f"{L}gate{b}0{j}")
                        c["branch"] += 1
                        dve.wait_ge(branch_hi, c["branch"])
                        hi, lo = branch_parts(b, T)
                        dve.tensor_tensor(lo[:, j, :], ys[b][:, j, 0:T], hi[:, j, :], ALU.subtract
                                          ).then_inc(branch_split, 1)
                    for hf in range(2):
                        for j in range(4):
                            name = f"{L}o{b}{hf}{j}"
                            gate = f"{L}gate{b}{hf}{j}"
                            split(name)
                            dve.wait_ge(freed["act"], plan.freed[gate][1])
                            ps, y = bank(name)[:, 0:T], Y[:, hf * 4 + j, 0:T]
                            dst = y if b == 0 else TMP[:, j % 2, 0:T]
                            dve.tensor_tensor(dst, SG[:, j, 0:T], ps, ALU.mult).then_inc(freed["dve"], 1)
                            own(name)
                            if b:
                                ins = dve.tensor_tensor(y, y, TMP[:, j % 2, 0:T], ALU.add)
                                if b == n - 1:
                                    c["merged"] += 1
                                    ins.then_inc(merged, 1)
                                    dve.wait_ge(merged, c["merged"])
                                    if hf:
                                        merged_rest(j)
                                else:
                                    step(ins)
                for j in range(4):
                    merged_rest(4 + j)

            def route(j):
                r = TMP[:, 1, j * S:j * S + S]
                at = VEC_AT["priority"][0]
                pri8, pri4 = VEC[:, at:at + 8], VEC[:, at + 4:at + 8]
                name = f"router{j}"
                dve.tensor_copy(r[:, 0:36], bank(name)[:, 0:36]).then_inc(freed["dve"], 1)
                own(name)
                col = {n: r[:, i:i + 1] for n, i in dict(gmax=49, gw=50, best=51, m1=104, m2=105, dist=106,
                                                         ratio=107, s=108, w1=110, w2=111).items()}

                def first_of_max(out, v, m, pri, tmp):
                    step(dve.tensor_reduce(m, v, AX.X, ALU.max))
                    step(dve.scalar_tensor_tensor(out=tmp, in0=v, scalar=m, in1=pri, op0=ALU.is_equal, op1=ALU.mult))
                    step(dve.tensor_reduce(col["best"], tmp, AX.X, ALU.max))
                    step(dve.tensor_scalar(out, tmp, col["best"], None, ALU.is_equal))
                first_of_max(r[:, 52:56], r[:, 0:4], col["gmax"], pri4, r[:, 56:60])
                dve.tensor_scalar(r[:, 40:44], r[:, 0:4], col["gmax"], None, ALU.subtract).then_inc(router_group, 1)
                e8 = r[:, 64:72]
                step(dve.tensor_scalar(e8, r[:, 4:12], r[:, 52:53], None, ALU.mult))
                for g in range(1, N_GROUPS):
                    step(dve.scalar_tensor_tensor(out=e8, in0=r[:, 4 + 8 * g:12 + 8 * g], scalar=r[:, 52 + g:53 + g],
                                                  in1=e8, op0=ALU.mult, op1=ALU.add))
                oh1, oh2 = r[:, 80:88], r[:, 88:96]
                first_of_max(oh1, e8, col["m1"], pri8, r[:, 72:80])
                step(dve.scalar_tensor_tensor(out=r[:, 96:104], in0=oh1, scalar=NEG, in1=e8, op0=ALU.mult, op1=ALU.add))
                first_of_max(oh2, r[:, 96:104], col["m2"], pri8, r[:, 72:80])
                dve.tensor_tensor(col["dist"], col["m2"], col["m1"], ALU.subtract).then_inc(router_top, 1)
                dve.wait_ge(router_exp, 2 * j + 2)
                step(dve.reciprocal(col["gw"], r[:, 48:49]))
                step(dve.tensor_scalar(col["s"], col["ratio"], 1.0, None, ALU.add))
                step(dve.reciprocal(col["s"], col["s"]))
                step(dve.tensor_tensor(col["w1"], col["s"], col["gw"], ALU.mult))
                step(dve.tensor_tensor(col["w2"], col["w1"], col["ratio"], ALU.mult))
                c8 = r[:, 112:120]
                step(dve.tensor_scalar(c8, oh1, col["w1"], None, ALU.mult))
                step(dve.scalar_tensor_tensor(out=c8, in0=oh2, scalar=col["w2"], in1=c8, op0=ALU.mult, op1=ALU.add))
                for g in range(N_GROUPS):
                    ins = dve.tensor_scalar(SM[:, 64 + 32 * j + 8 * g:72 + 32 * j + 8 * g], c8, r[:, 52 + g:53 + g],
                                            None, ALU.mult)
                ins.then_inc(combined, 1)

            dve.wait_ge(loaded_x, 48)
            for name, dim in (("qn_g", SWA_D), ("naq_0", NA_D), ("naq_1", NA_D), ("mq_0", MLA_QK), ("mq_1", MLA_QK)):
                step(dve.tensor_scalar(vec(name), vec(name), dim ** -0.5, None, ALU.mult))
            split("n_mix")
            norm_split(S, lambda st, k: vec("mix_g", k))
            for j in range(4):
                split(f"sq{j}")
            for j in range(SWA_KV):
                split(f"sk{j}")
            for j in range(ST):
                split(f"sv{j}")
            qk = QK.rearrange("p j n -> p (j n)")
            for i in range(3):
                split(f"hn1_{i}")
                dve.wait_ge(hn_rstd, i + 1)
                x = qk[:, i * 512:i * 512 + 512]
                dve.scalar_tensor_tensor(out=x, in0=x, scalar=vec("qn_g" if i < 2 else "kn_g"), in1=R[:, 1 - i % 2, :],
                                         op0=ALU.mult, op1=ALU.mult).then_inc(hn_done, 1)
            c["hn"] = 3
            for name in four("rq") + four("rk") + ["rv0", "rv1"] + four("rg"):
                split(name)
            next_phase()
            dve.wait_ge(loaded_in, 16 * 7)
            for hd in range(RET_H):
                name = f"ret_s{hd}"
                ps = bank(name)
                if hd >= 2:
                    dve.wait_ge(tile_ready, plan.tile_at[f"ret_y{hd - 2}"] + 1)
                dve.tensor_tensor(RSM[:, hd % 2, :], BRET[:, hd, :], ps[:, 0:384], ALU.mult).then_inc(masked, 1)
                dve.wait_ge(masked, hd + 1)
                dve.nop().then_inc(freed["dve"], 1)
            yr = YR.rearrange("p h n -> p (h n)")
            for j in range(2):
                name = f"ret_mean{j}"
                at = slice(j * 512, j * 512 + 512)
                dve.scalar_tensor_tensor(out=yr[:, at], in0=bank(name), scalar=-1.0 / RET_D, in1=yr[:, at],
                                         op0=ALU.mult, op1=ALU.add).then_inc(freed["dve"], 1)
                own(name)
                dve.nop().then_inc(centred, 1)
            next_phase()
            attention(swa_units())
            next_phase()
            split("Agate000")
            wait_rstd(2)
            for hd in range(RET_H):
                r = R[:, hd // 2, (hd % 2) * S:(hd % 2) * S + S]
                step(dve.scalar_tensor_tensor(out=YR[:, hd, :], in0=YR[:, hd, :], scalar=vec("ret_g", hd), in1=r,
                                              op0=ALU.mult, op1=ALU.mult))
                dve.scalar_tensor_tensor(out=YR[:, hd, :], in0=YR[:, hd, :], scalar=vec("ret_b", hd),
                                         in1=RG[:, hd, :], op0=ALU.add, op1=ALU.mult).then_inc(ret_done, 1)
            YA = BR[:, 0:KD * S].rearrange("p (k n) -> p k n", k=KD)
            merge("A", [YR, YS], YA, S)
            for j in range(KD):
                name = f"Aout{j}"
                dve.tensor_tensor(X[:, j, 0:S], X[:, j, 0:S], bank(name)[:, 0:S], ALU.add).then_inc(freed["dve"], 1)
                own(name)
                c["x"] += 1
                dve.nop().then_inc(x_ready, 1)
            split("n_ffn")
            norm_split(S, lambda st, k: vec("ffn_g", k), where=NS2)
            step(dve.memset(TMP[:, 0, :], 0.0))

            def moe_rest(count, c_, q_mod):
                dve.wait_ge(moe_hi, count)
                src, hi, lo = moe_chunk(q_mod, c_)
                dve.tensor_tensor(lo, src, hi, ALU.subtract).then_inc(moe_lo, 1)
            split("router1")
            for q in range(3):
                moe_rest(q + 1, q, q)
            route(0)
            moe_rest(4, 3, 3)
            route(1)

            def weigh(x, e):
                sg = SGM[:, x, :]
                dve.tensor_tensor(sg, sg, PS[:, GU_BANKS[x][1], :], ALU.mult).then_inc(moe_mul, 1)
                dve.wait_ge(moe_mul, e(1))
                sg = sg.rearrange("p (f n) -> p f n", f=FT)
                row = A[:, bass.ds(e(0) * S, S)]
                for f in range(FT):
                    ins = dve.tensor_tensor(sg[:, f, :], sg[:, f, :], row, ALU.mult)
                ins.then_inc(moe_weighed, 1)

            def hidden_rest(x, count):
                dve.wait_ge(moe_hid_hi, count)
                dve.tensor_tensor(HIDL[:, x, :], SGM[:, x, :], HIDH[:, x, :], ALU.subtract).then_inc(moe_hid, 1)

            def modulation(r, landed_count, steps):
                m, st = r // 2, r % 2
                if st == 0:
                    dve.wait_ge(mw_landed[m], landed_count)
                wait_after(dve, mod_step, steps)
                dve.tensor_tensor_reduce(out=JUNK[:, :], in0=MW[:, m, :], in1=SC[:, st, :], scale=1.0, scalar=0.0,
                                         op0=ALU.mult, op1=ALU.add, accum_out=MR[:, r:r + 1]).then_inc(mod_step, 1)

            def modulated(e, steps):
                dve.wait_ge(mod_step, steps)
                for st in range(2):
                    dst = MOD_FLAT[:, bass.ds(e * (2 * MT), 2 * MT)].rearrange("p (m s) -> p m s", s=2)[:, :, st]
                    src = MR.rearrange("p (m s) -> p m s", s=2)[:, :, st]
                    ins = dve.tensor_tensor(dst, src, BMOD[:, bass.ds(e * MT, MT)], ALU.add)
                ins.then_inc(mod_acc, 1)

            dve.wait_ge(silu_c, 1)

            def expert(x):
                j = 1 - x.j
                for q in range(6):
                    moe_rest(x.at(6, q - 1), q, 4 + q)
                    if q == 0 and x.j == 1:
                        wait_after(dve, mod_acc, x.pair(1))
                    if q == 1:
                        if x.i is None and x.base == 1:
                            dve.wait_ge(comb_in[0], 16)
                        dve.wait_ge(moe_silu, x.at(1))
                        dve.wait_ge(moe_used, x.at(6, -4))
                        weigh(j, lambda n: x.at(1, n - 1) if n == 0 else x.at(1))
                    if q == 2:
                        hidden_rest(j, x.at(1))
                    last = x.i is None and x.base == N_EXP - 1
                    if last or q % 2 == 0:
                        r = q if last else q // 2 + (0 if x.j else 3)
                        modulation(r, x.pair(16, 16), x.pair(2 * MT, r))
                if last or x.j == 0:
                    modulated(x.pair(1), x.pair(2 * MT, 2 * MT))
                if x.i is None and x.base == 2:
                    dve.wait_ge(comb_in[1], 16)
            experts(dve, expert)
            j = (N_EXP - 1) % 2
            dve.wait_ge(moe_silu, N_EXP)
            dve.wait_ge(moe_used, 6 * N_EXP - 2)
            weigh(j, lambda n: N_EXP - 1 if n == 0 else N_EXP)
            hidden_rest(j, N_EXP)
            for q in range(4, 6):
                moe_rest(MOE_CHUNKS - 5 + q, q, MOE_CHUNKS - 6 + q)
            dve.wait_ge(mod_acc, N_EXP // 2)
            dve.wait_ge(moe_used, MOE_CHUNKS)
            for d in range(KD):
                y = PS[:, 4 + d // 2, (d % 2) * S:(d % 2) * S + S]
                dve.tensor_tensor(X[:, d, 0:S], X[:, d, 0:S], y, ALU.add).then_inc(x_ready, 1)
            c["x"] += KD
            dve.wait_ge(x_ready, c["x"])
            split("n_pleg")
            norm_split(S, lambda st, k: vec("pleg_g", k))
            split("n_ple")
            norm(KD, lambda k: PL[:, k, :], lambda k: PL[:, k, :], S, lambda k: vec("ple_g", k), r=1)
            dve.wait_ge(normed, c["normed"])
            for j in range(KD):
                split(f"pleg{j}")
                dve.wait_ge(freed["act"], plan.freed[f"pleg{j}"][1])
                dve.tensor_tensor(TMP[:, j % 2, 0:S], SG[:, j % 4, 0:S], PL[:, j, :], ALU.mult).then_inc(gate_used, 1)
                dve.wait_ge(gate_used, j + 1)
                dve.tensor_tensor(X[:, j, 0:S], X[:, j, 0:S], TMP[:, j % 2, 0:S], ALU.add).then_inc(x_ready, 1)
                c["x"] += 1
                dve.wait_ge(x_ready, c["x"])

            def gains(l):
                for n, (g, tile) in enumerate(((f"g1_{l}", 8), (f"g2_{l}", 32))):
                    at = VEC_AT[g][0]
                    for s in range(2 if n == 0 or l == 0 else 1):
                        step(dve.scalar_tensor_tensor(out=MA[:, n, s, :], in0=MOD[:, l, tile:tile + KD, s], scalar=1.0,
                                                      in1=VEC[:, at:at + KD], op0=ALU.add, op1=ALU.mult))
            gains(0)

            for l in range(2):
                L, b = f"B{l}", lens(l)
                T = b["T"]

                def residual(name, j, tile, last=True):
                    for s in range(T // S):
                        at = slice(s * S, s * S + S)
                        ins = dve.scalar_tensor_tensor(out=X[:, j, at], in0=bank(name)[:, at],
                                                       scalar=MOD[:, l, tile + j, s:s + 1], in1=X[:, j, at],
                                                       op0=ALU.mult, op1=ALU.add)
                        if s < T // S - 1:
                            step(ins)
                    ins.then_inc(freed["dve"], 1)
                    if last:
                        own(name)
                        c["x"] += 1
                        dve.nop().then_inc(x_ready, 1)
                split(f"{L}n1")
                norm_modulated(512, 0, l, 0)
                items = norm_items(l)
                mv = SM[:, 40:40 + 2 * (T // P)].rearrange("p (t s) -> p t s", s=2)

                def project(name, n=4):
                    behind = norms_behind(l, name) if name in ("q", "cq", "u") else {}
                    for j in range(n):
                        split(f"{L}{name}{j}")
                        for tile, _ in behind.get(j, []):
                            i = int(tile[6:])
                            split(tile)
                            dve.wait_ge(hn_rstd, c["hn"] + 1)
                            for x, (gain, k) in zip(items[i][0], items[i][4]):
                                w = x.shape[-1]
                                ins = dve.scalar_tensor_tensor(out=x, in0=x, scalar=vec(gain, k),
                                                               in1=R[:, 1 - i % 2, 0:w], op0=ALU.mult, op1=ALU.mult)
                            ins.then_inc(hn_done, 1)
                            c["hn"] += 1
                project("k")
                project("q")
                project("cq", 2)
                project("ckv", 1)
                project("kr", 1)
                for q_ in range(T // P):
                    split(f"{L}gv{q_}")
                    dve.wait_ge(freed["act"], plan.freed[f"{L}gv{q_}"][1])
                    step(dve.bn_stats(SM[:, 192:198], b["GV"][:, q_, :]))
                    ins = dve.bn_aggr(mv[:, q_, :], SM[:, 192:198])
                    if q_ < T // P - 1:
                        step(ins)
                    else:
                        ins.then_inc(gv_stats, 1)
                for j in range(4):
                    split(f"{L}v{j}")
                if l:
                    dve.wait_ge(lc_loaded, 16)

                def gating_norm(q_):
                    v = b["GV"][:, q_, :]
                    step(dve.tensor_scalar(v, v, mv[:, q_, 0:1], SM[:, 56 + q_:57 + q_], ALU.subtract, ALU.mult))
                    step(dve.tensor_tensor(v, v, LC[:, LC_G:LC_G + 512], ALU.mult))
                    ins = dve.tensor_tensor(v, v, LC[:, LC_B:LC_B + 512], ALU.add)
                    if q_ < T // P - 1:
                        step(ins)
                    else:
                        ins.then_inc(gv_ready, 1)
                split(f"{L}u0")
                dve.wait_ge(gv_rstd, l + 1)
                for q_ in range(T // P):
                    gating_norm(q_)
                    if q_ == 1:
                        split(f"{L}u0")
                project("u")
                for j in range(4):
                    dve.wait_ge(freed["act"], plan.freed[f"{L}u{j}"][1])
                for q_ in range(T // P):
                    u = b["U"][:, :, q_ * P:q_ * P + P]
                    ps = bank(f"{L}mix{q_}").rearrange("p (g n) -> p g n", g=GM_G)
                    dve.tensor_tensor(u, u, ps, ALU.mult).then_inc(freed["dve"], 1)
                next_phase()
                attention(na_units(l))
                next_phase()

                def head(i):
                    return b["MQ"][0:MLA_QK, i, :] if i < MLA_H else b["MK"][0:MLA_QK, i - MLA_H, :]

                def scale(i):
                    Ti = T if i < MLA_H else 512
                    name = f"{L}raw{i}"
                    dve.wait_ge(ml_sq, c["ml"] + i + 1)
                    dve.tensor_scalar(head(i)[:, 0:Ti], bank(name)[0:MLA_QK, 0:Ti],
                                      vec(f"mq_{l}" if i < MLA_H else f"mk_{l}")[0:MLA_QK], None, ALU.mult
                                      ).then_inc(freed["dve"], 1)

                def rotate(i):
                    Ti = T if i < MLA_H else 512
                    name = f"{L}rx{i}"
                    own(f"{L}raw{i}")
                    tmp, x = TMP[0:MLA_QK, i % 2, 0:S], head(i)
                    dve.tensor_tensor(tmp, SIN, bank(name)[0:MLA_QK, 0:S], ALU.mult).then_inc(freed["dve"], 1)
                    own(name)
                    step(dve.tensor_tensor(x[:, 0:S], x[:, 0:S], COS, ALU.mult))
                    step(dve.tensor_tensor(x[:, 0:S], x[:, 0:S], tmp, ALU.add))
                    dve.wait_ge(ml_rstd, c["ml"] + i + 1)
                    dve.tensor_tensor(x[:, 0:Ti], x[:, 0:Ti], R[0:MLA_QK, i % 2, 0:Ti], ALU.mult).then_inc(ml_done, 1)
                scale(0)
                for i in range(2 * MLA_H):
                    if i + 1 < 2 * MLA_H:
                        scale(i + 1)
                    rotate(i)
                c["ml"] += 2 * MLA_H
                next_phase()
                attention(mla_units(l))
                next_phase()
                merge(L, [b["YN"], b["U"], b["YM"]], b["Y"], T)
                for j in range(KD):
                    residual(f"{L}out{j}", j, 16)
                split(f"{L}n2")
                norm_modulated(T, 1, l, 24, NS2)
                hid0 = FFN // P * l
                steps2 = [(n, st) for n in range(MOD_TILES) for st in range(2 if n < 2 * KD else 1)]

                def modulate_next():
                    if l or c["mod2"] == len(steps2):
                        return
                    n, st = steps2[c["mod2"]]
                    c["mod2"] += 1
                    if c["mod2"] == 1:
                        dve.wait_ge(silu_again, 1)
                    else:
                        dve.wait_ge(mod2_step, c["mod2"] - 1)
                    if st == 0:
                        dve.wait_ge(mw2_landed[n % 2], 16 * (n // 2 + 1))
                    dve.tensor_tensor_reduce(out=JUNK[:, :], in0=MW2[:, n % 2, :], in1=SC2[:, st, :], scale=1.0,
                                             scalar=0.0, op0=ALU.mult, op1=ALU.add,
                                             accum_out=MOD[:, 1, n, st:st + 1]).then_inc(mod2_step, 1)
                    if c["mod2"] == len(steps2) or steps2[c["mod2"]][0] > n:
                        dve.wait_ge(mod2_step, c["mod2"])
                        dve.nop().then_inc(mod2_used, 1)

                def up(g):
                    def rest(j):
                        dve.wait_ge(hid_sq, hid0 + g * GT + j + 1)
                        dve.wait_ge(hid_hi, hid0 + g * GT + j + 1)
                        hi, lo = hidden(g, j, T)
                        dve.tensor_tensor(lo, SQ[:, j % 2, 0:T], hi, ALU.subtract).then_inc(hid_ready, 1)
                    for j in range(GT):
                        name = f"{L}up{g * GT + j}"
                        split(name)
                        dve.wait_ge(freed["act"], plan.freed[name][1])
                        if g * GT + j >= 2:
                            dve.wait_ge(hid_ready, hid0 + g * GT + j - 1)
                        relu = TMP[:, j % 2, 0:T]
                        dve.tensor_tensor(SQ[:, j % 2, 0:T], relu, relu, ALU.mult).then_inc(hid_sq, 1)
                        if j:
                            rest(j - 1)
                        modulate_next()
                    rest(GT - 1)

                def down(g):
                    for j in range(KD):
                        if g:
                            own(f"{L}down{g - 1}_{j}")
                        residual(f"{L}down{g}_{j}", j, 40, last=g == GROUPS_F - 1)
                        modulate_next()
                for g in range(GROUPS_F):
                    up(g)
                    if g:
                        down(g - 1)
                down(GROUPS_F - 1)
                if l == 0:
                    b1 = VEC_AT["bmod"][0] + MOD_TILES
                    for st, n in ((0, MOD_TILES), (1, 2 * KD)):
                        step(dve.tensor_tensor(MOD[:, 1, 0:n, st], MOD[:, 1, 0:n, st], VEC[:, b1:b1 + n], ALU.add))
                    gains(1)
            next_phase()


def rows(a, n):
    return np.broadcast_to(np.asarray(a).reshape(1, -1), (n, np.asarray(a).size))


def constants():
    f = np.float32
    j = np.arange(P)
    cst = np.zeros((P, 3, P), f)
    cst[:, 0] = np.eye(P)
    cst[:, 1] = 1.0
    cst[:, 2] = (j[:, None] // 64 == j[None, :] // 64)
    lg = np.log1p(-np.exp2(-5.0 - np.arange(RET_H)))
    diff = np.arange(S)[None, :] - j[:, None]
    ret = np.where(diff[:, None, :] >= 0, np.exp(np.maximum(diff, 0)[:, None, :] * lg[None, :, None]), 0.0)
    ret = ret * RET_D ** -0.5
    ret = np.concatenate([ret, ret[:, :, 0:P]], axis=2).reshape(P, -1)
    rel = j[:, None] + P - np.arange(2 * P)[None, :]
    slopes = np.exp2(-8.0 * np.arange(1, SWA_H + 1) / SWA_H)
    swa = np.where(((rel >= 0) & (rel < P))[:, None, :], -slopes[None, :, None] * rel[:, None, :], NEG)
    mask1 = np.concatenate([ret, swa.reshape(P, -1)], axis=1).astype(f)
    tok = np.arange(S)
    freqs = (f(10000.0) ** (-np.arange(8, dtype=f) / f(8))).astype(f)
    rope = np.zeros((P, 2 * S + 2 * MLA_QK), f)
    rope[:, 0:S] = 1.0
    for axis, place in enumerate((tok // GRID_W, tok % GRID_W)):
        ang = place.astype(f)[None, :] * freqs[:, None]
        for half in range(2):
            r = MLA_NOPE + 16 * axis + 8 * half
            rope[r:r + 8, 0:S] = np.cos(ang)
            rope[r:r + 8, S:2 * S] = np.sin(ang)
        a, b = MLA_NOPE + 16 * axis + np.arange(8), MLA_NOPE + 16 * axis + 8 + np.arange(8)
        rope[b, 2 * S + a] = -1.0
        rope[a, 2 * S + b] = 1.0
    rope[np.arange(MLA_ROPE), 2 * S + MLA_QK + MLA_NOPE + np.arange(MLA_ROPE)] = 1.0
    return cst, mask1, rope


def window_bias(rpb):
    q, k = np.arange(S)[:, None], np.arange(S)[None, :]
    dr = k // GRID_W - q // GRID_W + 7
    cq, ck = q % GRID_W, k % GRID_W
    dc = np.clip(ck - cq, -(WIN_W - 1), WIN_W - 1) + WIN_W - 1
    c0 = np.clip(cq - WIN_W // 2, 0, GRID_W - WIN_W)
    inside = (ck >= c0) & (ck < c0 + WIN_W)
    out = np.where(inside[None], rpb[:, dr, dc], np.float32(NEG))
    return out.reshape(NA_H, ST, P, S).transpose(2, 1, 0, 3).reshape(P, -1)


def layout(i):
    f = np.float32
    i = {k: np.asarray(v) for k, v in i.items()}
    cst, mask1, rope = constants()

    def cols(a):
        return a.reshape(-1, P).T

    def twice(a):
        return np.concatenate([a, a]).reshape(P, 1)

    def padded(a):
        return np.concatenate([a, np.zeros(P - a.size, f)]).reshape(P, 1)
    vec = [np.full((P, 1), EPS, f), cols(i["mix_norm_g"][0]), cols(i["ffn_norm_g"][0]), cols(i["ple_gate_norm_g"][0]),
           cols(i["ple_norm_g"][0]), cols(i["ret_gn_g"][0]), cols(i["ret_gn_b"][0]), twice(i["q_norm_g"][0]),
           twice(i["k_norm_g"][0]), rows(i["attn_sinks"][0], P), rows(np.arange(8, 0, -1).astype(f), P)]
    for l in range(2):
        vec += [cols(i["g_norm1_2"][l]), cols(i["g_norm2_2"][l]), twice(i["na_q_gain_2"][l]),
                twice(i["na_k_gain_2"][l]), cols(i["mla_cq_gain_2"][l]), cols(i["mla_ckv_gain_2"][l]),
                padded(i["mla_q_gain_2"][l]), padded(i["mla_k_gain_2"][l])]
    vec.append(cols(i["b_mod_2"].reshape(-1)))
    ukv = i["mla_w_ukv_2"].reshape(2, P, MLA_H, MLA_NOPE + MLA_V)
    nope = np.concatenate([ukv[..., :MLA_NOPE], np.zeros((2, P, MLA_H, MLA_ROPE), f)], axis=3)
    ukv = np.concatenate([nope.reshape(2, P, -1), ukv[..., MLA_NOPE:].reshape(2, P, -1)], axis=2)
    lc = np.stack([np.concatenate([rows(i["gm_ln_g_2"][l], P), rows(i["gm_ln_b_2"][l], P),
                                   i["gm_w_s_2"][l].transpose(2, 0, 1).reshape(P, -1),
                                   rows(i["gm_b_s_2"][l], P)], axis=1) for l in range(2)])
    return dict(
        xT=i["x"][0].T, ctxT=i["ctx_2"][0].T, pT=i["p"][0, 0].T, vec=np.concatenate(vec, axis=1), cst=cst,
        rope=rope, mask1=mask1, lc=lc, na_bias=np.stack([window_bias(i["na_rpb_2"][l]) for l in range(2)]),
        w_in=i["w_in"][0],
        w_sk=np.concatenate([i["w_in"][0][:, C1["sk"] + 64 * (j // 2):C1["sk"] + 64 * (j // 2) + 64]
                             for j in range(4)], axis=1), w_ret_o=i["w_ret_o"][0], w_swa_o=i["w_swa_o"][0], w_out=i["w_out"][0],
        w_r=np.concatenate([i["w_router_group"][0], i["w_router_expert"][0]], axis=1),
        b_r=np.concatenate([i["b_router_group"][0], i["b_router_expert"][0]])[None],
        w_gate=i["w_exp_gate"][0], w_up=i["w_exp_up"][0], w_down=i["w_exp_down"][0], w_ple=i["w_ple"][0],
        w_ple_gate=i["w_ple_gate"][0],
        w_mod=i["w_mod_2"][0].T.reshape(N_EXP // 2, MOD_COLS, D),
        w_mod2=i["w_mod_2"][1].T.reshape(MOD_TILES, P, D),
        c_rows=np.concatenate([rows(i["c_2"], P), rows(i["c_ctx_2"], P)], axis=1),
        w_in_2=i["w_in_2"], na_w_o=i["na_w_o_2"],
        gm_w_o=i["gm_w_o_2"], w_uq=i["mla_w_uq_2"], w_ukv=ukv, mla_w_o=i["mla_w_o_2"], w_out_2=i["w_out_2"],
        ffn_w1=i["ffn_w1_2"], ffn_w2=i["ffn_w2_2"])


def build(nc, arrays):
    t = {name: nc.dram_tensor(f"in_{name}", a.shape, F32, kind="ExternalInput").ap() for name, a in arrays.items()}
    t["comb_rows"] = nc.dram_tensor("comb_rows", (N_EXP, S), F32, kind="Internal").ap()
    program(nc, t, nc.dram_tensor("out", (D, S), F32, kind="ExternalOutput").ap())


def kernel(**inputs):
    import concourse.bacc as _bacc
    from concourse.bass_utils import run_bass_kernel_spmd as _run

    nc = _bacc.Bacc("TRN2", target_bir_lowering=False, num_devices=1)
    arrays = {k: np.ascontiguousarray(v) for k, v in layout(inputs).items()}
    build(nc, arrays)
    r = _run(nc, [{f"in_{k}": v for k, v in arrays.items()}], core_ids=[0])
    return np.ascontiguousarray(r.results[0]["out"].T)[None]
```
